# Optimizing a Trainium2 kernel written in Bass

```python
import jax, jax.numpy as jnp
from jax import lax
import numpy as np

D_MODEL = 1024
BATCH = 1
SEQ = 1024
DEPTH = 1
DEC_BATCH = 1
DEC_SEQ = 32
PAST_LEN = 256

CHUNK = 64
Q_BLOCK = 128
N_HEADS = 8
QK_NOPE = 64
QK_ROPE = 32
V_HEAD = 64
KV_LORA = 256
Q_LORA = 768
D_ATTN = N_HEADS * V_HEAD
D_CONV = 512
CONV_W = 3
D_MIX = D_ATTN + D_CONV
D_IN_PROJ = Q_LORA + KV_LORA + QK_ROPE + 3 * D_CONV
D_FF = ((8 * D_MODEL + 3 * 256 - 1) // (3 * 256)) * 256
ROPE_THETA = 10000.0
EPS = 1e-6
SM_SCALE = (QK_NOPE + QK_ROPE) ** -0.5

kernel_name = "hybrid_mla_shortconv_streaming_step"

def rms_norm(x, g):
    xf = x.astype(jnp.float32)
    y = xf * lax.rsqrt(jnp.mean(jnp.square(xf), axis=-1, keepdims=True) + EPS)
    return (y * g.astype(jnp.float32)).astype(x.dtype)

def apply_rope(x, pos):
    half = QK_ROPE // 2
    inv_freq = ROPE_THETA ** (-jnp.arange(half, dtype=jnp.float32) / half)
    ang = pos.astype(jnp.float32)[:, None] * inv_freq[None, :]
    cos = jnp.cos(ang)[None, :, None, :]
    sin = jnp.sin(ang)[None, :, None, :]
    xf = x.astype(jnp.float32)
    x1, x2 = xf[..., :half], xf[..., half:]
    return jnp.concatenate([x1 * cos - x2 * sin, x1 * sin + x2 * cos], axis=-1).astype(x.dtype)

def attend(q_nope, q_rope, q_pos, k_nope, k_rope, v, k_pos):
    s = (jnp.einsum("bqhd,bkhd->bhqk", q_nope, k_nope)
         + jnp.einsum("bqhr,bkr->bhqk", q_rope, k_rope)).astype(jnp.float32) * SM_SCALE
    allowed = (k_pos[None, :] // CHUNK) <= (q_pos[:, None] // CHUNK)
    s = jnp.where(allowed[None, None], s, jnp.finfo(jnp.float32).min)
    p = jax.nn.softmax(s, axis=-1).astype(v.dtype)
    return jnp.einsum("bhqk,bkhd->bqhd", p, v)

def chunk_causal_attention(q_nope, q_rope, q_pos, k_nope, k_rope, v, k_pos):
    B, S = q_nope.shape[0], q_nope.shape[1]
    if S <= Q_BLOCK:
        return attend(q_nope, q_rope, q_pos, k_nope, k_rope, v, k_pos)
    nb = S // Q_BLOCK

    def to_blocks(t):
        return jnp.moveaxis(t.reshape(B, nb, Q_BLOCK, *t.shape[2:]), 1, 0)

    qp = q_pos.reshape(nb, Q_BLOCK)
    out = lax.map(lambda a: attend(a[0], a[1], a[2], k_nope, k_rope, v, k_pos),
                  (to_blocks(q_nope), to_blocks(q_rope), qp))
    return jnp.moveaxis(out, 0, 1).reshape(B, S, N_HEADS, V_HEAD)

def hybrid_mixer(h, pos, past_latent, past_k_rope, conv_prev,
                 w_in, q_norm_g, w_uq, kv_norm_g, w_ukv, conv_w, conv_b, w_out):
    B, S, _ = h.shape
    proj = h @ w_in
    i1 = Q_LORA
    i2 = i1 + KV_LORA
    i3 = i2 + QK_ROPE
    i4 = i3 + D_CONV
    i5 = i4 + D_CONV
    c_q, c_kv, k_r, u, g_b, g_c = jnp.split(proj, [i1, i2, i3, i4, i5], axis=-1)

    q = (rms_norm(c_q, q_norm_g) @ w_uq).reshape(B, S, N_HEADS, QK_NOPE + QK_ROPE)
    q_nope = q[..., :QK_NOPE]
    q_rope = apply_rope(q[..., QK_NOPE:], pos)
    latent = rms_norm(c_kv, kv_norm_g)
    k_rope_new = apply_rope(k_r[:, :, None, :], pos)[:, :, 0, :]
    if past_latent is None:
        all_latent, all_k_rope, k_pos = latent, k_rope_new, pos
    else:
        P = past_latent.shape[1]
        all_latent = jnp.concatenate([past_latent, latent], axis=1)
        all_k_rope = jnp.concatenate([past_k_rope, k_rope_new], axis=1)
        k_pos = jnp.concatenate([jnp.arange(P, dtype=jnp.int32), pos])
    T = all_latent.shape[1]
    kv = (all_latent @ w_ukv).reshape(B, T, N_HEADS, QK_NOPE + V_HEAD)
    k_nope, v = kv[..., :QK_NOPE], kv[..., QK_NOPE:]
    attn = chunk_causal_attention(q_nope, q_rope, pos, k_nope, all_k_rope, v, k_pos)

    gated_in = g_c * u
    ext = jnp.concatenate([conv_prev, gated_in], axis=1)
    conv = (conv_w[0] * ext[:, :S] + conv_w[1] * ext[:, 1:S + 1]
            + conv_w[2] * ext[:, 2:S + 2] + conv_b)
    y_conv = g_b * conv

    mix = jnp.concatenate([attn.reshape(B, S, D_ATTN), y_conv], axis=-1) @ w_out
    return mix, latent, k_rope_new, ext[:, S:]

def layer(x, c, pos, past_latent, past_k_rope, conv_prev,
          w_ada, b_ada, norm_mix_g, w_in, q_norm_g, w_uq, kv_norm_g, w_ukv,
          conv_w, conv_b, w_out, norm_ffn_g, w_gate, w_up, w_down):
    mod = jax.nn.silu(c) @ w_ada + b_ada
    sh1, sc1, g1, sh2, sc2, g2 = jnp.split(mod[:, None, :], 6, axis=-1)
    h = rms_norm(x, norm_mix_g) * (1 + sc1) + sh1
    mix, latent, k_rope_new, conv_state = hybrid_mixer(
        h, pos, past_latent, past_k_rope, conv_prev,
        w_in, q_norm_g, w_uq, kv_norm_g, w_ukv, conv_w, conv_b, w_out)
    x = x + g1 * mix
    h = rms_norm(x, norm_ffn_g) * (1 + sc2) + sh2
    ff = (jax.nn.silu(h @ w_gate) * (h @ w_up)) @ w_down
    x = x + g2 * ff
    return x, latent, k_rope_new, conv_state

def setup_inputs(seed: int = 0) -> dict:
    key = jax.random.key(seed)
    ks = jax.random.split(key, 24)

    def nrm(k, shape, s):
        return jax.random.normal(k, shape, jnp.float32) * s

    return {
        "x_prompt": nrm(ks[0], (BATCH, SEQ, D_MODEL), 1.0),
        "x_sample": nrm(ks[1], (DEC_BATCH, DEC_SEQ, D_MODEL), 1.0),
        "c_prompt": nrm(ks[2], (BATCH, D_MODEL), 1.0),
        "c_sample": nrm(ks[3], (DEC_BATCH, D_MODEL), 1.0),
        "cache_kv_latent": nrm(ks[4], (DEPTH, DEC_BATCH, PAST_LEN, KV_LORA), 1.0),
        "cache_k_rope": nrm(ks[5], (DEPTH, DEC_BATCH, PAST_LEN, QK_ROPE), 1.0),
        "state_conv": nrm(ks[6], (DEPTH, DEC_BATCH, CONV_W - 1, D_CONV), 0.5),
        "w_ada": nrm(ks[7], (DEPTH, D_MODEL, 6 * D_MODEL), 0.5 * D_MODEL ** -0.5),
        "b_ada": nrm(ks[8], (DEPTH, 6 * D_MODEL), 0.02),
        "norm_mix_g": 1.0 + nrm(ks[9], (DEPTH, D_MODEL), 0.02),
        "w_in": nrm(ks[10], (DEPTH, D_MODEL, D_IN_PROJ), D_MODEL ** -0.5),
        "q_norm_g": 1.0 + nrm(ks[11], (DEPTH, Q_LORA), 0.02),
        "w_uq": nrm(ks[12], (DEPTH, Q_LORA, N_HEADS * (QK_NOPE + QK_ROPE)), Q_LORA ** -0.5),
        "kv_norm_g": 1.0 + nrm(ks[13], (DEPTH, KV_LORA), 0.02),
        "w_ukv": nrm(ks[14], (DEPTH, KV_LORA, N_HEADS * (QK_NOPE + V_HEAD)), KV_LORA ** -0.5),
        "conv_w": nrm(ks[15], (DEPTH, CONV_W, D_CONV), CONV_W ** -0.5),
        "conv_b": nrm(ks[16], (DEPTH, D_CONV), 0.02),
        "w_out": nrm(ks[17], (DEPTH, D_MIX, D_MODEL), D_MIX ** -0.5),
        "norm_ffn_g": 1.0 + nrm(ks[18], (DEPTH, D_MODEL), 0.02),
        "w_gate": nrm(ks[19], (DEPTH, D_MODEL, D_FF), D_MODEL ** -0.5),
        "w_up": nrm(ks[20], (DEPTH, D_MODEL, D_FF), D_MODEL ** -0.5),
        "w_down": nrm(ks[21], (DEPTH, D_FF, D_MODEL), D_FF ** -0.5),
        "final_norm_g": 1.0 + nrm(ks[22], (D_MODEL,), 0.02),
    }

def reference(x_prompt, x_sample, c_prompt, c_sample, cache_kv_latent, cache_k_rope, state_conv,
              w_ada, b_ada, norm_mix_g, w_in, q_norm_g, w_uq, kv_norm_g, w_ukv,
              conv_w, conv_b, w_out, norm_ffn_g, w_gate, w_up, w_down, final_norm_g):
    S = x_prompt.shape[1]
    P = cache_kv_latent.shape[2]
    Sd = x_sample.shape[1]
    pos_p = jnp.arange(S, dtype=jnp.int32)
    pos_s = P + jnp.arange(Sd, dtype=jnp.int32)
    conv_zero = jnp.zeros((x_prompt.shape[0], CONV_W - 1, D_CONV), x_prompt.dtype)

    xp, xs = x_prompt, x_sample
    lat_p, kr_p, cv_p, lat_s, kr_s, cv_s = [], [], [], [], [], []
    for l in range(DEPTH):
        w = (w_ada[l], b_ada[l], norm_mix_g[l], w_in[l], q_norm_g[l], w_uq[l], kv_norm_g[l], w_ukv[l],
             conv_w[l], conv_b[l], w_out[l], norm_ffn_g[l], w_gate[l], w_up[l], w_down[l])
        xp, a, b, c = layer(xp, c_prompt, pos_p, None, None, conv_zero, *w)
        lat_p.append(a)
        kr_p.append(b)
        cv_p.append(c)
        xs, a, b, c = layer(xs, c_sample, pos_s, cache_kv_latent[l], cache_k_rope[l], state_conv[l], *w)
        lat_s.append(a)
        kr_s.append(b)
        cv_s.append(c)

    y_prompt = rms_norm(xp, final_norm_g)
    y_sample = rms_norm(xs, final_norm_g)
    new_latent_p = jnp.stack(lat_p)
    new_k_rope_p = jnp.stack(kr_p)
    new_conv_p = jnp.stack(cv_p)
    new_latent_s = jnp.stack(lat_s)
    new_k_rope_s = jnp.stack(kr_s)
    new_conv_s = jnp.stack(cv_s)
    return (y_prompt, y_sample, new_latent_p, new_k_rope_p, new_conv_p, new_latent_s, new_k_rope_s, new_conv_s)


_drawn_inputs = setup_inputs


def setup_inputs(seed=0):
    import zlib

    import numpy as np

    out = dict(_drawn_inputs(seed))
    spreads = {}
    factors = {'cache_kv_latent': 3.052,
     'cache_k_rope': 6.111,
     'state_conv': 3.357,
     'q_norm_g': 8.0,
     'w_uq': 2.837,
     'conv_b': 8.0,
     'norm_ffn_g': 8.0,
     'final_norm_g': 2.815}
    for name, (base, spread) in spreads.items():
        noise = np.random.default_rng([zlib.crc32(name.encode()), seed]).standard_normal(out[name].shape)
        drawn = base * np.exp(spread * noise) if base else spread * noise
        out[name] = __import__('jax').numpy.asarray(drawn.astype(out[name].dtype))
    for name, factor in factors.items():
        out[name] = (out[name] * factor).astype(out[name].dtype)
    return out
```

```python
from contextlib import ExitStack

import numpy as np

import concourse.bass as bass
from concourse import mybir

F32 = mybir.dt.float32
F32R = mybir.dt.float32r
ALU = mybir.AluOpType
ACT = mybir.ActivationFunctionType
AX_X = mybir.AxisListType.X

P = 128
D = 1024
KD = D // P
S = 1024
SD = 32
T = S + SD
NCH = 3
CH = T // NCH
PAST = 256
TK = S + PAST + SD
HEADS = 8
NOPE, ROPE, VH = 64, 32, 64
HALF = ROPE // 2
KVR, QR = 256, 768
KQ, KKV = QR // P, KVR // P
DCONV = 512
NJ = DCONV // P
CW = 3
DFF = 2816
NG = DFF // (2 * P)
CHUNK = 64
EPS = 1e-6
SCALE = float(NOPE + ROPE) ** -0.5
BIG = 1e30
ARENA = 207 * 1024

C_KV = QR
C_KR = C_KV + KVR
C_U = C_KR + ROPE
C_GB = C_U + DCONV
C_GC = C_GB + DCONV

V_BADA, V_NMIX, V_QG, V_KVG, V_CW, V_CB, V_FFN, V_FIN, V_C, V_ST, V_END = (
    0, 48, 56, 62, 64, 76, 80, 88, 96, 112, 120)
SH1, SC1, G1, SH2, SC2, G2 = (8 * n for n in range(6))

S_CONV = 0
S_COUT = S_CONV + 3 * NJ
S_CKV = S_COUT + 4
S_KR = S_CKV + KKV
S_CQ = S_KR + 1
S_AOUT = S_CQ + KQ
S_FFN = S_AOUT + 4
S_LOOP = S_FFN + 4
S_LAST = S_LOOP + 6 * (NG - 1)
S_END = S_LAST + 2
G_N1 = 0
G_CONV = 1
G_COUT = G_CONV + 3 * NJ
G_CKV = G_COUT + KD
G_KR = G_CKV + KKV
G_NKV = G_KR + 1
G_CQ = G_NKV + 1
G_NQ = G_CQ + KQ
G_X1 = G_NQ + 1
G_AOUT = G_X1 + 2
G_N2 = G_AOUT + KD
G_FFN = G_N2 + 1
G_LOOP = G_FFN + 4
G_LAST = G_LOOP + 12 * (NG - 1)
G_FIN = G_LAST + 8

UNITS = 9
PAIR_UNITS = 2 * UNITS


def unit_of(u):
    e, t = divmod(u, UNITS)
    if t < UNITS - 1:
        return e, P * t, P, 0, P * (t + 1), [(v, P) for v in range(t + 1)]
    return e, S, SD, S, PAST + SD, [(8, P), (9, P), (10, SD)]


def build(nc, x_prompt, x_sample, c_prompt, c_sample, cache_kv_latent, cache_k_rope, state_conv,
          w_ada, b_ada, norm_mix_g, w_in, q_norm_g, w_uq, kv_norm_g, w_ukv, conv_w, conv_b, w_out,
          norm_ffn_g, w_gate, w_up, w_down, final_norm_g, c_ident, c_cos, c_sin, c_qmask, c_kmask,
          y_prompt, y_sample, lat_p, kr_p, cv_p, lat_s, kr_s, cv_s):
    ctx = ExitStack()
    with ctx:
        U = T * 4
        start = nc.sbuf_base
        ctx.enter_context(nc.sbuf_tensor("arena", [P, ARENA // 4], F32))

        def at(name, shape, dt, off):
            size = 4 * int(np.prod(shape[1:]))
            assert off % 32 == 0 and off + size <= ARENA, (name, off, size)
            return nc.alloc_sbuf_tensor_at(name, shape, dt, offset=ARENA0 + off)

        ARENA0 = -(-start // 32) * 32
        X = at("X", [P, KD, T], F32, 0)
        RAW = at("RAW", [P, 2, KD * P], F32, 8 * U)
        WH = at("WH", [P, 2, KD * P], F32R, 8 * U + 8192)
        WL = at("WL", [P, 2, KD * P], F32R, 8 * U + 16384)
        o = 8 * U + 24576
        COS = at("COS", [P, T], F32, o)
        SIN = at("SIN", [P, T], F32, o + U)
        PTS = at("PTS", [P, 2, KD * P], F32, o)
        IDENT = at("IDENT", [P, P], F32, o + 2 * U)
        ONES = at("ONES", [P, P], F32, o + 2 * U + 512)
        VEC = at("VEC", [P, P], F32, o + 2 * U + 1024)
        CS = at("CS", [P, KD, 2], F32, o + 2 * U + 1536)
        MOD = at("MOD", [P, 48, 2], F32, o + 2 * U + 1600)
        A1 = at("A1", [P, 2, KD], F32, o + 2 * U + 1984)
        A2 = at("A2", [P, 2, KD], F32, o + 2 * U + 2048)
        MX = at("MX", [P, 2], F32, o + 2 * U + 2112)
        NM = at("NM", [P, 2], F32, o + 2 * U + 2144)
        SUM = at("SUM", [P, 2], F32, o + 2 * U + 2176)
        RCP = at("RCP", [P, 2], F32, o + 2 * U + 2208)
        ST = at("ST", [P, NJ, 2 * (CW - 1)], F32, o + 2 * U + 2240)
        B = o + 2 * U + 2304
        HH = at("HH", [P, KD, T], F32R, B)
        HL = at("HL", [P, KD, T], F32R, B + 8 * U)
        YH = at("YH", [P, NJ, T], F32R, B + 16 * U)
        YL = at("YL", [P, NJ, T], F32R, B + 20 * U)
        SQ1 = at("SQ1", [P, 2, T], F32, B + 16 * U)
        SS1 = at("SS1", [P, T], F32, B + 18 * U)
        TT1 = at("TT1", [P, 2, T], F32, B + 19 * U)
        XR = at("XR", [P, 2, D], F32, B + 24 * U)
        VR = at("VR", [P, P], F32, B + 24 * U + 8192)
        UU = at("UU", [P, T + 2], F32, B + 24 * U)
        CC = at("CC", [P, T], F32, B + 24 * U + 4256)
        BB = at("BB", [P, T], F32, B + 25 * U + 4256)
        GG = at("GG", [P, T + 4], F32, B + 26 * U + 4256)
        ADA = at("ADA", [P, 2, KD, 2 * P], F32, B + 28 * U + 4256)
        CQ = at("CQ", [P, KQ, T], F32, B + 16 * U)
        CKV = at("CKV", [P, KKV, T], F32, B + 22 * U)
        KR = at("KR", [P, TK], F32, B + 24 * U)
        o = B + 24 * U + 5248
        SQ2 = at("SQ2", [P, T], F32, o)
        SSK = at("SSK", [P, T], F32, o + U)
        SSQ = at("SSQ", [P, T], F32, o + 2 * U)
        TR = at("TR", [P, T], F32, o + 3 * U)
        WQ = at("WQ", [P, KQ, QR], F32, o + 4 * U)
        QROT = at("QROT", [P, 2, T], F32, B)
        WKV = at("WKV", [P, KKV, HEADS * (NOPE + VH)], F32, B)
        LAT = at("LAT", [P, KKV, TK], F32, B + 2 * U)
        o = B + 2 * U + 10496
        KT = [at(f"KT{e}", [P, TK], F32, o + 5248 * e) for e in range(2)]
        QT = [at(f"QT{e}", [P, T], F32, o + 10496 + U * e) for e in range(2)]
        o = o + 10496 + 2 * U
        V = at("V", [P, 11, P], F32, o)
        WQP = at("WQP", [P, KQ, 2, NOPE], F32, o + 5632)
        WKP = at("WKP", [P, KKV, 2, NOPE], F32, o + 8704)
        WVP = at("WVP", [P, KKV, 2, VH], F32, o + 10752)
        o = o + 12800
        AOH = at("AOH", [P, NJ, T], F32R, o)
        assert o + 4 * U <= B + 16 * U
        QF = at("QF", [P, T], F32, o)
        PL = at("PL", [P, 2, KVR], F32, o + U)
        PK = at("PK", [P, 2, ROPE], F32, o + U + 2048)
        LO = at("LO", [P, 2, KVR], F32, o + U + 2304)
        KO = at("KO", [P, 2, ROPE], F32, o + U + 4352)
        WQR = at("WQR", [P, KQ, 2, HEADS, HALF], F32, o + U + 4608)
        PP = at("PP", [P, 2, D], F32, B + 22 * U)
        AOL = at("AOL", [P, NJ, T], F32R, B + 24 * U)
        SQ3 = at("SQ3", [P, 2, T], F32, B)
        SS3 = at("SS3", [P, T], F32, B + 2 * U)
        TT3 = at("TT3", [P, 2, T], F32, B + 3 * U)
        H2H = at("H2H", [P, KD, T], F32R, B + 16 * U)
        H2L = at("H2L", [P, KD, T], F32R, B + 24 * U)
        AH = at("AH", [P, 4, T], F32R, B + 5 * U)
        AL = at("AL", [P, 4, T], F32R, B + 9 * U)
        SG = at("SG", [P, 2, T], F32, B + 13 * U)
        SQ4 = at("SQ4", [P, 2, T], F32, B + 16 * U)
        SS4 = at("SS4", [P, T], F32, B + 18 * U)
        ORW = at("ORW", [P, 2, D], F32, B + 19 * U)

        PS = ctx.enter_context(nc.psum_tensor("PS", [P, 8, 512], F32))
        rope_dram = nc.dram_tensor("q_rope_rows", [2, P, T], F32, kind="Internal").ap()

        def sem(name):
            return ctx.enter_context(nc.semaphore(name))

        vec_loaded = sem("vec_loaded")
        ident_loaded = sem("ident_loaded")
        tables_loaded = sem("tables_loaded")
        ones_set = sem("ones_set")
        vec_full = sem("vec_full")
        vec_ready = sem("vec_ready")
        x_turned = sem("x_turned")
        x_kept_dve = sem("x_kept_dve")
        x_kept_act = sem("x_kept_act")
        cond_ready = sem("cond_ready")
        ada_used = sem("ada_used")
        mod_kept = sem("mod_kept")
        scales_ready = sem("scales_ready")
        w_hi = sem("w_hi")
        w_lo = sem("w_lo")
        kr_half_loaded = sem("kr_half_loaded")
        squared = sem("squared")
        summed = sem("summed")
        dev_ready = sem("dev_ready")
        rstd_ready = sem("rstd_ready")
        h_scaled = sem("h_scaled")
        h_full = sem("h_full")
        h_hi = sem("h_hi")
        h_lo = sem("h_lo")
        pads_set = sem("pads_set")
        gated = sem("gated")
        conv_step = sem("conv_step")
        y_full = sem("y_full")
        y_hi = sem("y_hi")
        y_lo = sem("y_lo")
        states_kept = sem("states_kept")
        k_rope_step = sem("k_rope_step")
        lat_ready = sem("lat_ready")
        q_ready = sem("q_ready")
        wq_loaded = sem("wq_loaded")
        wkv_loaded = sem("wkv_loaded")
        past_loaded = sem("past_loaded")
        past_turned = sem("past_turned")
        past_kept = sem("past_kept")
        zeroed = sem("zeroed")
        wq_rotary = sem("wq_rotary")
        pool_zeroed = sem("pool_zeroed")
        mask_loaded = sem("mask_loaded")
        q_rope_step = sem("q_rope_step")
        rope_stored = sem("rope_stored")
        k_rope_copied = sem("k_rope_copied")
        rows_turned = sem("rows_turned")
        rows_kept = sem("rows_kept")
        wp_ready = sem("wp_ready")
        q_full = sem("q_full")
        k_full = sem("k_full")
        v_full = sem("v_full")
        q_kept = sem("q_kept")
        k_kept = sem("k_kept")
        v_kept = sem("v_kept")
        rope_loaded = sem("rope_loaded")
        s_full = sem("s_full")
        max_ready = sem("max_ready")
        nm_ready = sem("nm_ready")
        exp_done = sem("exp_done")
        rcp_ready = sem("rcp_ready")
        p_ready = sem("p_ready")
        p_turned = sem("p_turned")
        pt_kept = sem("pt_kept")
        o_full = sem("o_full")
        o_hi = sem("o_hi")
        o_kept = sem("o_kept")
        silu_ready = sem("silu_ready")
        a_full = sem("a_full")
        a_hi = sem("a_hi")
        y_ready = sem("y_ready")
        y_turned = sem("y_turned")
        y_kept_dve = sem("y_kept_dve")
        y_kept_act = sem("y_kept_act")
        states_stored = sem("states_stored")
        x_loaded = [sem(f"x_loaded{n}") for n in range(2)]
        ada_loaded = [sem(f"ada_loaded{n}") for n in range(2)]
        raw_loaded = [sem(f"raw_loaded{n}") for n in range(2)]
        ps_full = [sem(f"ps_full{n}") for n in range(2)]
        ps_free = [sem(f"ps_free{n}") for n in range(2)]
        rows_stored = [sem(f"rows_stored{n}") for n in range(2)]
        y_stored = [sem(f"y_stored{n}") for n in range(2)]
        block = ctx.enter_context(nc.Block())

        win = w_in[0].rearrange("(k p) m -> p k m", p=P)
        wada = w_ada[0].rearrange("(k p) m -> p k m", p=P)
        wout = w_out[0].rearrange("(k p) m -> p k m", p=P)
        wg = w_gate[0].rearrange("(k p) m -> p k m", p=P)
        wu = w_up[0].rearrange("(k p) m -> p k m", p=P)
        wd = w_down[0].rearrange("(k p) m -> p k m", p=P)

        def raw(s, k=KD):
            return RAW[:, s % 2, :].rearrange("p (k m) -> p k m", k=k)

        def hi_lo(s, k=KD):
            return [w[:, s % 2, :].rearrange("p (k m) -> p k m", k=k) for w in (WH, WL)]

        def chunks(g, rows=slice(0, P)):
            b = NCH * (g % 2)
            return PS[rows, b:b + NCH, 0:CH]

        def in_chunks(ap):
            return ap.rearrange("p (n c) -> p n c", n=NCH)

        def streams(g):
            b = NCH * (g % 2)
            return [(PS[:, b:b + 2, 0:CH], slice(0, 2 * CH), 0), (PS[:, b + 2, 0:S - 2 * CH], slice(2 * CH, S), 0),
                    (PS[:, b + 2, S - 2 * CH:CH], slice(S, T), 1)]

        def tile_of(buf, k):
            return buf[:, k, :] if isinstance(k, int) else \
                buf[:, bass.ds(k, 1), :].rearrange("p a t -> p (a t)")

        def wait_filled(eng, g, dyn=0):
            eng.wait_ge(ps_full[g % 2], dyn + (g // 2 + 1))

        def wait_kept(eng, g, dyn=0):
            eng.wait_ge(ps_free[g % 2], dyn + (g // 2 + 2))

        def wait_loaded(eng, s, dyn=0):
            eng.wait_ge(raw_loaded[s % 2], 16 * dyn + 16 * (s // 2 + 1))

        @block.sync
        def _(sp):
            sp.dma_start(VR[V_BADA:V_NMIX, :], b_ada[0].rearrange("(j p) -> j p", p=P)).then_inc(vec_loaded, 16)
            for row, src in ((V_NMIX, norm_mix_g[0]), (V_QG, q_norm_g[0]), (V_KVG, kv_norm_g[0]),
                             (V_CB, conv_b[0]), (V_FFN, norm_ffn_g[0]), (V_FIN, final_norm_g),
                             (V_C, c_prompt[0]), (V_C + KD, c_sample[0])):
                n = src.shape[0] // P
                sp.dma_start(VR[row:row + n, :], src.rearrange("(j p) -> j p", p=P)).then_inc(vec_loaded, 16)
            sp.dma_start(VR[V_CW:V_CB, :], conv_w[0].rearrange("w (j p) -> (w j) p", p=P)).then_inc(vec_loaded, 16)
            sp.dma_start(VR[V_ST:V_END, :], state_conv[0, 0].rearrange("r (j p) -> (r j) p", p=P))\
                .then_inc(vec_loaded, 16)
            sp.dma_start(IDENT[:], c_ident).then_inc(ident_loaded, 16)

            for n in range(UNITS):
                if n >= 2:
                    sp.wait_ge(x_turned, n - 1)
                if n < KD:
                    sp.dma_start(XR[:, n % 2], x_prompt[0, n * P:(n + 1) * P, :]).then_inc(x_loaded[n % 2], 16)
                else:
                    sp.dma_start(XR[0:SD, n % 2], x_sample[0]).then_inc(x_loaded[n % 2], 16)

            def load_ada(n, col):
                sp.dma_start(ADA[:, n % 2], wada[:, :, bass.ds(col, 2 * P)]).then_inc(ada_loaded[n % 2], 16)

            def load_slot(s, src, k=KD, dyn=0):
                sp.wait_ge(w_lo, 2 * dyn + (s + 1))
                sp.dma_start(raw(s, k), src).then_inc(raw_loaded[s % 2], 16)

            for n in range(8):
                sp.wait_ge(ada_used, n + 1)
                load_ada(n, n * 2 * P)
            with sp.Fori(0, 2) as i:
                for n in range(6):
                    j, q = divmod(n, 3)
                    sp.wait_ge(ada_used, 6 * i + (n + 9))
                    load_ada(n, (6 * i + (n + 8)) * (2 * P))
                    load_slot(n, win[:, :, bass.ds((2 * i + j) * P + (C_U, C_GC, C_GB)[q], P)], dyn=3 * i)
            with sp.Fori(0, 2) as i:
                for n in range(2):
                    sp.wait_ge(ada_used, 2 * i + (n + 21))
                    load_ada(n, (2 * i + (n + 20)) * (2 * P))
                    load_slot(S_COUT + n, wout[:, NJ:KD, bass.ds((2 * i + n) * (2 * P), 2 * P)], k=NJ, dyn=i)
            sp.dma_start(COS[:], c_cos).then_inc(tables_loaded, 16)
            sp.dma_start(SIN[:], c_sin).then_inc(tables_loaded, 16)
            sp.wait_ge(states_kept, NJ)
            for dst, col in ((cv_p, 0), (cv_s, CW - 1)):
                for j in range(NJ):
                    sp.dma_start(dst[0, 0][:, j * P:(j + 1) * P].rearrange("r p -> p r"),
                                 ST[:, j, col:col + CW - 1],
                                 allow_slow_non_contiguous=True).then_inc(states_stored, 16)
            for n in range(KKV):
                load_slot(S_CKV + n, win[:, :, C_KV + n * P:C_KV + (n + 1) * P])
            sp.wait_ge(w_lo, S_KR + 1)
            for q, done in ((0, kr_half_loaded), (1, raw_loaded[S_KR % 2])):
                sp.dma_start(raw(S_KR)[:, :, 32 * q:32 * q + HALF],
                             win[:, :, C_KR + q * HALF:C_KR + (q + 1) * HALF]).then_inc(done, 16)
            sp.wait_ge(ada_used, 26)
            sp.dma_start(WQ[:], w_uq[0].rearrange("(k p) m -> p k m", p=P)).then_inc(wq_loaded, 16)
            for n in range(KQ):
                load_slot(S_CQ + n, win[:, :, n * P:(n + 1) * P])
            for n in range(2):
                load_slot(S_AOUT + n, wout[:, 0:NJ, n * 2 * P:(n + 1) * 2 * P], k=NJ)
            wait_filled(sp, G_CQ + KQ - 1)
            sp.dma_start(PL[:], cache_kv_latent[0, 0].rearrange("(n p) m -> p n m", p=P)).then_inc(past_loaded, 16)
            sp.dma_start(PK[:], cache_k_rope[0, 0].rearrange("(n p) m -> p n m", p=P)).then_inc(past_loaded, 16)
            sp.wait_ge(pool_zeroed, 4)
            for e, row in ((0, 80), (1, 16)):
                sp.dma_start(QT[e][row:row + KD, :], c_qmask).then_inc(mask_loaded, 16)
                sp.dma_start(KT[e][row:row + KD, :], c_kmask).then_inc(mask_loaded, 16)
            for n in range(UNITS):
                sp.wait_ge(rows_kept, n + 1)
                r, dst, kdst = (slice(0, P), lat_p, kr_p) if n < KD else (slice(0, SD), lat_s, kr_s)
                t = slice(n * P, (n + 1) * P) if n < KD else slice(0, SD)
                sp.dma_start(dst[0, 0, t, :], LO[r, n % 2]).then_inc(rows_stored[n % 2], 16)
                sp.dma_start(kdst[0, 0, t, :], KO[r, n % 2]).then_inc(rows_stored[n % 2], 16)
            sp.wait_ge(q_rope_step, 4)
            for q in range(2):
                sp.dma_start(rope_dram[q], QROT[:, q]).then_inc(rope_stored, 16)
            sp.wait_ge(rope_stored, 32)
            sp.dma_start(WKV[:], w_ukv[0].rearrange("(k p) m -> p k m", p=P)).then_inc(wkv_loaded, 16)

            def load_rope(first_row):
                for e, rows in ((0, (64, 96)), (1, (0, 32))):
                    for q in range(2):
                        sp.dma_start(QT[e][rows[q]:rows[q] + HALF, :],
                                     rope_dram[q, bass.ds(first_row + HALF * e, HALF), :]).then_inc(rope_loaded, 16)

            load_rope(0)
            with sp.Fori(1, NJ) as j:
                sp.wait_ge(s_full, PAIR_UNITS * j)
                load_rope(2 * HALF * j)
            for n in range(2, 4):
                load_slot(S_AOUT + n, wout[:, 0:NJ, n * 2 * P:(n + 1) * 2 * P], k=NJ)

            def load_gate_up(s, tile, dyn=0):
                for n in range(4):
                    load_slot(s + n, (wg, wu)[n % 2][:, :, bass.ds(tile * P + (n // 2) * P, P)], dyn=dyn)

            def load_down(s, tile, dyn=0):
                for n in range(2):
                    load_slot(s + n, wd[:, bass.ds(tile, 2), n * 512:(n + 1) * 512], k=2, dyn=dyn)

            load_gate_up(S_FFN, 0)
            with sp.Fori(0, (NG - 1) // 2) as i:
                for n in range(2):
                    load_gate_up(S_LOOP + 6 * n, 4 * i + 2 * (n + 1), dyn=6 * i)
                    load_down(S_LOOP + 6 * n + 4, 4 * i + 2 * n, dyn=6 * i)
            load_down(S_LAST, 2 * (NG - 1))
            for n in range(UNITS):
                sp.wait_ge(y_kept_dve, n + 1)
                sp.wait_ge(y_kept_act, n + 1)
                dst = y_prompt[0, n * P:(n + 1) * P, :] if n < KD else y_sample[0]
                sp.dma_start(dst, ORW[0:P if n < KD else SD, n % 2]).then_inc(y_stored[n % 2], 16)
            sp.wait_ge(states_stored, 16 * 2 * NJ)
            for n in range(2):
                sp.wait_ge(rows_stored[n], 32 * (5 - n))
                sp.wait_ge(y_stored[n], 16 * (5 - n))

        @block.tensor
        def _(pe):
            pe.sem_inc(ada_used, 2)
            pe.sem_inc(v_full, 1)
            pe.wait_ge(vec_loaded, 16 * 11)
            pe.wait_ge(ident_loaded, 16)
            pe.transpose(PS[:, 7, 0:V_END], VR[0:V_END, :], IDENT[0:V_END, 0:V_END]).then_inc(vec_full, 1)
            for n in range(UNITS):
                r = P if n < KD else SD
                pe.wait_ge(x_loaded[n % 2], 16 * (n // 2 + 1))
                if n >= 2:
                    pe.wait_ge(x_kept_dve, n - 1)
                    pe.wait_ge(x_kept_act, n - 1)
                for k in range(KD):
                    mm = pe.transpose(PS[:, 2 * (n % 2) + k // 4, (k % 4) * P:(k % 4) * P + r],
                                      XR[0:r, n % 2, k * P:(k + 1) * P], IDENT[0:r, 0:r])
                mm.then_inc(x_turned, 1)

            def ada(n, bank, col, dyn=0):
                pe.wait_ge(ada_loaded[n % 2], 16 * dyn + 16 * (n // 2 + 1))
                for m in range(2):
                    for k in range(KD):
                        mm = pe.matmul(PS[:, bank, bass.ds(col + 2 * m, 2)], ADA[:, n % 2, k, m * P:(m + 1) * P],
                                       CS[:, k, :], start=(k == 0), stop=(k == KD - 1))
                mm.then_inc(ada_used, 1)

            pe.wait_ge(cond_ready, 1)
            for n in range(8):
                ada(n, 6, 4 * n)

            def begin_slot(s, dyn=0):
                pe.wait_ge(w_lo, 2 * dyn + (s + 3))

            def begin_group(g, dyn=0):
                pe.wait_ge(ps_free[g % 2], dyn + (g // 2 + 1))

            def product(g, weights, moving, ks, before=None):
                b = NCH * (g % 2)
                for k in ks:
                    if before:
                        before(k)
                    for w, xs in ((weights[0][k], moving), (weights[1][k], moving[:1])):
                        for n in range(NCH):
                            for x in xs:
                                mm = pe.matmul(PS[:, b + n, 0:CH], w, x[k][:, n * CH:(n + 1) * CH],
                                               start=(k == 0 and w is weights[0][k] and x is xs[0]),
                                               stop=(k == ks[-1] and w is weights[1][k]))
                mm.then_inc(ps_full[g % 2], 1)
                return mm

            def cut(pair, first=0):
                return [{k: buf[:, first + k, :] for k in range(buf.shape[1] - first)} for buf in pair]

            def weights_of(s, k=KD, m=0):
                return [{n: w[:, n, m * P:(m + 1) * P] for n in range(k)} for w in hi_lo(s, k)]

            def total(g, ss, tiles_summed):
                pe.wait_ge(summed, tiles_summed)
                begin_group(g)
                for n in range(NCH):
                    mm = pe.matmul(PS[:, NCH * (g % 2) + n, 0:CH], ONES[:], ss[:, n * CH:(n + 1) * CH],
                                   start=True, stop=True)
                mm.then_inc(ps_full[g % 2], 1)

            pe.wait_ge(ones_set, 1)
            total(G_N1, SS1, 7)
            h = cut((HH, HL))
            with pe.Fori(0, 2) as i:
                for n in range(6):
                    begin_slot(n, 3 * i)
                    begin_group(G_CONV + n, 3 * i)
                    product(G_CONV + n, weights_of(n), h, range(KD),
                            before=(lambda k: pe.wait_ge(h_lo, k + 1)) if n == 0 else None)
                    ada(n, 7, 24 * i + 4 * n, 3 * i + 4)
            y = cut((YH, YL))
            with pe.Fori(0, 2) as i:
                for n in range(2):
                    begin_slot(S_COUT + n, i)
                    for m in range(2):
                        g = G_COUT + 2 * n + m
                        begin_group(g, 2 * i)
                        product(g, weights_of(S_COUT + n, NJ, m), y, range(NJ),
                                before=(lambda k: pe.wait_ge(y_lo, k + 2)) if n + m == 0 else None)
                    ada(n, 6, 8 * i + 4 * n, i + 10)
            for n in range(KKV + 1):
                begin_slot(S_CKV + n)
                begin_group(G_CKV + n)
                product(G_CKV + n, weights_of(S_CKV + n), h, range(KD))
            total(G_NKV, SSK, 8)
            with pe.Fori(0, KQ // 2) as i:
                for n in range(2):
                    begin_slot(S_CQ + n, i)
                    begin_group(G_CQ + n, i)
                    product(G_CQ + n, weights_of(S_CQ + n), h, range(KD))
            total(G_NQ, SSQ, 14)
            pe.wait_ge(past_loaded, 32)
            for n in range(2):
                for f in range(KKV):
                    pe.transpose(PS[:, 6, (2 * f + n) * P:(2 * f + n + 1) * P], PL[:, n, f * P:(f + 1) * P], IDENT[:])
                for q in range(2):
                    mm = pe.transpose(PS[0:HALF, 7, (2 * q + n) * P:(2 * q + n + 1) * P],
                                      PK[:, n, q * HALF:(q + 1) * HALF], IDENT[:])
            mm.then_inc(past_turned, 1)

            pe.wait_ge(wq_rotary, 2)
            for q in range(2):
                begin_group(G_X1 + q)
                for k in range(KQ):
                    if q == 0:
                        pe.wait_ge(q_ready, k + 1)
                    for n in range(NCH):
                        mm = pe.matmul(PS[:, NCH * ((G_X1 + q) % 2) + n, 0:CH],
                                       WQR[:, k, q].rearrange("p h c -> p (h c)"),
                                       CQ[:, k, n * CH:(n + 1) * CH], start=(k == 0), stop=(k == KQ - 1))
                mm.then_inc(ps_full[(G_X1 + q) % 2], 1)
            pe.wait_ge(lat_ready, 4)
            pe.wait_ge(k_rope_step, 4)
            pe.wait_ge(past_kept, 3)
            for n in range(UNITS):
                r = P if n < KD else SD
                col = n * P if n < KD else S + PAST
                if n >= 2:
                    pe.wait_ge(rows_kept, n - 1)
                for f in range(KKV):
                    pe.transpose(PS[0:r, 6 + n % 2, f * P:(f + 1) * P], LAT[:, f, col:col + r], IDENT[:])
                pe.transpose(PS[0:r, 6 + n % 2, KVR:KVR + 48], KR[0:48, col:col + r], IDENT[0:48, 0:48])\
                    .then_inc(rows_turned, 1)
            pe.wait_ge(rows_kept, UNITS)
            pe.wait_ge(mask_loaded, 64)

            with pe.Fori(0, NJ) as j:
                pe.wait_ge(wp_ready, j + 1)
                pe.wait_ge(o_kept, PAIR_UNITS * j + 1)
                for k in range(KQ):
                    for n in range(NCH):
                        mm = pe.matmul(PS[:, n, 0:CH], WQP[:, k].rearrange("p e d -> p (e d)"),
                                       CQ[:, k, n * CH:(n + 1) * CH], start=(k == 0), stop=(k == KQ - 1))
                mm.then_inc(q_full, 1)
                for n in range(4):
                    for k in range(KKV):
                        mm = pe.matmul(PS[:, 3 + n, 0:TK // 4], WKP[:, k].rearrange("p e d -> p (e d)"),
                                       LAT[:, k, n * (TK // 4):(n + 1) * (TK // 4)], start=(k == 0), stop=(k == 1))
                mm.then_inc(k_full, 1)
                for v in range(11):
                    r = P if v < 10 else SD
                    if v == 4:
                        pe.wait_ge(q_kept, 2 * j + 2)
                    for k in range(KKV):
                        mm = pe.matmul(PS[0:r, (7, 0, 1)[v // 4], (v % 4) * P:(v % 4 + 1) * P],
                                       LAT[:, k, v * P:v * P + r], WVP[:, k].rearrange("p e d -> p (e d)"),
                                       start=(k == 0), stop=(k == 1))
                mm.then_inc(v_full, 1)
                pe.wait_ge(k_kept, 2 * j + 2)
                pe.wait_ge(v_kept, j + 1)
                pe.wait_ge(rope_loaded, 64 * j + 64)

                def scores(u):
                    e, q0, nq, k0, nk, _ = unit_of(u)
                    if u >= 2:
                        pe.wait_ge(exp_done, PAIR_UNITS * j + (u - 1))
                    for c in range(0, nk, 512):
                        w = min(512, nk - c)
                        mm = pe.matmul(PS[0:nq, 2 * (u % 2) + c // 512, 0:w], QT[e][:, q0:q0 + nq],
                                       KT[e][:, k0 + c:k0 + c + w], start=True, stop=True)
                    mm.then_inc(s_full, 1)

                def turn(u):
                    e, q0, nq, k0, nk, tiles = unit_of(u)
                    pe.wait_ge(p_ready, PAIR_UNITS * j + (u + 1))
                    if u >= 1:
                        pe.wait_ge(pt_kept, PAIR_UNITS * j + u)
                    for b, (_, r) in enumerate(tiles):
                        mm = pe.transpose(PS[0:r, 4 + b // 4, (b % 4) * P:(b % 4 + 1) * P],
                                          PP[:, u % 2, b * P:b * P + r], IDENT[:])
                    mm.then_inc(p_turned, 1)

                def values(u):
                    e, q0, nq, k0, nk, tiles = unit_of(u)
                    pe.wait_ge(pt_kept, PAIR_UNITS * j + (u + 1))
                    if u >= 2:
                        pe.wait_ge(o_kept, PAIR_UNITS * j + u)
                    for b, (v, r) in enumerate(tiles):
                        mm = pe.matmul(PS[:, 6 + u % 2, 0:nq], V[0:r, v, :], PTS[0:r, u % 2, b * P:b * P + nq],
                                       start=(b == 0), stop=(b == len(tiles) - 1))
                    mm.then_inc(o_full, 1)

                scores(0)
                for u in range(PAIR_UNITS):
                    if u + 1 < PAIR_UNITS:
                        scores(u + 1)
                    turn(u)
                    if u >= 1:
                        values(u - 1)
                values(PAIR_UNITS - 1)

            ao = cut((AOH, AOL))
            pe.wait_ge(o_kept, PAIR_UNITS * NJ + 1)
            with pe.Fori(0, 2) as i:
                for n in range(2):
                    begin_slot(S_AOUT + n, i)
                    for m in range(2):
                        g = G_AOUT + 2 * n + m
                        begin_group(g, 2 * i)
                        product(g, weights_of(S_AOUT + n, NJ, m), ao, range(NJ))
            total(G_N2, SS3, 22)
            h2 = cut((H2H, H2L))

            def gate_up(s, g, dyn_s=0, dyn_g=0, first=False):
                for n in range(4):
                    begin_slot(s + n, dyn_s)
                    begin_group(g + n, dyn_g)
                    product(g + n, weights_of(s + n), h2, range(KD),
                            before=(lambda k: pe.wait_ge(h_lo, KD + k + 1)) if first and n == 0 else None)

            def down(s, g, a0, tiles_ready, dyn_s=0, dyn_g=0):
                pe.wait_ge(a_full, tiles_ready)
                for n in range(2):
                    begin_slot(s + n, dyn_s)
                    for m in range(4):
                        begin_group(g + 4 * n + m, dyn_g)
                        product(g + 4 * n + m, weights_of(s + n, 2, m), cut((AH, AL), a0), range(2))

            gate_up(S_FFN, G_FFN, first=True)
            with pe.Fori(0, (NG - 1) // 2) as i:
                for n in range(2):
                    gate_up(S_LOOP + 6 * n, G_LOOP + 12 * n, 6 * i, 12 * i)
                    down(S_LOOP + 6 * n + 4, G_LOOP + 12 * n + 4, 2 * n, 4 * i + (2 * n + 4), 6 * i, 12 * i)
            down(S_LAST, G_LAST, 0, 2 * NG + 2)
            total(G_FIN, SS4, 30)
            for n in range(UNITS):
                r = P if n < KD else SD
                if n == 0:
                    pe.wait_ge(y_ready, KD)
                if n >= 2:
                    pe.wait_ge(y_kept_dve, n - 1)
                    pe.wait_ge(y_kept_act, n - 1)
                for k in range(KD):
                    mm = pe.transpose(PS[0:r, 2 * (n % 2) + k // 4, (k % 4) * P:(k % 4 + 1) * P],
                                      X[:, k, n * P:n * P + r], IDENT[:])
                mm.then_inc(y_turned, 1)

        @block.scalar
        def _(act):
            def split_hi(s, g, dyn=0, dyn_g=0):
                wait_loaded(act, s, dyn)
                wait_filled(act, g, dyn_g)
                act.activation(WH[:, s % 2, :], RAW[:, s % 2, :], ACT.Copy).then_inc(w_hi, 1)

            act.wait_ge(vec_ready, 1)
            act.activation(CS[:].rearrange("p k s -> p s k"),
                           VEC[:, V_C:V_C + 2 * KD].rearrange("p (s k) -> p s k", s=2), ACT.Silu)\
                .then_inc(cond_ready, 1)
            for n in range(UNITS):
                r = P if n < KD else SD
                act.wait_ge(x_turned, n + 1)
                act.activation(X[:, 4:8, n * P:n * P + r],
                               PS[:, 2 * (n % 2) + 1, :].rearrange("p (k t) -> p k t", k=4)[:, :, 0:r], ACT.Copy)\
                    .then_inc(x_kept_act, 1)
            wait_loaded(act, 0)
            act.activation(WH[:, 0, :], RAW[:, 0, :], ACT.Copy).then_inc(w_hi, 1)

            act.wait_ge(x_kept_dve, UNITS)
            act.wait_ge(x_kept_act, UNITS)
            for k in range(KD):
                if k >= 3:
                    act.wait_ge(summed, k - 2)
                act.activation(SS1[:] if k == 0 else SQ1[:, k % 2, :], X[:, k, :], ACT.Square)\
                    .then_inc(squared, 1)

            def root(ss, g):
                wait_kept(act, g)
                act.activation(ss[:], ss[:], ACT.Sqrt).then_inc(dev_ready, 1)

            def modulate(tt, hh, a, shift, n):
                for k in range(KD):
                    act.wait_ge(h_scaled, KD * n + k + 1)
                    for st, t in ((0, slice(0, S)), (1, slice(S, T))):
                        ins = act.activation(tt[:, k % 2, t], tt[:, k % 2, t], ACT.Identity,
                                             bias=MOD[:, shift + k, st:st + 1], scale=a[:, st, k:k + 1])
                    ins.then_inc(h_full, 1)
                    act.wait_ge(h_full, KD * n + k + 1)
                    act.activation(hh[:, k, :], tt[:, k % 2, :], ACT.Copy).then_inc(h_hi, 1)

            root(SS1, G_N1)
            act.wait_ge(scales_ready, 2)
            modulate(TT1, HH, A1, SH1, 0)

            def keep(g, dst, dyn=0):
                wait_filled(act, g, dyn)
                act.activation(in_chunks(dst), chunks(g), ACT.Copy).then_inc(ps_free[g % 2], 1)

            with act.Fori(0, 2) as i:
                for n in range(6):
                    j, q = divmod(n, 3)
                    split_hi(n + 1, G_CONV + n - 1, 3 * i, 3 * i)
                    act.wait_ge((y_full, y_lo, y_full)[q], 2 * i + (j + 1))
                    keep(G_CONV + n, (UU[:, 0:T], CC[:], BB[:])[q], 3 * i)
            with act.Fori(0, 2) as i:
                for n in range(2):
                    split_hi(S_COUT + n + 1, G_COUT + 2 * n - 1, i, 2 * i)
            for n in range(KKV):
                if n == 1:
                    act.wait_ge(kr_half_loaded, 16)
                split_hi(S_CKV + n + 1, G_CKV + n - 1)
                keep(G_CKV + n, CKV[:, n, :])
                wait_kept(act, G_CKV + n)
                act.activation((SSK, SQ2)[n][:], CKV[:, n, :], ACT.Square).then_inc(squared, 1)
            split_hi(S_KR + 1, G_KR - 1)
            root(SSK, G_NKV)
            for n in range(KQ):
                split_hi(S_CQ + n + 1, G_CQ + n - 1)
                keep(G_CQ + n, CQ[:, n, :])
                wait_kept(act, G_CQ + n)
                act.wait_ge(summed, n + 8)
                act.activation(SQ2[:], CQ[:, n, :], ACT.Square).then_inc(squared, 1)
            act.wait_ge(wq_loaded, 16)
            wait_filled(act, G_CQ + KQ - 1)
            for q in range(2):
                c = NOPE + q * HALF
                act.activation(WQR[:, :, q], WQ[:].rearrange("p k (h c) -> p k h c", h=HEADS)[:, :, :, c:c + HALF],
                               ACT.Copy).then_inc(wq_rotary, 1)
            root(SSQ, G_NQ)

            act.wait_ge(past_turned, 1)
            act.activation(LAT[:, :, S:S + PAST], PS[:, 6, :].rearrange("p (f t) -> p f t", f=KKV), ACT.Copy)\
                .then_inc(past_kept, 1)
            for q in range(2):
                act.activation(KR[32 * q:32 * q + HALF, S:S + PAST], PS[0:HALF, 7, q * PAST:(q + 1) * PAST], ACT.Copy)\
                    .then_inc(past_kept, 1)
            for n in range(UNITS):
                r = slice(0, P if n < KD else SD)
                act.wait_ge(rows_turned, n + 1)
                if n >= 2:
                    act.wait_ge(rows_stored[n % 2], 32 * (n // 2))
                act.activation(LO[r, n % 2, :], PS[r, 6 + n % 2, 0:KVR], ACT.Copy)
                act.activation(KO[r, n % 2, :].rearrange("p (q d) -> p q d", q=2),
                               PS[r, 6 + n % 2, KVR:KVR + 64].rearrange("p (q d) -> p q d", q=2)[:, :, 0:HALF],
                               ACT.Copy).then_inc(rows_kept, 1)

            with act.Fori(0, NJ) as j:
                act.wait_ge(q_full, j + 1)
                for e in range(2):
                    rows = slice(NOPE * e, NOPE * (e + 1))
                    act.activation(in_chunks(QT[e][rows, :]), PS[rows, 0:NCH, 0:CH], ACT.Copy).then_inc(q_kept, 1)

                def exponentials(u):
                    e, q0, nq, k0, nk, tiles = unit_of(u)
                    act.wait_ge(nm_ready, PAIR_UNITS * j + (u + 1))
                    if u >= 2:
                        act.wait_ge(p_turned, PAIR_UNITS * j + (u - 1))
                    src = PS[0:nq, 2 * (u % 2):2 * (u % 2) + 2, :].rearrange("p b k -> p (b k)")[:, 0:nk]
                    act.activation(PP[0:nq, u % 2, 0:nk], src, ACT.Exp, bias=NM[0:nq, u % 2:u % 2 + 1],
                                   scale=SCALE, accum_out=SUM[0:nq, u % 2:u % 2 + 1]).then_inc(exp_done, 1)

                def keep_turned(u):
                    e, q0, nq, k0, nk, tiles = unit_of(u)
                    act.wait_ge(p_turned, PAIR_UNITS * j + (u + 1))
                    if u >= 2:
                        act.wait_ge(o_full, PAIR_UNITS * j + (u - 1))
                    whole = [r for _, r in tiles].count(P)
                    src = PS[:, 4:6, :].rearrange("p b (k q) -> p (b k) q", q=P)
                    dst = PTS[:, u % 2, :].rearrange("p (k q) -> p k q", q=P)
                    ins = act.activation(dst[:, 0:whole, 0:nq], src[:, 0:whole, 0:nq], ACT.Copy)
                    if whole < len(tiles):
                        ins = act.activation(dst[0:SD, whole, 0:nq], src[0:SD, whole, 0:nq], ACT.Copy)
                    ins.then_inc(pt_kept, 1)

                for u in range(PAIR_UNITS):
                    exponentials(u)
                    if u >= 1:
                        keep_turned(u - 1)
                keep_turned(PAIR_UNITS - 1)

            for m in range(KD):
                if m % 2 == 0:
                    split_hi(S_AOUT + m // 2 + 1, G_AOUT + m - 1)
                wait_kept(act, G_AOUT + m)
                act.wait_ge(summed, m + 14)
                act.activation(SQ3[:, 0, :], X[:, m, :], ACT.Square).then_inc(squared, 1)
            root(SS3, G_N2)
            act.wait_ge(scales_ready, 4)
            modulate(TT3, H2H, A2, SH2, 1)

            def gate_up(s, g, tile, dyn_s=0, dyn_g=0, dyn_t=0):
                for n in range(4):
                    split_hi(s + n + 1, g + n - 1, dyn_s, dyn_g)
                    if n % 2 == 0:
                        act.wait_ge(a_full, dyn_t + (tile + n // 2 + 1))
                        wait_filled(act, g + n, dyn_g)
                        act.activation(in_chunks(SG[:, n // 2, :]), chunks(g + n), ACT.Silu)\
                            .then_inc(ps_free[(g + n) % 2], 1)

            def down(s, g, dyn_s=0, dyn_g=0):
                for n in range(2):
                    split_hi(s + n + 1, g + 4 * n - 1, dyn_s, dyn_g)

            gate_up(S_FFN, G_FFN, 0)
            with act.Fori(0, (NG - 1) // 2) as i:
                for n in range(2):
                    gate_up(S_LOOP + 6 * n, G_LOOP + 12 * n, 2 * (n + 1), 6 * i, 12 * i, 4 * i)
                    down(S_LOOP + 6 * n + 4, G_LOOP + 12 * n + 4, 6 * i, 12 * i)
            split_hi(S_LAST + 1, G_LAST - 1)
            for m in range(KD):
                wait_kept(act, G_LAST + m)
                act.wait_ge(summed, 22 + m)
                act.activation(SQ4[:, 0, :], X[:, m, :], ACT.Square).then_inc(squared, 1)
            root(SS4, G_FIN)
            for n in range(UNITS):
                r = P if n < KD else SD
                act.wait_ge(y_turned, n + 1)
                if n >= 2:
                    act.wait_ge(y_stored[n % 2], 16 * (n // 2))
                act.activation(ORW[0:r, n % 2, 512:D], PS[0:r, 2 * (n % 2) + 1, :], ACT.Copy).then_inc(y_kept_act, 1)

        @block.vector
        def _(dve):
            dve.sem_inc(w_lo, 2)
            dve.sem_inc(y_full, 1)
            dve.sem_inc(y_lo, 1)
            dve.sem_inc(a_full, 2)
            dve.sem_inc(o_kept, 1)
            for n in range(2):
                dve.sem_inc(ps_free[n], 1)
            dve.memset(ONES[:], 1.0).then_inc(ones_set, 1)
            dve.wait_ge(vec_full, 1)
            dve.tensor_copy(VEC[:, 0:V_END], PS[:, 7, 0:V_END]).then_inc(vec_ready, 1)
            for n in range(UNITS):
                r = P if n < KD else SD
                dve.wait_ge(x_turned, n + 1)
                dve.tensor_copy(X[:, 0:4, n * P:n * P + r],
                                PS[:, 2 * (n % 2), :].rearrange("p (k t) -> p k t", k=4)[:, :, 0:r])\
                    .then_inc(x_kept_dve, 1)

            def add_square(ss, sq, sums, done=0):
                dve.wait_ge(squared, sums)
                dve.wait_ge(summed, done)
                dve.tensor_tensor(ss[:], ss[:], sq, ALU.add).then_inc(summed, 1)

            for k in range(1, KD):
                dve.wait_ge(squared, k + 1)
                if k >= 2:
                    dve.wait_ge(summed, k - 1)
                dve.tensor_tensor(SS1[:], SS1[:], SQ1[:, k % 2, :], ALU.add).then_inc(summed, 1)

            def variance(ss, g, width):
                wait_filled(dve, g)
                dve.tensor_scalar(in_chunks(ss[:]), chunks(g), 1.0 / width, EPS, ALU.mult, ALU.add)\
                    .then_inc(ps_free[g % 2], 1)

            def invert(ss, n):
                dve.wait_ge(dev_ready, n + 1)
                dve.reciprocal(ss[:], ss[:]).then_inc(rstd_ready, 1)
                dve.wait_ge(rstd_ready, n + 1)

            def add_bias(bank, first, n, done):
                src = PS[:, bank, 0:2 * n].rearrange("p (m s) -> p m s", s=2)
                for st in range(2):
                    ins = dve.tensor_tensor(MOD[:, first:first + n, st], src[:, :, st], VEC[:, first:first + n], ALU.add)
                ins.then_inc(mod_kept, 1)
                dve.wait_ge(mod_kept, done)

            def scales(a, sc, gain):
                for st in range(2):
                    dve.scalar_tensor_tensor(a[:, st, :], MOD[:, sc:sc + KD, st], 1.0, VEC[:, gain:gain + KD],
                                             ALU.add, ALU.mult).then_inc(scales_ready, 1)

            dve.wait_ge(vec_ready, 1)
            variance(SS1, G_N1, D)
            invert(SS1, 0)
            dve.wait_ge(ada_used, 10)
            add_bias(6, 0, 16, 1)
            scales(A1, SC1, V_NMIX)

            def split_lo(s, dyn=0):
                dve.wait_ge(w_hi, 2 * dyn + (s + 1))
                dve.tensor_tensor(WL[:, s % 2, :], RAW[:, s % 2, :], WH[:, s % 2, :].bitcast(F32), ALU.subtract)\
                    .then_inc(w_lo, 1)

            split_lo(0)

            def normed(tt, ss, hh, hl, n):
                def rest(k):
                    dve.wait_ge(h_hi, KD * n + k + 1)
                    dve.tensor_tensor(hl[:, k, :], tt[:, k % 2, :], hh[:, k, :].bitcast(F32), ALU.subtract)\
                        .then_inc(h_lo, 1)
                for k in range(KD):
                    if k >= 2:
                        dve.wait_ge(h_lo, KD * n + k - 1)
                    dve.tensor_tensor(tt[:, k % 2, :], X[:, k, :], ss[:], ALU.mult).then_inc(h_scaled, 1)
                    if k >= 1:
                        rest(k - 1)
                rest(KD - 1)

            normed(TT1, SS1, HH, HL, 0)
            dve.wait_ge(h_lo, KD)
            dve.memset(GG[:, 0:CW - 1], 0.0).then_inc(pads_set, 1)

            with dve.Fori(0, 2) as i:
                for n in range(6):
                    split_lo(n + 1, 3 * i)
                    if n % 3 < 2:
                        continue
                    jj = n // 3
                    j = 2 * i + jj
                    g = G_CONV + n
                    wait_kept(dve, g - 2, 3 * i)
                    wait_kept(dve, g - 1, 3 * i)
                    dve.wait_ge(y_full, j + 1)
                    dve.tensor_copy(GG[:, S + 2:S + 4],
                                    VEC[:, V_ST:V_END].rearrange("p (r j) -> p r j", r=CW - 1)[:, :, bass.ds(j, 1)]
                                    .rearrange("p r a -> p (r a)"))
                    dve.tensor_tensor(GG[:, 2:S + 2], CC[:, 0:S], UU[:, 0:S], ALU.mult)
                    dve.tensor_tensor(GG[:, S + 4:], CC[:, S:T], UU[:, S:T], ALU.mult).then_inc(gated, 1)
                    dve.wait_ge(gated, j + 1)
                    dve.tensor_copy(tile_of(ST, j)[:, 0:2], GG[:, S:S + 2])
                    dve.tensor_copy(tile_of(ST, j)[:, 2:4], GG[:, T + 2:T + 4]).then_inc(states_kept, 1)
                    taps = [VEC[:, bass.ds(V_CW + NJ * w + j, 1)] for w in range(CW)]
                    dve.tensor_scalar(UU[:], GG[:, 0:T + 2], taps[0], VEC[:, bass.ds(V_CB + j, 1)],
                                      ALU.mult, ALU.add).then_inc(conv_step, 1)
                    for w in (1, 2):
                        dve.wait_ge(conv_step, 3 * j + w)
                        dve.scalar_tensor_tensor(UU[:], GG[:, w:T + 2 + w], taps[w], UU[:], ALU.mult, ALU.add)\
                            .then_inc(conv_step, 1)
                    wait_kept(dve, g, 3 * i)
                    dve.wait_ge(conv_step, 3 * j + 3)
                    dve.tensor_tensor(CC[:, 0:S], BB[:, 0:S], UU[:, 0:S], ALU.mult)
                    dve.tensor_tensor(CC[:, S:T], BB[:, S:T], UU[:, S + 2:T + 2], ALU.mult).then_inc(y_full, 1)
                    dve.wait_ge(y_full, j + 2)
                    dve.tensor_copy(tile_of(YH, j), CC[:]).then_inc(y_hi, 1)
                    dve.wait_ge(y_hi, j + 1)
                    dve.tensor_tensor(tile_of(YL, j), CC[:], tile_of(YH, j).bitcast(F32), ALU.subtract)\
                        .then_inc(y_lo, 1)

            dve.wait_ge(ada_used, 22)
            add_bias(7, 16, 24, 2)
            scales(A2, SC2, V_FFN)

            def add_gated(g, gate, m, dyn_g=0):
                wait_filled(dve, g, dyn_g)
                for src, t, st in streams(g):
                    dst = X[:, m, t] if isinstance(m, int) else X[:, bass.ds(m, 1), t].rearrange("p a t -> p (a t)")
                    if t.start == 0:
                        dst = dst.rearrange("p (n c) -> p n c", n=2)
                    scalar = MOD[:, gate + m, st:st + 1] if isinstance(m, int) else \
                        MOD[:, bass.ds(m + gate, 1), st:st + 1].rearrange("p a s -> p (a s)")
                    ins = dve.scalar_tensor_tensor(dst, src, scalar, dst, ALU.mult, ALU.add)
                ins.then_inc(ps_free[g % 2], 1)

            with dve.Fori(0, 2) as i:
                for n in range(2):
                    split_lo(S_COUT + n + 1, i)
                    for m in range(2):
                        add_gated(G_COUT + 2 * n + m, G1, 4 * i + (2 * n + m), 2 * i)
            dve.wait_ge(ada_used, 26)
            add_bias(6, 40, 8, 3)
            dve.memset(KR[0:64, :], 0.0).then_inc(zeroed, 1)
            dve.memset(SSQ[:], 0.0).then_inc(zeroed, 1)
            for n in range(KKV):
                split_lo(S_CKV + n + 1)
            split_lo(S_KR + 1)
            dve.wait_ge(squared, 10)
            dve.tensor_tensor(SSK[:], SSK[:], SQ2[:], ALU.add).then_inc(summed, 1)

            g = G_KR
            dve.wait_ge(tables_loaded, 32)
            dve.wait_ge(zeroed, 2)
            wait_filled(dve, g)
            lo, up = slice(0, HALF), slice(32, 32 + HALF)

            def key_part(rows, ap, t):
                v = ap[rows, t.start + (PAST if t.start == S else 0):t.stop + (PAST if t.start == S else 0)]
                return v.rearrange("p (n c) -> p n c", n=2) if t.start == 0 else v

            def token_part(rows, ap, t):
                v = ap[rows, t]
                return v.rearrange("p (n c) -> p n c", n=2) if t.start == 0 else v

            for dst, wide, rows, src_rows, table in (
                    (KR, True, lo, lo, COS), (TR, False, lo, up, SIN), (KR, True, up, lo, SIN), (TR, False, up, up, COS)):
                for src, t, st in streams(g):
                    out = key_part(rows, dst, t) if wide else token_part(rows, dst, t)
                    ins = dve.tensor_tensor(out, src[src_rows], token_part(src_rows, table, t), ALU.mult)
            ins.then_inc(ps_free[g % 2], 1)
            wait_kept(dve, g)
            for rows, op in ((lo, ALU.subtract), (up, ALU.add)):
                for t, off in ((slice(0, S), 0), (slice(S, T), PAST)):
                    k = KR[rows, t.start + off:t.stop + off]
                    dve.tensor_tensor(k, k, TR[rows, t], op).then_inc(k_rope_step, 1)

            variance(SSK, G_NKV, KVR)
            with dve.Fori(0, KQ // 2) as i:
                for n in range(2):
                    split_lo(S_CQ + n + 1, i)
                    dve.wait_ge(squared, 2 * i + (n + 11))
                    dve.wait_ge(summed, 2 * i + (n + 8))
                    dve.tensor_tensor(SSQ[:], SSQ[:], SQ2[:], ALU.add).then_inc(summed, 1)
            invert(SSK, 1)
            variance(SSQ, G_NQ, QR)
            for f in range(KKV):
                for t, off in ((slice(0, S), 0), (slice(S, T), PAST)):
                    dve.scalar_tensor_tensor(LAT[:, f, t.start + off:t.stop + off], CKV[:, f, t],
                                             VEC[:, V_KVG + f:V_KVG + f + 1], SSK[:, t], ALU.mult, ALU.mult)\
                        .then_inc(lat_ready, 1)
            invert(SSQ, 2)
            for k in range(KQ):
                dve.scalar_tensor_tensor(CQ[:, k, :], CQ[:, k, :], VEC[:, V_QG + k:V_QG + k + 1], SSQ[:],
                                         ALU.mult, ALU.mult).then_inc(q_ready, 1)
            g = G_X1
            for q in range(2):
                wait_filled(dve, g + q)
            for n, (t1, t2, op) in enumerate(((COS, SIN, ALU.subtract), (SIN, COS, ALU.add))):
                if n == 1:
                    dve.wait_ge(q_rope_step, 3)
                a = dve.tensor_tensor(in_chunks(QROT[:, n, :]), chunks(g), in_chunks(t1[:]), ALU.mult)
                b = dve.tensor_tensor(in_chunks(QF[:]), chunks(g + 1), in_chunks(t2[:]), ALU.mult)
                if n == 0:
                    a.then_inc(q_rope_step, 1)
                    b.then_inc(q_rope_step, 1)
                    dve.wait_ge(q_rope_step, 2)
                else:
                    a.then_inc(ps_free[g % 2], 1)
                    b.then_inc(ps_free[(g + 1) % 2], 1)
                    wait_kept(dve, g)
                    wait_kept(dve, g + 1)
                dve.tensor_tensor(QROT[:, n, :], QROT[:, n, :], QF[:], op).then_inc(q_rope_step, 1)
            dve.wait_ge(k_rope_step, 4)
            dve.wait_ge(past_kept, 3)
            dve.wait_ge(pool_zeroed, 4)
            for e, rows in ((0, (64, 96)), (1, (0, 32))):
                for q in range(2):
                    dve.tensor_copy(KT[e][rows[q]:rows[q] + HALF, :], KR[32 * q:32 * q + HALF, :])\
                        .then_inc(k_rope_copied, 1)

            with dve.Fori(0, NJ) as j:
                dve.wait_ge(k_full, j + 1)
                for e in range(2):
                    rows = slice(NOPE * e, NOPE * (e + 1))
                    dve.tensor_copy(KT[e][rows, :].rearrange("p (n c) -> p n c", n=4), PS[rows, 3:7, 0:TK // 4])\
                        .then_inc(k_kept, 1)
                dve.wait_ge(v_full, j + 2)
                for a, b, bank, r in ((0, 4, 7, P), (4, 8, 0, P), (8, 10, 1, P), (10, 11, 1, SD)):
                    col = 2 * P if a == 10 else 0
                    ins = dve.tensor_copy(V[0:r, a:b, :],
                                          PS[0:r, bank, col:col + (b - a) * P].rearrange("p (v d) -> p v d", d=P))
                ins.then_inc(v_kept, 1)

                def maxima(u):
                    e, q0, nq, k0, nk, tiles = unit_of(u)
                    U0 = PAIR_UNITS * j
                    dve.wait_ge(s_full, U0 + (u + 1))
                    src = PS[0:nq, 2 * (u % 2):2 * (u % 2) + 2, :].rearrange("p b k -> p (b k)")[:, 0:nk]
                    dve.reduce_max(MX[0:nq, u % 2:u % 2 + 1], src, AX_X).then_inc(max_ready, 1)
                    dve.wait_ge(max_ready, U0 + (u + 1))
                    dve.tensor_scalar(NM[0:nq, u % 2:u % 2 + 1], MX[0:nq, u % 2:u % 2 + 1], -SCALE, None, ALU.mult)\
                        .then_inc(nm_ready, 1)

                def divide(u):
                    e, q0, nq, k0, nk, tiles = unit_of(u)
                    U0 = PAIR_UNITS * j
                    dve.wait_ge(exp_done, U0 + (u + 1))
                    dve.reciprocal(RCP[0:nq, u % 2:u % 2 + 1], SUM[0:nq, u % 2:u % 2 + 1]).then_inc(rcp_ready, 1)
                    dve.wait_ge(rcp_ready, U0 + (u + 1))
                    dve.tensor_scalar(PP[0:nq, u % 2, 0:nk], PP[0:nq, u % 2, 0:nk], RCP[0:nq, u % 2:u % 2 + 1], None,
                                      ALU.mult).then_inc(p_ready, 1)

                def keep_output(u):
                    e, q0, nq, k0, nk, tiles = unit_of(u)
                    U0 = PAIR_UNITS * j
                    dve.wait_ge(o_full, U0 + (u + 1))
                    rows = slice(VH * e, VH * (e + 1))
                    src = PS[rows, 6 + u % 2, 0:nq]
                    hi = AOH[rows, bass.ds(j, 1), q0:q0 + nq].rearrange("p a t -> p (a t)")
                    lo = AOL[rows, bass.ds(j, 1), q0:q0 + nq].rearrange("p a t -> p (a t)")
                    dve.tensor_copy(hi, src).then_inc(o_hi, 1)
                    dve.wait_ge(o_hi, U0 + (u + 1))
                    dve.tensor_tensor(lo, src, hi.bitcast(F32), ALU.subtract).then_inc(o_kept, 1)

                for u in range(PAIR_UNITS):
                    maxima(u)
                    if u >= 1:
                        divide(u - 1)
                    if u >= 2:
                        keep_output(u - 2)
                divide(PAIR_UNITS - 1)
                keep_output(PAIR_UNITS - 2)
                keep_output(PAIR_UNITS - 1)

            dve.memset(SS3[:], 0.0).then_inc(zeroed, 1)
            dve.wait_ge(zeroed, 3)

            with dve.Fori(0, 2) as i:
                for n in range(2):
                    split_lo(S_AOUT + n + 1, i)
                    for m in range(2):
                        add_gated(G_AOUT + 2 * n + m, G1, 4 * i + (2 * n + m), 2 * i)
                        dve.wait_ge(squared, 4 * i + (2 * n + m + 17))
                        dve.wait_ge(summed, 4 * i + (2 * n + m + 14))
                        dve.tensor_tensor(SS3[:], SS3[:], SQ3[:, 0, :], ALU.add).then_inc(summed, 1)
            variance(SS3, G_N2, D)
            invert(SS3, 3)
            normed(TT3, SS3, H2H, H2L, 1)

            def gate_up(s, g, tile, a0, dyn_s=0, dyn_g=0, dyn_t=0):
                for n in range(4):
                    split_lo(s + n + 1, dyn_s)
                    if n % 2 == 1:
                        t = n // 2
                        count = dyn_t + (tile + t + 1)
                        wait_kept(dve, g + n - 1, dyn_g)
                        wait_filled(dve, g + n, dyn_g)
                        dve.tensor_tensor(in_chunks(SG[:, t, :]), chunks(g + n), in_chunks(SG[:, t, :]), ALU.mult)\
                            .then_inc(ps_free[(g + n) % 2], 1)
                        wait_kept(dve, g + n, dyn_g)
                        dve.tensor_copy(AH[:, a0 + t, :], SG[:, t, :]).then_inc(a_hi, 1)
                        dve.wait_ge(a_hi, count)
                        dve.tensor_tensor(AL[:, a0 + t, :], SG[:, t, :], AH[:, a0 + t, :].bitcast(F32), ALU.subtract)\
                            .then_inc(a_full, 1)

            def down(s, g, dyn_s=0, dyn_g=0):
                for n in range(2):
                    split_lo(s + n + 1, dyn_s)
                    for m in range(4):
                        add_gated(g + 4 * n + m, G2, 4 * n + m, dyn_g)

            gate_up(S_FFN, G_FFN, 0, 0)
            with dve.Fori(0, (NG - 1) // 2) as i:
                for n in range(2):
                    gate_up(S_LOOP + 6 * n, G_LOOP + 12 * n, 2 * (n + 1), 2 * (1 - n), 6 * i, 12 * i, 4 * i)
                    down(S_LOOP + 6 * n + 4, G_LOOP + 12 * n + 4, 6 * i, 12 * i)
            split_lo(S_LAST + 1)
            dve.memset(SS4[:], 0.0).then_inc(zeroed, 1)
            dve.wait_ge(zeroed, 4)
            for m in range(KD):
                add_gated(G_LAST + m, G2, m)
                if m >= 1:
                    add_square(SS4, SQ4[:, 0, :], 24 + m, 21 + m)
            add_square(SS4, SQ4[:, 0, :], 24 + KD, 21 + KD)
            variance(SS4, G_FIN, D)
            invert(SS4, 4)
            for k in range(KD):
                dve.scalar_tensor_tensor(X[:, k, :], X[:, k, :], VEC[:, V_FIN + k:V_FIN + k + 1], SS4[:],
                                         ALU.mult, ALU.mult).then_inc(y_ready, 1)
            for n in range(UNITS):
                r = P if n < KD else SD
                dve.wait_ge(y_turned, n + 1)
                if n >= 2:
                    dve.wait_ge(y_stored[n % 2], 16 * (n // 2))
                dve.tensor_copy(ORW[0:r, n % 2, 0:512], PS[0:r, 2 * (n % 2), :]).then_inc(y_kept_dve, 1)

        @block.gpsimd
        def _(pool):
            wait_filled(pool, G_CQ + KQ - 1)
            for e in range(2):
                pool.memset(QT[e][:], 0.0).then_inc(pool_zeroed, 1)
                pool.memset(KT[e][:], 0.0).then_inc(pool_zeroed, 1)
            pool.wait_ge(wq_loaded, 16)
            pool.wait_ge(wkv_loaded, 16)
            with pool.Fori(0, NJ) as j:
                pool.wait_ge(v_full, j + 1)
                for e in range(2):
                    h = 2 * j + e
                    pool.tensor_copy(WQP[:, :, e, :], WQ[:, :, bass.ds(h * (NOPE + ROPE), NOPE)])
                    pool.tensor_copy(WKP[:, :, e, :], WKV[:, :, bass.ds(h * (NOPE + VH), NOPE)])
                    ins = pool.tensor_copy(WVP[:, :, e, :], WKV[:, :, bass.ds(h * (NOPE + VH) + NOPE, VH)])
                ins.then_inc(wp_ready, 1)


_INS = ["x_prompt", "x_sample", "c_prompt", "c_sample", "cache_kv_latent", "cache_k_rope", "state_conv",
        "w_ada", "b_ada", "norm_mix_g", "w_in", "q_norm_g", "w_uq", "kv_norm_g", "w_ukv", "conv_w", "conv_b",
        "w_out", "norm_ffn_g", "w_gate", "w_up", "w_down", "final_norm_g"]
_OUTS = [(1, S, D), (1, SD, D), (1, 1, S, KVR), (1, 1, S, ROPE), (1, 1, CW - 1, DCONV),
         (1, 1, SD, KVR), (1, 1, SD, ROPE), (1, 1, CW - 1, DCONV)]


def constants():
    inv = np.float32(10000.0) ** (-np.arange(HALF, dtype=np.float32) / np.float32(HALF))
    pos = np.concatenate([np.arange(S), PAST + np.arange(SD)]).astype(np.float32)
    ang = (pos[:, None] * inv[None, :]).astype(np.float32)
    cos = np.tile(np.cos(ang).T, (HEADS, 1)).astype(np.float32)
    sin = np.tile(np.sin(ang).T, (HEADS, 1)).astype(np.float32)
    qmask = np.zeros((KD, T), np.float32)
    kmask = np.zeros((KD, TK), np.float32)
    for t in range(KD):
        qmask[t, t * P:t * P + CHUNK] = -BIG
        kmask[t, t * P + CHUNK:(t + 1) * P] = 1.0
    return {"c_ident": np.eye(P, dtype=np.float32), "c_cos": cos, "c_sin": sin, "c_qmask": qmask, "c_kmask": kmask}


def kernel(**inputs):
    import concourse.bacc as bacc
    from concourse.bass_utils import run_bass_kernel_spmd

    nc = bacc.Bacc("TRN2", target_bir_lowering=False, num_devices=1)
    arrays, args = {}, []
    named = [(n, np.ascontiguousarray(inputs[n])) for n in _INS] + list(constants().items())
    for name, a in named:
        arrays[f"in_{name}"] = a
        args.append(nc.dram_tensor(f"in_{name}", a.shape, mybir.dt.from_np(a.dtype), kind="ExternalInput").ap())
    for i, shape in enumerate(_OUTS):
        args.append(nc.dram_tensor(f"out_{i}", shape, F32, kind="ExternalOutput").ap())
    build(nc, *args)
    r = run_bass_kernel_spmd(nc, [arrays], core_ids=[0])
    return tuple(r.results[0][f"out_{i}"] for i in range(len(_OUTS)))
```

```python
from contextlib import ExitStack

import numpy as np

import concourse.bass as bass
from concourse import mybir

F32 = mybir.dt.float32
F32R = mybir.dt.float32r
ALU = mybir.AluOpType
ACT = mybir.ActivationFunctionType
AX_X = mybir.AxisListType.X

P = 128
D = 1024
KD = D // P
S = 1024
SD = 32
T = S + SD
NCH = 3
CH = T // NCH
PAST = 256
TK = S + PAST + SD
HEADS = 8
NOPE, ROPE, VH = 64, 32, 64
HALF = ROPE // 2
KVR, QR = 256, 768
KQ, KKV = QR // P, KVR // P
DCONV = 512
NJ = DCONV // P
CW = 3
DFF = 2816
NG = DFF // (2 * P)
CHUNK = 64
EPS = 1e-6
SCALE = float(NOPE + ROPE) ** -0.5
BIG = 1e30
ARENA = 207 * 1024

C_KV = QR
C_KR = C_KV + KVR
C_U = C_KR + ROPE
C_GB = C_U + DCONV
C_GC = C_GB + DCONV

V_BADA, V_NMIX, V_QG, V_KVG, V_CW, V_CB, V_FFN, V_FIN, V_C, V_ST, V_END = (
    0, 48, 56, 62, 64, 76, 80, 88, 96, 112, 120)
SH1, SC1, G1, SH2, SC2, G2 = (8 * n for n in range(6))

S_CONV = 0
S_COUT = S_CONV + 3 * NJ
S_CKV = S_COUT + 4
S_KR = S_CKV + KKV
S_CQ = S_KR + 1
S_AOUT = S_CQ + KQ
S_FFN = S_AOUT + 4
S_LOOP = S_FFN + 4
S_LAST = S_LOOP + 6 * (NG - 1)
S_END = S_LAST + 2
G_N1 = 0
G_CONV = 1
G_COUT = G_CONV + 3 * NJ
G_CKV = G_COUT + KD
G_KR = G_CKV + KKV
G_NKV = G_KR + 1
G_CQ = G_NKV + 1
G_NQ = G_CQ + KQ
G_X1 = G_NQ + 1
G_AOUT = G_X1 + 2
G_N2 = G_AOUT + KD
G_FFN = G_N2 + 1
G_LOOP = G_FFN + 4
G_LAST = G_LOOP + 12 * (NG - 1)
G_FIN = G_LAST + 8

UNITS = 9
PAIR_UNITS = 2 * UNITS


UNIT_ORDER = [it for n in range(UNITS) for it in ((0, (UNITS - 1 - n) % UNITS), (1, (n - 1) % UNITS))]


def unit_of(u):
    e, t = UNIT_ORDER[u]
    if t < UNITS - 1:
        return e, P * t, P, 0, P * (t + 1), [(v, P) for v in range(t + 1)]
    return e, S, SD, S, PAST + SD, [(8, P), (9, P), (10, SD)]


def build(nc, x_prompt, x_sample, c_prompt, c_sample, cache_kv_latent, cache_k_rope, state_conv,
          w_ada, b_ada, norm_mix_g, w_in, q_norm_g, w_uq, kv_norm_g, w_ukv, conv_w, conv_b, w_out,
          norm_ffn_g, w_gate, w_up, w_down, final_norm_g, c_ident, c_cos, c_sin, c_qmask, c_kmask,
          y_prompt, y_sample, lat_p, kr_p, cv_p, lat_s, kr_s, cv_s):
    ctx = ExitStack()
    with ctx:
        U = T * 4
        start = nc.sbuf_base
        ctx.enter_context(nc.sbuf_tensor("arena", [P, ARENA // 4], F32))

        def at(name, shape, dt, off):
            size = 4 * int(np.prod(shape[1:]))
            assert off % 32 == 0 and off + size <= ARENA, (name, off, size)
            return nc.alloc_sbuf_tensor_at(name, shape, dt, offset=ARENA0 + off)

        ARENA0 = -(-start // 32) * 32
        X = at("X", [P, KD, T], F32, 0)
        RAW = at("RAW", [P, 2, KD * P], F32, 8 * U)
        WH = at("WH", [P, 2, KD * P], F32R, 8 * U + 8192)
        WL = at("WL", [P, 2, KD * P], F32R, 8 * U + 16384)
        o = 8 * U + 24576
        COS = at("COS", [P, T], F32, o)
        SIN = at("SIN", [P, T], F32, o + U)
        PTS = at("PTS", [P, 2, KD * P], F32, o)
        IDENT = at("IDENT", [P, P], F32, o + 2 * U)
        ONES = at("ONES", [P, P], F32, o + 2 * U + 512)
        VEC = at("VEC", [P, P], F32, o + 2 * U + 1024)
        CS = at("CS", [P, KD, 2], F32, o + 2 * U + 1536)
        MOD = at("MOD", [P, 48, 2], F32, o + 2 * U + 1600)
        A1 = at("A1", [P, 2, KD], F32, o + 2 * U + 1984)
        A2 = at("A2", [P, 2, KD], F32, o + 2 * U + 2048)
        MX = at("MX", [P, 2], F32, o + 2 * U + 2112)
        NM = at("NM", [P, 2], F32, o + 2 * U + 2144)
        SUM = at("SUM", [P, 2], F32, o + 2 * U + 2176)
        RCP = at("RCP", [P, 2], F32, o + 2 * U + 2208)
        ST = at("ST", [P, NJ, 2 * (CW - 1)], F32, o + 2 * U + 2240)
        MS = at("MS", [P, UNITS + 7], F32, o + 2 * U + 2304)
        RT = at("RT", [P, UNITS + 7], F32, o + 2 * U + 2368)
        B = o + 2 * U + 2432
        HH = at("HH", [P, KD, T], F32R, B)
        HL = at("HL", [P, KD, T], F32R, B + 8 * U)
        YH = at("YH", [P, NJ, T], F32R, B + 16 * U)
        YL = at("YL", [P, NJ, T], F32R, B + 20 * U)
        ADA0 = at("ADA0", [P, KD, 16 * P], F32, B)
        XN = at("XN", [P, KD, T], F32, B + 16 * U)
        XJ = at("XJ", [P, D], F32, B + 16 * U)
        XR = at("XR", [P, 4, D], F32, B + 24 * U)
        VR = at("VR", [P, P], F32, B + 24 * U + 16384)
        UU = at("UU", [P, T + 2], F32, B + 24 * U)
        CC = at("CC", [P, T], F32, B + 24 * U + 4256)
        BB = at("BB", [P, T], F32, B + 25 * U + 4256)
        GG = at("GG", [P, T + 4], F32, B + 26 * U + 4256)
        ADA = at("ADA", [P, 2, KD, 2 * P], F32, B + 28 * U + 4256)
        ACC = at("ACC", [P, 2, 2 * P], F32, B + 28 * U + 4256 + 16384)
        CQ = at("CQ", [P, KQ, T], F32, B + 16 * U)
        CKV = at("CKV", [P, KKV, T], F32, B + 22 * U)
        KR = at("KR", [P, TK], F32, B + 24 * U)
        o = B + 24 * U + 5248
        SQ2 = at("SQ2", [P, T], F32, o)
        SSK = at("SSK", [P, T], F32, o + U)
        SSQ = at("SSQ", [P, T], F32, o + 2 * U)
        TR = at("TR", [P, T], F32, o + 3 * U)
        WQ = at("WQ", [P, KQ, QR], F32, o + 4 * U)
        QROT = at("QROT", [P, 2, T], F32, B)
        WKV = at("WKV", [P, KKV, HEADS * (NOPE + VH)], F32, B)
        LAT = at("LAT", [P, KKV, TK], F32, B + 2 * U)
        o = B + 2 * U + 10496
        KT = [at(f"KT{e}", [P, TK], F32, o + 5248 * e) for e in range(2)]
        QT = [at(f"QT{e}", [P, T], F32, o + 10496 + U * e) for e in range(2)]
        o = o + 10496 + 2 * U
        V = at("V", [P, 11, P], F32, o)
        WQP = at("WQP", [P, KQ, 2, NOPE], F32, o + 5632)
        WKP = at("WKP", [P, KKV, 2, NOPE], F32, o + 8704)
        WVP = at("WVP", [P, KKV, 2, VH], F32, o + 10752)
        o = o + 12800
        AOH = at("AOH", [P, NJ, T], F32R, o)
        assert o + 4 * U <= B + 16 * U
        QF = at("QF", [P, T], F32, o)
        PL = at("PL", [P, 2, KVR], F32, o + U)
        PK = at("PK", [P, 2, ROPE], F32, o + U + 2048)
        LO = at("LO", [P, 2, KVR], F32, o + U + 2304)
        KO = at("KO", [P, 2, ROPE], F32, o + U + 4352)
        WQR = at("WQR", [P, KQ, 2, HEADS, HALF], F32, o + U + 4608)
        PP = at("PP", [P, 2, D], F32, B + 22 * U)
        AOL = at("AOL", [P, NJ, T], F32R, B + 24 * U)
        SQ3 = at("SQ3", [P, 2, T], F32, B)
        SS3 = at("SS3", [P, T], F32, B + 2 * U)
        TT3 = at("TT3", [P, 2, T], F32, B + 3 * U)
        H2H = at("H2H", [P, KD, T], F32R, B + 16 * U)
        H2L = at("H2L", [P, KD, T], F32R, B + 24 * U)
        AH = at("AH", [P, 4, T], F32R, B + 5 * U)
        AL = at("AL", [P, 4, T], F32R, B + 9 * U)
        SG = at("SG", [P, 2, T], F32, B + 13 * U)
        SQ4 = at("SQ4", [P, 2, T], F32, B + 16 * U)
        SS4 = at("SS4", [P, T], F32, B + 18 * U)
        ORW = at("ORW", [P, 2, D], F32, B + 19 * U)

        PS = ctx.enter_context(nc.psum_tensor("PS", [P, 8, 512], F32))
        rope_dram = nc.dram_tensor("q_rope_rows", [2, P, T], F32, kind="Internal").ap()

        def sem(name):
            return ctx.enter_context(nc.semaphore(name))

        vec_loaded = sem("vec_loaded")
        ident_loaded = sem("ident_loaded")
        tables_loaded = sem("tables_loaded")
        ones_set = sem("ones_set")
        vec_full = sem("vec_full")
        vec_ready = sem("vec_ready")
        x_turned = sem("x_turned")
        x_kept_dve = sem("x_kept_dve")
        x_kept_act = sem("x_kept_act")
        cond_ready = sem("cond_ready")
        square_summed = sem("square_summed")
        tok_var = sem("tok_var")
        tok_dev = sem("tok_dev")
        tok_rstd = sem("tok_rstd")
        ada0_used = sem("ada0_used")
        acc_step = sem("acc_step")
        acc_ready = sem("acc_ready")
        ada_used = sem("ada_used")
        mod_kept = sem("mod_kept")
        scales_ready = sem("scales_ready")
        w_hi = sem("w_hi")
        w_lo = sem("w_lo")
        kr_half_loaded = sem("kr_half_loaded")
        squared = sem("squared")
        summed = sem("summed")
        dev_ready = sem("dev_ready")
        rstd_ready = sem("rstd_ready")
        h_scaled = sem("h_scaled")
        h_full = sem("h_full")
        h_hi = sem("h_hi")
        h_lo = sem("h_lo")
        pads_set = sem("pads_set")
        gated = sem("gated")
        conv_step = sem("conv_step")
        y_full = sem("y_full")
        y_hi = sem("y_hi")
        y_lo = sem("y_lo")
        states_kept = sem("states_kept")
        k_rope_step = sem("k_rope_step")
        lat_ready = sem("lat_ready")
        q_ready = sem("q_ready")
        wq_loaded = sem("wq_loaded")
        wkv_loaded = sem("wkv_loaded")
        past_loaded = sem("past_loaded")
        past_turned = sem("past_turned")
        past_kept = sem("past_kept")
        zeroed = sem("zeroed")
        wq_rotary = sem("wq_rotary")
        pool_zeroed = sem("pool_zeroed")
        mask_loaded = sem("mask_loaded")
        q_rope_step = sem("q_rope_step")
        rope_stored = sem("rope_stored")
        k_rope_copied = sem("k_rope_copied")
        rows_turned = sem("rows_turned")
        rows_kept = sem("rows_kept")
        wqp_ready = sem("wqp_ready")
        wkvp_ready = sem("wkvp_ready")
        q_full = sem("q_full")
        k_full = sem("k_full")
        v_full = sem("v_full")
        q_kept = sem("q_kept")
        k_kept = sem("k_kept")
        v_kept = sem("v_kept")
        rope_loaded = sem("rope_loaded")
        s_full = sem("s_full")
        max_ready = sem("max_ready")
        nm_ready = sem("nm_ready")
        exp_done = sem("exp_done")
        rcp_ready = sem("rcp_ready")
        p_ready = sem("p_ready")
        p_turned = sem("p_turned")
        pt_kept = sem("pt_kept")
        o_full = sem("o_full")
        o_hi = sem("o_hi")
        o_kept = sem("o_kept")
        silu_ready = sem("silu_ready")
        a_full = sem("a_full")
        a_hi = sem("a_hi")
        y_ready = sem("y_ready")
        y_turned = sem("y_turned")
        y_kept_dve = sem("y_kept_dve")
        y_kept_act = sem("y_kept_act")
        states_stored = sem("states_stored")
        x_loaded = [sem(f"x_loaded{n}") for n in range(4)]
        ada0_loaded = [sem(f"ada0_loaded{n}") for n in range(4)]
        ada_loaded = [sem(f"ada_loaded{n}") for n in range(2)]
        raw_loaded = [sem(f"raw_loaded{n}") for n in range(2)]
        ps_full = [sem(f"ps_full{n}") for n in range(2)]
        ps_free = [sem(f"ps_free{n}") for n in range(2)]
        rows_stored = [sem(f"rows_stored{n}") for n in range(2)]
        y_stored = [sem(f"y_stored{n}") for n in range(2)]
        block = ctx.enter_context(nc.Block())

        win = w_in[0].rearrange("(k p) m -> p k m", p=P)
        wada = w_ada[0].rearrange("(k p) m -> p k m", p=P)
        wout = w_out[0].rearrange("(k p) m -> p k m", p=P)
        wg = w_gate[0].rearrange("(k p) m -> p k m", p=P)
        wu = w_up[0].rearrange("(k p) m -> p k m", p=P)
        wd = w_down[0].rearrange("(k p) m -> p k m", p=P)

        def raw(s, k=KD):
            return RAW[:, s % 2, :].rearrange("p (k m) -> p k m", k=k)

        def hi_lo(s, k=KD):
            return [w[:, s % 2, :].rearrange("p (k m) -> p k m", k=k) for w in (WH, WL)]

        def chunks(g, rows=slice(0, P)):
            b = NCH * (g % 2)
            return PS[rows, b:b + NCH, 0:CH]

        def in_chunks(ap):
            return ap.rearrange("p (n c) -> p n c", n=NCH)

        def streams(g):
            b = NCH * (g % 2)
            return [(PS[:, b:b + 2, 0:CH], slice(0, 2 * CH), 0), (PS[:, b + 2, 0:S - 2 * CH], slice(2 * CH, S), 0),
                    (PS[:, b + 2, S - 2 * CH:CH], slice(S, T), 1)]

        def tile_of(buf, k):
            return buf[:, k, :] if isinstance(k, int) else \
                buf[:, bass.ds(k, 1), :].rearrange("p a t -> p (a t)")

        def wait_filled(eng, g, dyn=0):
            eng.wait_ge(ps_full[g % 2], dyn + (g // 2 + 1))

        def wait_kept(eng, g, dyn=0):
            eng.wait_ge(ps_free[g % 2], dyn + (g // 2 + 2))

        def wait_loaded(eng, s, dyn=0):
            eng.wait_ge(raw_loaded[s % 2], 16 * dyn + 16 * (s // 2 + 1))

        @block.sync
        def _(sp):
            sp.dma_start(IDENT[:], c_ident).then_inc(ident_loaded, 16)

            for n in range(UNITS):
                if n >= 4:
                    sp.wait_ge(x_turned, n - 3)
                    sp.wait_ge(square_summed, n - 3)
                src = x_prompt[0, n * P:(n + 1) * P, :] if n < KD else x_sample[0]
                sp.dma_start(XR[0:P if n < KD else SD, n % 4], src).then_inc(x_loaded[n % 4], 16)
            for n in range(4):
                sp.dma_start(ADA0[:, :, n * 4 * P:(n + 1) * 4 * P], wada[:, :, n * 4 * P:(n + 1) * 4 * P])\
                    .then_inc(ada0_loaded[n], 16)

            def load_ada(n, col):
                sp.dma_start(ADA[:, n % 2], wada[:, :, bass.ds(col, 2 * P)]).then_inc(ada_loaded[n % 2], 16)

            def load_slot(s, src, k=KD, dyn=0):
                sp.wait_ge(w_lo, 2 * dyn + (s + 1))
                sp.dma_start(raw(s, k), src).then_inc(raw_loaded[s % 2], 16)

            with sp.Fori(0, 2) as i:
                for n in range(6):
                    j, q = divmod(n, 3)
                    load_slot(n, win[:, :, bass.ds((2 * i + j) * P + (C_U, C_GC, C_GB)[q], P)], dyn=3 * i)
                    sp.wait_ge(acc_ready, 12 * i + (2 * n + 2))
                    load_ada(n, (6 * i + (n + 8)) * (2 * P))
            with sp.Fori(0, 2) as i:
                for n in range(2):
                    load_slot(S_COUT + n, wout[:, NJ:KD, bass.ds((2 * i + n) * (2 * P), 2 * P)], k=NJ, dyn=i)
                    sp.wait_ge(acc_ready, 4 * i + (2 * n + 26))
                    load_ada(n, (2 * i + (n + 20)) * (2 * P))
            sp.dma_start(COS[:], c_cos).then_inc(tables_loaded, 16)
            sp.dma_start(SIN[:], c_sin).then_inc(tables_loaded, 16)
            sp.wait_ge(states_kept, NJ)
            for dst, col in ((cv_p, 0), (cv_s, CW - 1)):
                for j in range(NJ):
                    sp.dma_start(dst[0, 0][:, j * P:(j + 1) * P].rearrange("r p -> p r"),
                                 ST[:, j, col:col + CW - 1],
                                 allow_slow_non_contiguous=True).then_inc(states_stored, 16)
            for n in range(KKV):
                load_slot(S_CKV + n, win[:, :, C_KV + n * P:C_KV + (n + 1) * P])
            sp.wait_ge(w_lo, S_KR + 1)
            for q, done in ((0, kr_half_loaded), (1, raw_loaded[S_KR % 2])):
                sp.dma_start(raw(S_KR)[:, :, 32 * q:32 * q + HALF],
                             win[:, :, C_KR + q * HALF:C_KR + (q + 1) * HALF]).then_inc(done, 16)
            sp.wait_ge(ada_used, 17)
            sp.dma_start(WQ[:], w_uq[0].rearrange("(k p) m -> p k m", p=P)).then_inc(wq_loaded, 16)
            for n in range(KQ):
                load_slot(S_CQ + n, win[:, :, n * P:(n + 1) * P])
            for n in range(2):
                load_slot(S_AOUT + n, wout[:, 0:NJ, n * 2 * P:(n + 1) * 2 * P], k=NJ)
            wait_filled(sp, G_CQ + KQ - 1)
            sp.dma_start(PL[:], cache_kv_latent[0, 0].rearrange("(n p) m -> p n m", p=P)).then_inc(past_loaded, 16)
            sp.dma_start(PK[:], cache_k_rope[0, 0].rearrange("(n p) m -> p n m", p=P)).then_inc(past_loaded, 16)
            sp.wait_ge(pool_zeroed, 4)
            for e, row in ((0, 80), (1, 16)):
                sp.dma_start(QT[e][row:row + KD, :], c_qmask).then_inc(mask_loaded, 16)
                sp.dma_start(KT[e][row:row + KD, :], c_kmask).then_inc(mask_loaded, 16)
            for n in range(UNITS):
                sp.wait_ge(rows_kept, n + 1)
                r, dst, kdst = (slice(0, P), lat_p, kr_p) if n < KD else (slice(0, SD), lat_s, kr_s)
                t = slice(n * P, (n + 1) * P) if n < KD else slice(0, SD)
                sp.dma_start(dst[0, 0, t, :], LO[r, n % 2]).then_inc(rows_stored[n % 2], 16)
                sp.dma_start(kdst[0, 0, t, :], KO[r, n % 2]).then_inc(rows_stored[n % 2], 16)
            sp.wait_ge(q_rope_step, 4)
            for q in range(2):
                sp.dma_start(rope_dram[q], QROT[:, q]).then_inc(rope_stored, 16)
            sp.wait_ge(rope_stored, 32)
            sp.dma_start(WKV[:], w_ukv[0].rearrange("(k p) m -> p k m", p=P)).then_inc(wkv_loaded, 16)

            def load_rope(first_row):
                for e, rows in ((0, (64, 96)), (1, (0, 32))):
                    for q in range(2):
                        sp.dma_start(QT[e][rows[q]:rows[q] + HALF, :],
                                     rope_dram[q, bass.ds(first_row + HALF * e, HALF), :]).then_inc(rope_loaded, 16)

            load_rope(0)
            with sp.Fori(1, NJ) as j:
                sp.wait_ge(s_full, PAIR_UNITS * j)
                load_rope(2 * HALF * j)
            for n in range(2, 4):
                load_slot(S_AOUT + n, wout[:, 0:NJ, n * 2 * P:(n + 1) * 2 * P], k=NJ)

            def load_gate_up(s, tile, dyn=0):
                for n in range(4):
                    load_slot(s + n, (wg, wu)[n % 2][:, :, bass.ds(tile * P + (n // 2) * P, P)], dyn=dyn)

            def load_down(s, tile, dyn=0):
                for n in range(2):
                    load_slot(s + n, wd[:, bass.ds(tile, 2), n * 512:(n + 1) * 512], k=2, dyn=dyn)

            load_gate_up(S_FFN, 0)
            with sp.Fori(0, (NG - 1) // 2) as i:
                for n in range(2):
                    load_gate_up(S_LOOP + 6 * n, 4 * i + 2 * (n + 1), dyn=6 * i)
                    load_down(S_LOOP + 6 * n + 4, 4 * i + 2 * n, dyn=6 * i)
            load_down(S_LAST, 2 * (NG - 1))
            for n in range(UNITS):
                sp.wait_ge(y_kept_dve, n + 1)
                sp.wait_ge(y_kept_act, n + 1)
                dst = y_prompt[0, n * P:(n + 1) * P, :] if n < KD else y_sample[0]
                sp.dma_start(dst, ORW[0:P if n < KD else SD, n % 2]).then_inc(y_stored[n % 2], 16)
            sp.wait_ge(states_stored, 16 * 2 * NJ)
            for n in range(2):
                sp.wait_ge(rows_stored[n], 32 * (5 - n))
                sp.wait_ge(y_stored[n], 16 * (5 - n))

        @block.tensor
        def _(pe):
            pe.sem_inc(ada_used, 1)
            pe.sem_inc(q_full, 1)
            pe.sem_inc(v_full, 1)
            pe.wait_ge(vec_loaded, 16 * 11)
            pe.wait_ge(ident_loaded, 16)
            pe.transpose(PS[:, 7, 0:V_END], VR[0:V_END, :], IDENT[0:V_END, 0:V_END]).then_inc(vec_full, 1)
            for n in range(UNITS):
                r = P if n < KD else SD
                pe.wait_ge(x_loaded[n % 4], 16 * (n // 4 + 1))
                if n >= 2:
                    pe.wait_ge(x_kept_dve, n - 1)
                    pe.wait_ge(x_kept_act, n - 1)
                for k in range(KD):
                    mm = pe.transpose(PS[:, 2 * (n % 2) + k // 4, (k % 4) * P:(k % 4) * P + r],
                                      XR[0:r, n % 4, k * P:(k + 1) * P], IDENT[0:r, 0:r])
                mm.then_inc(x_turned, 1)

            def ada(n, bank, col, dyn=0):
                pe.wait_ge(acc_ready, 2 * dyn + (2 * n + 6))
                for m in range(2):
                    for st in range(2):
                        mm = pe.matmul(PS[:, bank, bass.ds(col + (2 * m + st), 1)], ACC[:, st, m * P:(m + 1) * P],
                                       ONES[:, 0:1], start=True, stop=True)
                mm.then_inc(ada_used, 1)

            def begin_slot(s, dyn=0):
                pe.wait_ge(w_lo, 2 * dyn + (s + 3))

            def begin_group(g, dyn=0):
                pe.wait_ge(ps_free[g % 2], dyn + (g // 2 + 1))

            def product(g, weights, moving, ks, before=None):
                b = NCH * (g % 2)
                for k in ks:
                    if before:
                        before(k)
                    for w, xs in ((weights[0][k], moving), (weights[1][k], moving[:1])):
                        for n in range(NCH):
                            for x in xs:
                                mm = pe.matmul(PS[:, b + n, 0:CH], w, x[k][:, n * CH:(n + 1) * CH],
                                               start=(k == 0 and w is weights[0][k] and x is xs[0]),
                                               stop=(k == ks[-1] and w is weights[1][k]))
                mm.then_inc(ps_full[g % 2], 1)
                return mm

            def cut(pair, first=0):
                return [{k: buf[:, first + k, :] for k in range(buf.shape[1] - first)} for buf in pair]

            def weights_of(s, k=KD, m=0):
                return [{n: w[:, n, m * P:(m + 1) * P] for n in range(k)} for w in hi_lo(s, k)]

            def total(g, ss, tiles_summed):
                pe.wait_ge(summed, tiles_summed)
                begin_group(g)
                for n in range(NCH):
                    mm = pe.matmul(PS[:, NCH * (g % 2) + n, 0:CH], ONES[:], ss[:, n * CH:(n + 1) * CH],
                                   start=True, stop=True)
                mm.then_inc(ps_full[g % 2], 1)

            def spread(g, norm):
                pe.wait_ge(tok_rstd, norm)
                begin_group(g)
                for n in range(UNITS):
                    r = P if n < KD else SD
                    mm = pe.matmul(PS[:, NCH * (g % 2) + n // 4, (n % 4) * P:(n % 4) * P + r],
                                   RT[0:r, n:n + 1].broadcast_to([r, P]), IDENT[0:r, 0:r], start=True, stop=True)
                mm.then_inc(ps_full[g % 2], 1)

            pe.wait_ge(cond_ready, 1)
            for m in range(16):
                if m % 4 == 0:
                    pe.wait_ge(ada0_loaded[m // 4], 16)
                if m == 2:
                    pe.wait_ge(x_kept_dve, UNITS)
                    pe.wait_ge(x_kept_act, UNITS)
                    spread(G_N1, 1)
                for k in range(KD):
                    mm = pe.matmul(PS[:, 6, 2 * m:2 * m + 2], ADA0[:, k, m * P:(m + 1) * P], CS[:, k, :],
                                   start=(k == 0), stop=(k == KD - 1))
            mm.then_inc(ada0_used, 1)
            h = cut((HH, HL))
            with pe.Fori(0, 2) as i:
                for n in range(6):
                    begin_slot(n, 3 * i)
                    begin_group(G_CONV + n, 3 * i)
                    product(G_CONV + n, weights_of(n), h, range(KD),
                            before=(lambda k: pe.wait_ge(h_lo, k + 1)) if n == 0 else None)
                    ada(n, 7, 24 * i + 4 * n, 6 * i)
            y = cut((YH, YL))
            with pe.Fori(0, 2) as i:
                for n in range(2):
                    begin_slot(S_COUT + n, i)
                    for m in range(2):
                        g = G_COUT + 2 * n + m
                        begin_group(g, 2 * i)
                        product(g, weights_of(S_COUT + n, NJ, m), y, range(NJ),
                                before=(lambda k: pe.wait_ge(y_lo, k + 2)) if n + m == 0 else None)
                    ada(n, 6, 8 * i + 4 * n, 2 * i + 12)
            for n in range(KKV + 1):
                begin_slot(S_CKV + n)
                begin_group(G_CKV + n)
                product(G_CKV + n, weights_of(S_CKV + n), h, range(KD))
            total(G_NKV, SSK, 1)
            with pe.Fori(0, KQ // 2) as i:
                for n in range(2):
                    begin_slot(S_CQ + n, i)
                    begin_group(G_CQ + n, i)
                    product(G_CQ + n, weights_of(S_CQ + n), h, range(KD))
            total(G_NQ, SSQ, 7)
            pe.wait_ge(past_loaded, 32)
            for n in range(2):
                for f in range(KKV):
                    pe.transpose(PS[:, 6, (2 * f + n) * P:(2 * f + n + 1) * P], PL[:, n, f * P:(f + 1) * P], IDENT[:])
                for q in range(2):
                    mm = pe.transpose(PS[0:HALF, 7, (2 * q + n) * P:(2 * q + n + 1) * P],
                                      PK[:, n, q * HALF:(q + 1) * HALF], IDENT[:])
            mm.then_inc(past_turned, 1)

            pe.wait_ge(wq_rotary, 2)
            for q in range(2):
                begin_group(G_X1 + q)
                for k in range(KQ):
                    if q == 0:
                        pe.wait_ge(q_ready, k + 1)
                    for n in range(NCH):
                        mm = pe.matmul(PS[:, NCH * ((G_X1 + q) % 2) + n, 0:CH],
                                       WQR[:, k, q].rearrange("p h c -> p (h c)"),
                                       CQ[:, k, n * CH:(n + 1) * CH], start=(k == 0), stop=(k == KQ - 1))
                mm.then_inc(ps_full[(G_X1 + q) % 2], 1)
            def query_product(j):
                pe.wait_ge(wqp_ready, j + 1)
                pe.wait_ge(exp_done, PAIR_UNITS * j + 1)
                for k in range(KQ):
                    for n in range(NCH):
                        mm = pe.matmul(PS[:, n, 0:CH], WQP[:, k].rearrange("p e d -> p (e d)"),
                                       CQ[:, k, n * CH:(n + 1) * CH], start=(k == 0), stop=(k == KQ - 1))
                mm.then_inc(q_full, 1)

            begin_group(G_X1 + 2)
            begin_group(G_X1 + 3)
            query_product(0)
            pe.wait_ge(lat_ready, 4)
            pe.wait_ge(k_rope_step, 4)
            pe.wait_ge(past_kept, 3)
            for n in range(UNITS):
                r = P if n < KD else SD
                col = n * P if n < KD else S + PAST
                if n >= 2:
                    pe.wait_ge(rows_kept, n - 1)
                for f in range(KKV):
                    pe.transpose(PS[0:r, 6 + n % 2, f * P:(f + 1) * P], LAT[:, f, col:col + r], IDENT[:])
                pe.transpose(PS[0:r, 6 + n % 2, KVR:KVR + 48], KR[0:48, col:col + r], IDENT[0:48, 0:48])\
                    .then_inc(rows_turned, 1)
            pe.wait_ge(rows_kept, UNITS)
            pe.wait_ge(mask_loaded, 64)

            def pair(j, more):
                pe.wait_ge(wkvp_ready, j + 1)
                pe.wait_ge(pt_kept, PAIR_UNITS * j + 1)
                pe.wait_ge(o_kept, PAIR_UNITS * j + 1)
                for n in range(4):
                    for k in range(KKV):
                        mm = pe.matmul(PS[:, 3 + n, 0:TK // 4], WKP[:, k].rearrange("p e d -> p (e d)"),
                                       LAT[:, k, n * (TK // 4):(n + 1) * (TK // 4)], start=(k == 0), stop=(k == 1))
                mm.then_inc(k_full, 1)
                for v in range(11):
                    r = P if v < 10 else SD
                    if v == 4:
                        pe.wait_ge(q_kept, 2 * j + 2)
                    for k in range(KKV):
                        mm = pe.matmul(PS[0:r, (7, 0, 1)[v // 4], (v % 4) * P:(v % 4 + 1) * P],
                                       LAT[:, k, v * P:v * P + r], WVP[:, k].rearrange("p e d -> p (e d)"),
                                       start=(k == 0), stop=(k == 1))
                mm.then_inc(v_full, 1)
                pe.wait_ge(k_kept, 2 * j + 2)
                pe.wait_ge(v_kept, j + 1)
                pe.wait_ge(rope_loaded, 64 * j + 64)

                def scores(u):
                    e, q0, nq, k0, nk, _ = unit_of(u)
                    if u >= 2:
                        pe.wait_ge(exp_done, PAIR_UNITS * j + u)
                    for c in range(0, nk, 512):
                        w = min(512, nk - c)
                        mm = pe.matmul(PS[0:nq, 2 * (u % 2) + c // 512, 0:w], QT[e][:, q0:q0 + nq],
                                       KT[e][:, k0 + c:k0 + c + w], start=True, stop=True)
                    mm.then_inc(s_full, 1)

                def turn(u):
                    e, q0, nq, k0, nk, tiles = unit_of(u)
                    pe.wait_ge(p_ready, PAIR_UNITS * j + (u + 1))
                    if u >= 1:
                        pe.wait_ge(pt_kept, PAIR_UNITS * j + (u + 1))
                    for b, (_, r) in enumerate(tiles):
                        mm = pe.transpose(PS[0:r, 4 + b // 4, (b % 4) * P:(b % 4 + 1) * P],
                                          PP[:, u % 2, b * P:b * P + r], IDENT[:])
                    mm.then_inc(p_turned, 1)

                def values(u):
                    e, q0, nq, k0, nk, tiles = unit_of(u)
                    pe.wait_ge(pt_kept, PAIR_UNITS * j + (u + 2))
                    if u >= 2:
                        pe.wait_ge(o_kept, PAIR_UNITS * j + u)
                    for b, (v, r) in enumerate(tiles):
                        mm = pe.matmul(PS[:, 6 + u % 2, 0:nq], V[0:r, v, :], PTS[0:r, u % 2, b * P:b * P + nq],
                                       start=(b == 0), stop=(b == len(tiles) - 1))
                    mm.then_inc(o_full, 1)

                scores(0)
                for u in range(PAIR_UNITS):
                    if u + 1 < PAIR_UNITS:
                        scores(u + 1)
                    if u >= 1:
                        turn(u - 1)
                    if u >= 2:
                        values(u - 2)
                if more:
                    query_product(j + 1)
                turn(PAIR_UNITS - 1)
                values(PAIR_UNITS - 2)
                values(PAIR_UNITS - 1)

            with pe.Fori(0, NJ - 1) as j:
                pair(j, True)
            pair(NJ - 1, False)

            ao = cut((AOH, AOL))
            pe.wait_ge(o_kept, PAIR_UNITS * NJ + 1)
            with pe.Fori(0, 2) as i:
                for n in range(2):
                    begin_slot(S_AOUT + n, i)
                    for m in range(2):
                        g = G_AOUT + 2 * n + m
                        begin_group(g, 2 * i)
                        product(g, weights_of(S_AOUT + n, NJ, m), ao, range(NJ))
            total(G_N2, SS3, 15)
            h2 = cut((H2H, H2L))

            def gate_up(s, g, dyn_s=0, dyn_g=0, first=False):
                for n in range(4):
                    begin_slot(s + n, dyn_s)
                    begin_group(g + n, dyn_g)
                    product(g + n, weights_of(s + n), h2, range(KD),
                            before=(lambda k: pe.wait_ge(h_lo, KD + k + 1)) if first and n == 0 else None)

            def down(s, g, a0, tiles_ready, dyn_s=0, dyn_g=0):
                pe.wait_ge(a_full, tiles_ready)
                for n in range(2):
                    begin_slot(s + n, dyn_s)
                    for m in range(4):
                        begin_group(g + 4 * n + m, dyn_g)
                        product(g + 4 * n + m, weights_of(s + n, 2, m), cut((AH, AL), a0), range(2))

            gate_up(S_FFN, G_FFN, first=True)
            with pe.Fori(0, (NG - 1) // 2) as i:
                for n in range(2):
                    gate_up(S_LOOP + 6 * n, G_LOOP + 12 * n, 6 * i, 12 * i)
                    down(S_LOOP + 6 * n + 4, G_LOOP + 12 * n + 4, 2 * n, 4 * i + (2 * n + 4), 6 * i, 12 * i)
            down(S_LAST, G_LAST, 0, 2 * NG + 2)
            total(G_FIN, SS4, 23)
            for n in range(UNITS):
                r = P if n < KD else SD
                if n == 0:
                    pe.wait_ge(y_ready, KD)
                if n >= 2:
                    pe.wait_ge(y_kept_dve, n - 1)
                    pe.wait_ge(y_kept_act, n - 1)
                for k in range(KD):
                    mm = pe.transpose(PS[0:r, 2 * (n % 2) + k // 4, (k % 4) * P:(k % 4 + 1) * P],
                                      X[:, k, n * P:n * P + r], IDENT[:])
                mm.then_inc(y_turned, 1)

        @block.scalar
        def _(act):
            def split_hi(s, g, dyn=0, dyn_g=0):
                wait_loaded(act, s, dyn)
                wait_filled(act, g, dyn_g)
                act.activation(WH[:, s % 2, :], RAW[:, s % 2, :], ACT.Copy).then_inc(w_hi, 1)

            act.dma_start(VR[V_BADA:V_NMIX, :], b_ada[0].rearrange("(j p) -> j p", p=P)).then_inc(vec_loaded, 16)
            for row, src in ((V_NMIX, norm_mix_g[0]), (V_QG, q_norm_g[0]), (V_KVG, kv_norm_g[0]),
                             (V_CB, conv_b[0]), (V_FFN, norm_ffn_g[0]), (V_FIN, final_norm_g),
                             (V_C, c_prompt[0]), (V_C + KD, c_sample[0])):
                n = src.shape[0] // P
                act.dma_start(VR[row:row + n, :], src.rearrange("(j p) -> j p", p=P)).then_inc(vec_loaded, 16)
            act.dma_start(VR[V_CW:V_CB, :], conv_w[0].rearrange("w (j p) -> (w j) p", p=P)).then_inc(vec_loaded, 16)
            act.dma_start(VR[V_ST:V_END, :], state_conv[0, 0].rearrange("r (j p) -> (r j) p", p=P))\
                .then_inc(vec_loaded, 16)
            act.wait_ge(vec_ready, 1)
            act.activation(CS[:].rearrange("p k s -> p s k"),
                           VEC[:, V_C:V_C + 2 * KD].rearrange("p (s k) -> p s k", s=2), ACT.Silu)\
                .then_inc(cond_ready, 1)
            for n in range(UNITS):
                r = P if n < KD else SD
                act.wait_ge(x_loaded[n % 4], 16 * (n // 4 + 1))
                if n >= 1:
                    act.wait_ge(square_summed, n)
                act.activation(XJ[0:r, :], XR[0:r, n % 4], ACT.Square, accum_out=MS[0:r, n:n + 1])\
                    .then_inc(square_summed, 1)
                act.wait_ge(x_turned, n + 1)
                act.activation(X[:, 4:8, n * P:n * P + r],
                               PS[:, 2 * (n % 2) + 1, :].rearrange("p (k t) -> p k t", k=4)[:, :, 0:r], ACT.Copy)\
                    .then_inc(x_kept_act, 1)
            act.wait_ge(tok_var, 1)
            act.activation(MS[:, 0:UNITS], MS[:, 0:UNITS], ACT.Sqrt).then_inc(tok_dev, 1)
            wait_loaded(act, 0)
            act.activation(WH[:, 0, :], RAW[:, 0, :], ACT.Copy).then_inc(w_hi, 1)

            act.wait_ge(scales_ready, 2)
            for k in range(KD):
                act.wait_ge(h_scaled, k + 1)
                for st, t in ((0, slice(0, S)), (1, slice(S, T))):
                    ins = act.activation(HH[:, k, t], XN[:, k, t], ACT.Identity,
                                         bias=MOD[:, SH1 + k, st:st + 1], scale=A1[:, st, k:k + 1])
                ins.then_inc(h_hi, 1)

            def root(ss, g):
                wait_kept(act, g)
                act.activation(ss[:], ss[:], ACT.Sqrt).then_inc(dev_ready, 1)

            def modulate(tt, hh, a, shift, n):
                for k in range(KD):
                    act.wait_ge(h_scaled, KD * n + k + 1)
                    for st, t in ((0, slice(0, S)), (1, slice(S, T))):
                        ins = act.activation(tt[:, k % 2, t], tt[:, k % 2, t], ACT.Identity,
                                             bias=MOD[:, shift + k, st:st + 1], scale=a[:, st, k:k + 1])
                    ins.then_inc(h_full, 1)
                    act.wait_ge(h_full, KD * n + k + 1)
                    act.activation(hh[:, k, :], tt[:, k % 2, :], ACT.Copy).then_inc(h_hi, 1)

            def keep(g, dst, dyn=0):
                wait_filled(act, g, dyn)
                act.activation(in_chunks(dst), chunks(g), ACT.Copy).then_inc(ps_free[g % 2], 1)

            with act.Fori(0, 2) as i:
                for n in range(6):
                    j, q = divmod(n, 3)
                    split_hi(n + 1, G_CONV + n - 1, 3 * i, 3 * i)
                    act.wait_ge((y_full, y_lo, y_full)[q], 2 * i + (j + 1))
                    keep(G_CONV + n, (UU[:, 0:T], CC[:], BB[:])[q], 3 * i)
            with act.Fori(0, 2) as i:
                for n in range(2):
                    split_hi(S_COUT + n + 1, G_COUT + 2 * n - 1, i, 2 * i)
            for n in range(KKV):
                if n == 1:
                    act.wait_ge(kr_half_loaded, 16)
                split_hi(S_CKV + n + 1, G_CKV + n - 1)
                keep(G_CKV + n, CKV[:, n, :])
                wait_kept(act, G_CKV + n)
                act.activation((SSK, SQ2)[n][:], CKV[:, n, :], ACT.Square).then_inc(squared, 1)
            split_hi(S_KR + 1, G_KR - 1)
            root(SSK, G_NKV)
            for n in range(KQ):
                split_hi(S_CQ + n + 1, G_CQ + n - 1)
                keep(G_CQ + n, CQ[:, n, :])
                wait_kept(act, G_CQ + n)
                act.wait_ge(summed, n + 1)
                act.activation(SQ2[:], CQ[:, n, :], ACT.Square).then_inc(squared, 1)
            act.wait_ge(wq_loaded, 16)
            wait_filled(act, G_CQ + KQ - 1)
            for q in range(2):
                c = NOPE + q * HALF
                act.activation(WQR[:, :, q], WQ[:].rearrange("p k (h c) -> p k h c", h=HEADS)[:, :, :, c:c + HALF],
                               ACT.Copy).then_inc(wq_rotary, 1)
            root(SSQ, G_NQ)

            act.wait_ge(past_turned, 1)
            act.activation(LAT[:, :, S:S + PAST], PS[:, 6, :].rearrange("p (f t) -> p f t", f=KKV), ACT.Copy)\
                .then_inc(past_kept, 1)
            for q in range(2):
                act.activation(KR[32 * q:32 * q + HALF, S:S + PAST], PS[0:HALF, 7, q * PAST:(q + 1) * PAST], ACT.Copy)\
                    .then_inc(past_kept, 1)
            for n in range(UNITS):
                r = slice(0, P if n < KD else SD)
                act.wait_ge(rows_turned, n + 1)
                if n >= 2:
                    act.wait_ge(rows_stored[n % 2], 32 * (n // 2))
                act.activation(LO[r, n % 2, :], PS[r, 6 + n % 2, 0:KVR], ACT.Copy)
                act.activation(KO[r, n % 2, :].rearrange("p (q d) -> p q d", q=2),
                               PS[r, 6 + n % 2, KVR:KVR + 64].rearrange("p (q d) -> p q d", q=2)[:, :, 0:HALF],
                               ACT.Copy).then_inc(rows_kept, 1)

            with act.Fori(0, NJ) as j:
                act.wait_ge(q_full, j + 2)
                for e in range(2):
                    rows = slice(NOPE * e, NOPE * (e + 1))
                    act.activation(in_chunks(QT[e][rows, :]), PS[rows, 0:NCH, 0:CH], ACT.Copy).then_inc(q_kept, 1)

                def exponentials(u):
                    e, q0, nq, k0, nk, tiles = unit_of(u)
                    act.wait_ge(nm_ready, PAIR_UNITS * j + (u + 1))
                    if u >= 2:
                        act.wait_ge(p_turned, PAIR_UNITS * j + (u - 1))
                    src = PS[0:nq, 2 * (u % 2):2 * (u % 2) + 2, :].rearrange("p b k -> p (b k)")[:, 0:nk]
                    act.activation(PP[0:nq, u % 2, 0:nk], src, ACT.Exp, bias=NM[0:nq, u % 2:u % 2 + 1],
                                   scale=SCALE, accum_out=SUM[0:nq, u % 2:u % 2 + 1]).then_inc(exp_done, 1)

                def keep_turned(u):
                    e, q0, nq, k0, nk, tiles = unit_of(u)
                    act.wait_ge(p_turned, PAIR_UNITS * j + (u + 1))
                    if u >= 2:
                        act.wait_ge(o_full, PAIR_UNITS * j + (u - 1))
                    whole = [r for _, r in tiles].count(P)
                    src = PS[:, 4:6, :].rearrange("p b (k q) -> p (b k) q", q=P)
                    dst = PTS[:, u % 2, :].rearrange("p (k q) -> p k q", q=P)
                    ins = act.activation(dst[:, 0:whole, 0:nq], src[:, 0:whole, 0:nq], ACT.Copy)
                    if whole < len(tiles):
                        ins = act.activation(dst[0:SD, whole, 0:nq], src[0:SD, whole, 0:nq], ACT.Copy)
                    ins.then_inc(pt_kept, 1)

                for u in range(PAIR_UNITS):
                    if u >= 2:
                        keep_turned(u - 2)
                    exponentials(u)
                keep_turned(PAIR_UNITS - 2)
                keep_turned(PAIR_UNITS - 1)

            for m in range(KD):
                if m % 2 == 0:
                    split_hi(S_AOUT + m // 2 + 1, G_AOUT + m - 1)
                wait_kept(act, G_AOUT + m)
                act.wait_ge(summed, m + 7)
                act.activation(SQ3[:, 0, :], X[:, m, :], ACT.Square).then_inc(squared, 1)
            root(SS3, G_N2)
            act.wait_ge(scales_ready, 4)
            modulate(TT3, H2H, A2, SH2, 1)

            def gate_up(s, g, tile, dyn_s=0, dyn_g=0, dyn_t=0):
                for n in range(4):
                    split_hi(s + n + 1, g + n - 1, dyn_s, dyn_g)
                    if n % 2 == 0:
                        act.wait_ge(a_full, dyn_t + (tile + n // 2 + 1))
                        wait_filled(act, g + n, dyn_g)
                        act.activation(in_chunks(SG[:, n // 2, :]), chunks(g + n), ACT.Silu)\
                            .then_inc(ps_free[(g + n) % 2], 1)

            def down(s, g, dyn_s=0, dyn_g=0):
                for n in range(2):
                    split_hi(s + n + 1, g + 4 * n - 1, dyn_s, dyn_g)

            gate_up(S_FFN, G_FFN, 0)
            with act.Fori(0, (NG - 1) // 2) as i:
                for n in range(2):
                    gate_up(S_LOOP + 6 * n, G_LOOP + 12 * n, 2 * (n + 1), 6 * i, 12 * i, 4 * i)
                    down(S_LOOP + 6 * n + 4, G_LOOP + 12 * n + 4, 6 * i, 12 * i)
            split_hi(S_LAST + 1, G_LAST - 1)
            for m in range(KD):
                wait_kept(act, G_LAST + m)
                act.wait_ge(summed, 15 + m)
                act.activation(SQ4[:, 0, :], X[:, m, :], ACT.Square).then_inc(squared, 1)
            root(SS4, G_FIN)
            for n in range(UNITS):
                r = P if n < KD else SD
                act.wait_ge(y_turned, n + 1)
                if n >= 2:
                    act.wait_ge(y_stored[n % 2], 16 * (n // 2))
                act.activation(ORW[0:r, n % 2, 512:D], PS[0:r, 2 * (n % 2) + 1, :], ACT.Copy).then_inc(y_kept_act, 1)

        @block.vector
        def _(dve):
            dve.sem_inc(w_lo, 2)
            dve.sem_inc(y_full, 1)
            dve.sem_inc(y_lo, 1)
            dve.sem_inc(a_full, 2)
            dve.sem_inc(o_kept, 1)
            dve.sem_inc(exp_done, 1)
            dve.sem_inc(pt_kept, 1)
            for n in range(2):
                dve.sem_inc(ps_free[n], 1)
            dve.sem_inc(acc_ready, 4)
            dve.memset(ONES[:], 1.0)
            dve.memset(MS[:], 1.0).then_inc(ones_set, 1)
            dve.wait_ge(vec_full, 1)
            dve.tensor_copy(VEC[:, 0:V_END], PS[:, 7, 0:V_END]).then_inc(vec_ready, 1)
            for n in range(UNITS):
                r = P if n < KD else SD
                dve.wait_ge(x_turned, n + 1)
                dve.tensor_copy(X[:, 0:4, n * P:n * P + r],
                                PS[:, 2 * (n % 2), :].rearrange("p (k t) -> p k t", k=4)[:, :, 0:r])\
                    .then_inc(x_kept_dve, 1)

            def add_square(ss, sq, sums, done=0):
                dve.wait_ge(squared, sums)
                dve.wait_ge(summed, done)
                dve.tensor_tensor(ss[:], ss[:], sq, ALU.add).then_inc(summed, 1)

            dve.wait_ge(square_summed, UNITS)
            dve.tensor_scalar(MS[:, 0:UNITS], MS[:, 0:UNITS], 1.0 / D, EPS, ALU.mult, ALU.add).then_inc(tok_var, 1)
            dve.wait_ge(tok_dev, 1)
            dve.reciprocal(RT[:, 0:UNITS], MS[:, 0:UNITS]).then_inc(tok_rstd, 1)

            def variance(ss, g, width):
                wait_filled(dve, g)
                dve.tensor_scalar(in_chunks(ss[:]), chunks(g), 1.0 / width, EPS, ALU.mult, ALU.add)\
                    .then_inc(ps_free[g % 2], 1)

            def invert(ss, n):
                dve.wait_ge(dev_ready, n + 1)
                dve.reciprocal(ss[:], ss[:]).then_inc(rstd_ready, 1)
                dve.wait_ge(rstd_ready, n + 1)

            def add_bias(bank, first, n, done):
                src = PS[:, bank, 0:2 * n].rearrange("p (m s) -> p m s", s=2)
                for st in range(2):
                    ins = dve.tensor_tensor(MOD[:, first:first + n, st], src[:, :, st], VEC[:, first:first + n], ALU.add)
                ins.then_inc(mod_kept, 1)
                dve.wait_ge(mod_kept, done)

            def scales(a, sc, gain):
                for st in range(2):
                    dve.scalar_tensor_tensor(a[:, st, :], MOD[:, sc:sc + KD, st], 1.0, VEC[:, gain:gain + KD],
                                             ALU.add, ALU.mult).then_inc(scales_ready, 1)

            dve.wait_ge(vec_ready, 1)
            wait_filled(dve, G_N1)
            dve.wait_ge(x_kept_dve, UNITS)
            dve.wait_ge(x_kept_act, UNITS)
            for k in range(KD):
                dve.tensor_tensor(XN[:, k, :], X[:, k, :], PS[:, 0:NCH, :].rearrange("p n c -> p (n c)")[:, 0:T],
                                  ALU.mult).then_inc(h_scaled, 1)
            dve.wait_ge(h_scaled, KD)
            dve.sem_inc(ps_free[G_N1 % 2], 1)
            dve.wait_ge(ada0_used, 1)
            add_bias(6, 0, 16, 1)
            scales(A1, SC1, V_NMIX)
            dve.wait_ge(scales_ready, 2)

            def split_lo(s, dyn=0):
                dve.wait_ge(w_hi, 2 * dyn + (s + 1))
                dve.tensor_tensor(WL[:, s % 2, :], RAW[:, s % 2, :], WH[:, s % 2, :].bitcast(F32), ALU.subtract)\
                    .then_inc(w_lo, 1)

            split_lo(0)

            def normed(tt, ss, hh, hl, n):
                def rest(k):
                    dve.wait_ge(h_hi, KD * n + k + 1)
                    dve.tensor_tensor(hl[:, k, :], tt[:, k % 2, :], hh[:, k, :].bitcast(F32), ALU.subtract)\
                        .then_inc(h_lo, 1)
                for k in range(KD):
                    if k >= 2:
                        dve.wait_ge(h_lo, KD * n + k - 1)
                    dve.tensor_tensor(tt[:, k % 2, :], X[:, k, :], ss[:], ALU.mult).then_inc(h_scaled, 1)
                    if k >= 1:
                        rest(k - 1)
                rest(KD - 1)

            for k in range(KD):
                dve.wait_ge(h_hi, k + 1)
                for st, t in ((0, slice(0, S)), (1, slice(S, T))):
                    ins = dve.tensor_scalar(XN[:, k, t], XN[:, k, t], A1[:, st, k:k + 1], MOD[:, SH1 + k, st:st + 1],
                                            ALU.mult, ALU.add)
                ins.then_inc(h_full, 1)
                dve.wait_ge(h_full, k + 1)
                dve.tensor_tensor(HL[:, k, :], XN[:, k, :], HH[:, k, :].bitcast(F32), ALU.subtract).then_inc(h_lo, 1)
            dve.wait_ge(h_lo, KD)

            def accumulate(n, dyn=0):
                dve.wait_ge(ada_loaded[n % 2], 8 * dyn + 16 * (n // 2 + 1))
                dve.wait_ge(ada_used, dyn + (n + 1))
                for k in range(KD):
                    for st in range(2):
                        w = ADA[:, n % 2, k, :]
                        if k == 0:
                            ins = dve.tensor_scalar(ACC[:, st, :], w, CS[:, k, st:st + 1], None, ALU.mult)
                        else:
                            dve.wait_ge(acc_step, 14 * dyn + (14 * n + 2 * k - 1 + st))
                            ins = dve.scalar_tensor_tensor(ACC[:, st, :], w, CS[:, k, st:st + 1], ACC[:, st, :],
                                                           ALU.mult, ALU.add)
                        ins.then_inc(acc_step if k < KD - 1 else acc_ready, 1)

            dve.memset(GG[:, 0:CW - 1], 0.0).then_inc(pads_set, 1)

            with dve.Fori(0, 2) as i:
                for n in range(6):
                    split_lo(n + 1, 3 * i)
                    accumulate(n, 6 * i)
                    if n % 3 < 2:
                        continue
                    jj = n // 3
                    j = 2 * i + jj
                    g = G_CONV + n
                    wait_kept(dve, g - 2, 3 * i)
                    wait_kept(dve, g - 1, 3 * i)
                    dve.wait_ge(y_full, j + 1)
                    dve.tensor_copy(GG[:, S + 2:S + 4],
                                    VEC[:, V_ST:V_END].rearrange("p (r j) -> p r j", r=CW - 1)[:, :, bass.ds(j, 1)]
                                    .rearrange("p r a -> p (r a)"))
                    dve.tensor_tensor(GG[:, 2:S + 2], CC[:, 0:S], UU[:, 0:S], ALU.mult)
                    dve.tensor_tensor(GG[:, S + 4:], CC[:, S:T], UU[:, S:T], ALU.mult).then_inc(gated, 1)
                    dve.wait_ge(gated, j + 1)
                    dve.tensor_copy(tile_of(ST, j)[:, 0:2], GG[:, S:S + 2])
                    dve.tensor_copy(tile_of(ST, j)[:, 2:4], GG[:, T + 2:T + 4]).then_inc(states_kept, 1)
                    taps = [VEC[:, bass.ds(V_CW + NJ * w + j, 1)] for w in range(CW)]
                    dve.tensor_scalar(UU[:], GG[:, 0:T + 2], taps[0], VEC[:, bass.ds(V_CB + j, 1)],
                                      ALU.mult, ALU.add).then_inc(conv_step, 1)
                    for w in (1, 2):
                        dve.wait_ge(conv_step, 3 * j + w)
                        dve.scalar_tensor_tensor(UU[:], GG[:, w:T + 2 + w], taps[w], UU[:], ALU.mult, ALU.add)\
                            .then_inc(conv_step, 1)
                    wait_kept(dve, g, 3 * i)
                    dve.wait_ge(conv_step, 3 * j + 3)
                    dve.tensor_tensor(CC[:, 0:S], BB[:, 0:S], UU[:, 0:S], ALU.mult)
                    dve.tensor_tensor(CC[:, S:T], BB[:, S:T], UU[:, S + 2:T + 2], ALU.mult).then_inc(y_full, 1)
                    dve.wait_ge(y_full, j + 2)
                    dve.tensor_copy(tile_of(YH, j), CC[:]).then_inc(y_hi, 1)
                    dve.wait_ge(y_hi, j + 1)
                    dve.tensor_tensor(tile_of(YL, j), CC[:], tile_of(YH, j).bitcast(F32), ALU.subtract)\
                        .then_inc(y_lo, 1)

            dve.wait_ge(ada_used, 13)
            add_bias(7, 16, 24, 2)
            scales(A2, SC2, V_FFN)

            def add_gated(g, gate, m, dyn_g=0):
                wait_filled(dve, g, dyn_g)
                for src, t, st in streams(g):
                    dst = X[:, m, t] if isinstance(m, int) else X[:, bass.ds(m, 1), t].rearrange("p a t -> p (a t)")
                    if t.start == 0:
                        dst = dst.rearrange("p (n c) -> p n c", n=2)
                    scalar = MOD[:, gate + m, st:st + 1] if isinstance(m, int) else \
                        MOD[:, bass.ds(m + gate, 1), st:st + 1].rearrange("p a s -> p (a s)")
                    ins = dve.scalar_tensor_tensor(dst, src, scalar, dst, ALU.mult, ALU.add)
                ins.then_inc(ps_free[g % 2], 1)

            with dve.Fori(0, 2) as i:
                for n in range(2):
                    split_lo(S_COUT + n + 1, i)
                    accumulate(n, 2 * i + 12)
                    for m in range(2):
                        add_gated(G_COUT + 2 * n + m, G1, 4 * i + (2 * n + m), 2 * i)
            dve.wait_ge(ada_used, 17)
            add_bias(6, 40, 8, 3)
            dve.memset(KR[0:64, :], 0.0).then_inc(zeroed, 1)
            dve.memset(SSQ[:], 0.0).then_inc(zeroed, 1)
            for n in range(KKV):
                split_lo(S_CKV + n + 1)
            split_lo(S_KR + 1)
            dve.wait_ge(squared, 2)
            dve.tensor_tensor(SSK[:], SSK[:], SQ2[:], ALU.add).then_inc(summed, 1)

            g = G_KR
            dve.wait_ge(tables_loaded, 32)
            dve.wait_ge(zeroed, 2)
            wait_filled(dve, g)
            lo, up = slice(0, HALF), slice(32, 32 + HALF)

            def key_part(rows, ap, t):
                v = ap[rows, t.start + (PAST if t.start == S else 0):t.stop + (PAST if t.start == S else 0)]
                return v.rearrange("p (n c) -> p n c", n=2) if t.start == 0 else v

            def token_part(rows, ap, t):
                v = ap[rows, t]
                return v.rearrange("p (n c) -> p n c", n=2) if t.start == 0 else v

            for dst, wide, rows, src_rows, table in (
                    (KR, True, lo, lo, COS), (TR, False, lo, up, SIN), (KR, True, up, lo, SIN), (TR, False, up, up, COS)):
                for src, t, st in streams(g):
                    out = key_part(rows, dst, t) if wide else token_part(rows, dst, t)
                    ins = dve.tensor_tensor(out, src[src_rows], token_part(src_rows, table, t), ALU.mult)
            ins.then_inc(ps_free[g % 2], 1)
            wait_kept(dve, g)
            for rows, op in ((lo, ALU.subtract), (up, ALU.add)):
                for t, off in ((slice(0, S), 0), (slice(S, T), PAST)):
                    k = KR[rows, t.start + off:t.stop + off]
                    dve.tensor_tensor(k, k, TR[rows, t], op).then_inc(k_rope_step, 1)

            variance(SSK, G_NKV, KVR)
            with dve.Fori(0, KQ // 2) as i:
                for n in range(2):
                    split_lo(S_CQ + n + 1, i)
                    dve.wait_ge(squared, 2 * i + (n + 3))
                    dve.wait_ge(summed, 2 * i + (n + 1))
                    dve.tensor_tensor(SSQ[:], SSQ[:], SQ2[:], ALU.add).then_inc(summed, 1)
            invert(SSK, 0)
            variance(SSQ, G_NQ, QR)
            for f in range(KKV):
                for t, off in ((slice(0, S), 0), (slice(S, T), PAST)):
                    dve.scalar_tensor_tensor(LAT[:, f, t.start + off:t.stop + off], CKV[:, f, t],
                                             VEC[:, V_KVG + f:V_KVG + f + 1], SSK[:, t], ALU.mult, ALU.mult)\
                        .then_inc(lat_ready, 1)
            invert(SSQ, 1)
            for k in range(KQ):
                dve.scalar_tensor_tensor(CQ[:, k, :], CQ[:, k, :], VEC[:, V_QG + k:V_QG + k + 1], SSQ[:],
                                         ALU.mult, ALU.mult).then_inc(q_ready, 1)
            g = G_X1
            for q in range(2):
                wait_filled(dve, g + q)
            for n, (t1, t2, op) in enumerate(((COS, SIN, ALU.subtract), (SIN, COS, ALU.add))):
                if n == 1:
                    dve.wait_ge(q_rope_step, 3)
                a = dve.tensor_tensor(in_chunks(QROT[:, n, :]), chunks(g), in_chunks(t1[:]), ALU.mult)
                b = dve.tensor_tensor(in_chunks(QF[:]), chunks(g + 1), in_chunks(t2[:]), ALU.mult)
                if n == 0:
                    a.then_inc(q_rope_step, 1)
                    b.then_inc(q_rope_step, 1)
                    dve.wait_ge(q_rope_step, 2)
                else:
                    a.then_inc(ps_free[g % 2], 1)
                    b.then_inc(ps_free[(g + 1) % 2], 1)
                    wait_kept(dve, g)
                    wait_kept(dve, g + 1)
                dve.tensor_tensor(QROT[:, n, :], QROT[:, n, :], QF[:], op).then_inc(q_rope_step, 1)
            dve.wait_ge(k_rope_step, 4)
            dve.wait_ge(past_kept, 3)
            dve.wait_ge(pool_zeroed, 4)
            for e, rows in ((0, (64, 96)), (1, (0, 32))):
                for q in range(2):
                    dve.tensor_copy(KT[e][rows[q]:rows[q] + HALF, :], KR[32 * q:32 * q + HALF, :])\
                        .then_inc(k_rope_copied, 1)

            with dve.Fori(0, NJ) as j:
                dve.wait_ge(k_full, j + 1)
                for e in range(2):
                    rows = slice(NOPE * e, NOPE * (e + 1))
                    dve.tensor_copy(KT[e][rows, :].rearrange("p (n c) -> p n c", n=4), PS[rows, 3:7, 0:TK // 4])\
                        .then_inc(k_kept, 1)
                dve.wait_ge(v_full, j + 2)
                for a, b, bank, r in ((0, 4, 7, P), (4, 8, 0, P), (8, 10, 1, P), (10, 11, 1, SD)):
                    col = 2 * P if a == 10 else 0
                    ins = dve.tensor_copy(V[0:r, a:b, :],
                                          PS[0:r, bank, col:col + (b - a) * P].rearrange("p (v d) -> p v d", d=P))
                ins.then_inc(v_kept, 1)

                def maxima(u):
                    e, q0, nq, k0, nk, tiles = unit_of(u)
                    U0 = PAIR_UNITS * j
                    dve.wait_ge(s_full, U0 + (u + 1))
                    src = PS[0:nq, 2 * (u % 2):2 * (u % 2) + 2, :].rearrange("p b k -> p (b k)")[:, 0:nk]
                    dve.reduce_max(MX[0:nq, u % 2:u % 2 + 1], src, AX_X).then_inc(max_ready, 1)
                    dve.wait_ge(max_ready, U0 + (u + 1))
                    dve.tensor_scalar(NM[0:nq, u % 2:u % 2 + 1], MX[0:nq, u % 2:u % 2 + 1], -SCALE, None, ALU.mult)\
                        .then_inc(nm_ready, 1)

                def divide(u):
                    e, q0, nq, k0, nk, tiles = unit_of(u)
                    U0 = PAIR_UNITS * j
                    dve.wait_ge(exp_done, U0 + (u + 2))
                    dve.reciprocal(RCP[0:nq, u % 2:u % 2 + 1], SUM[0:nq, u % 2:u % 2 + 1]).then_inc(rcp_ready, 1)
                    dve.wait_ge(rcp_ready, U0 + (u + 1))
                    dve.tensor_scalar(PP[0:nq, u % 2, 0:nk], PP[0:nq, u % 2, 0:nk], RCP[0:nq, u % 2:u % 2 + 1], None,
                                      ALU.mult).then_inc(p_ready, 1)

                def keep_output(u):
                    e, q0, nq, k0, nk, tiles = unit_of(u)
                    U0 = PAIR_UNITS * j
                    dve.wait_ge(o_full, U0 + (u + 1))
                    rows = slice(VH * e, VH * (e + 1))
                    src = PS[rows, 6 + u % 2, 0:nq]
                    hi = AOH[rows, bass.ds(j, 1), q0:q0 + nq].rearrange("p a t -> p (a t)")
                    lo = AOL[rows, bass.ds(j, 1), q0:q0 + nq].rearrange("p a t -> p (a t)")
                    dve.tensor_copy(hi, src).then_inc(o_hi, 1)
                    dve.wait_ge(o_hi, U0 + (u + 1))
                    dve.tensor_tensor(lo, src, hi.bitcast(F32), ALU.subtract).then_inc(o_kept, 1)

                for u in range(PAIR_UNITS):
                    maxima(u)
                    if u >= 1:
                        divide(u - 1)
                    if u >= 3:
                        keep_output(u - 3)
                divide(PAIR_UNITS - 1)
                keep_output(PAIR_UNITS - 3)
                keep_output(PAIR_UNITS - 2)
                keep_output(PAIR_UNITS - 1)

            dve.memset(SS3[:], 0.0).then_inc(zeroed, 1)
            dve.wait_ge(zeroed, 3)

            with dve.Fori(0, 2) as i:
                for n in range(2):
                    split_lo(S_AOUT + n + 1, i)
                    for m in range(2):
                        add_gated(G_AOUT + 2 * n + m, G1, 4 * i + (2 * n + m), 2 * i)
                        dve.wait_ge(squared, 4 * i + (2 * n + m + 9))
                        dve.wait_ge(summed, 4 * i + (2 * n + m + 7))
                        dve.tensor_tensor(SS3[:], SS3[:], SQ3[:, 0, :], ALU.add).then_inc(summed, 1)
            variance(SS3, G_N2, D)
            invert(SS3, 2)
            normed(TT3, SS3, H2H, H2L, 1)

            def gate_up(s, g, tile, a0, dyn_s=0, dyn_g=0, dyn_t=0):
                for n in range(4):
                    split_lo(s + n + 1, dyn_s)
                    if n % 2 == 1:
                        t = n // 2
                        count = dyn_t + (tile + t + 1)
                        wait_kept(dve, g + n - 1, dyn_g)
                        wait_filled(dve, g + n, dyn_g)
                        dve.tensor_tensor(in_chunks(SG[:, t, :]), chunks(g + n), in_chunks(SG[:, t, :]), ALU.mult)\
                            .then_inc(ps_free[(g + n) % 2], 1)
                        wait_kept(dve, g + n, dyn_g)
                        dve.tensor_copy(AH[:, a0 + t, :], SG[:, t, :]).then_inc(a_hi, 1)
                        dve.wait_ge(a_hi, count)
                        dve.tensor_tensor(AL[:, a0 + t, :], SG[:, t, :], AH[:, a0 + t, :].bitcast(F32), ALU.subtract)\
                            .then_inc(a_full, 1)

            def down(s, g, dyn_s=0, dyn_g=0):
                for n in range(2):
                    split_lo(s + n + 1, dyn_s)
                    for m in range(4):
                        add_gated(g + 4 * n + m, G2, 4 * n + m, dyn_g)

            gate_up(S_FFN, G_FFN, 0, 0)
            with dve.Fori(0, (NG - 1) // 2) as i:
                for n in range(2):
                    gate_up(S_LOOP + 6 * n, G_LOOP + 12 * n, 2 * (n + 1), 2 * (1 - n), 6 * i, 12 * i, 4 * i)
                    down(S_LOOP + 6 * n + 4, G_LOOP + 12 * n + 4, 6 * i, 12 * i)
            split_lo(S_LAST + 1)
            dve.memset(SS4[:], 0.0).then_inc(zeroed, 1)
            dve.wait_ge(zeroed, 4)
            for m in range(KD):
                add_gated(G_LAST + m, G2, m)
                if m >= 1:
                    add_square(SS4, SQ4[:, 0, :], 16 + m, 14 + m)
            add_square(SS4, SQ4[:, 0, :], 16 + KD, 14 + KD)
            variance(SS4, G_FIN, D)
            invert(SS4, 3)
            for k in range(KD):
                dve.scalar_tensor_tensor(X[:, k, :], X[:, k, :], VEC[:, V_FIN + k:V_FIN + k + 1], SS4[:],
                                         ALU.mult, ALU.mult).then_inc(y_ready, 1)
            for n in range(UNITS):
                r = P if n < KD else SD
                dve.wait_ge(y_turned, n + 1)
                if n >= 2:
                    dve.wait_ge(y_stored[n % 2], 16 * (n // 2))
                dve.tensor_copy(ORW[0:r, n % 2, 0:512], PS[0:r, 2 * (n % 2), :]).then_inc(y_kept_dve, 1)

        @block.gpsimd
        def _(pool):
            wait_filled(pool, G_CQ + KQ - 1)
            for e in range(2):
                pool.memset(QT[e][:], 0.0).then_inc(pool_zeroed, 1)
                pool.memset(KT[e][:], 0.0).then_inc(pool_zeroed, 1)
            pool.wait_ge(wq_loaded, 16)
            with pool.Fori(0, NJ) as j:
                pool.wait_ge(q_full, j + 1)
                for e in range(2):
                    h = 2 * j + e
                    ins = pool.tensor_copy(WQP[:, :, e, :], WQ[:, :, bass.ds(h * (NOPE + ROPE), NOPE)])
                ins.then_inc(wqp_ready, 1)
                pool.wait_ge(v_full, j + 1)
                pool.wait_ge(wkv_loaded, 16)
                for e in range(2):
                    h = 2 * j + e
                    pool.tensor_copy(WKP[:, :, e, :], WKV[:, :, bass.ds(h * (NOPE + VH), NOPE)])
                    ins = pool.tensor_copy(WVP[:, :, e, :], WKV[:, :, bass.ds(h * (NOPE + VH) + NOPE, VH)])
                ins.then_inc(wkvp_ready, 1)


_INS = ["x_prompt", "x_sample", "c_prompt", "c_sample", "cache_kv_latent", "cache_k_rope", "state_conv",
        "w_ada", "b_ada", "norm_mix_g", "w_in", "q_norm_g", "w_uq", "kv_norm_g", "w_ukv", "conv_w", "conv_b",
        "w_out", "norm_ffn_g", "w_gate", "w_up", "w_down", "final_norm_g"]
_OUTS = [(1, S, D), (1, SD, D), (1, 1, S, KVR), (1, 1, S, ROPE), (1, 1, CW - 1, DCONV),
         (1, 1, SD, KVR), (1, 1, SD, ROPE), (1, 1, CW - 1, DCONV)]


def constants():
    inv = np.float32(10000.0) ** (-np.arange(HALF, dtype=np.float32) / np.float32(HALF))
    pos = np.concatenate([np.arange(S), PAST + np.arange(SD)]).astype(np.float32)
    ang = (pos[:, None] * inv[None, :]).astype(np.float32)
    cos = np.tile(np.cos(ang).T, (HEADS, 1)).astype(np.float32)
    sin = np.tile(np.sin(ang).T, (HEADS, 1)).astype(np.float32)
    qmask = np.zeros((KD, T), np.float32)
    kmask = np.zeros((KD, TK), np.float32)
    for t in range(KD):
        qmask[t, t * P:t * P + CHUNK] = -BIG
        kmask[t, t * P + CHUNK:(t + 1) * P] = 1.0
    return {"c_ident": np.eye(P, dtype=np.float32), "c_cos": cos, "c_sin": sin, "c_qmask": qmask, "c_kmask": kmask}


def kernel(**inputs):
    import concourse.bacc as bacc
    from concourse.bass_utils import run_bass_kernel_spmd

    nc = bacc.Bacc("TRN2", target_bir_lowering=False, num_devices=1)
    arrays, args = {}, []
    named = [(n, np.ascontiguousarray(inputs[n])) for n in _INS] + list(constants().items())
    for name, a in named:
        arrays[f"in_{name}"] = a
        args.append(nc.dram_tensor(f"in_{name}", a.shape, mybir.dt.from_np(a.dtype), kind="ExternalInput").ap())
    for i, shape in enumerate(_OUTS):
        args.append(nc.dram_tensor(f"out_{i}", shape, F32, kind="ExternalOutput").ap())
    build(nc, *args)
    r = run_bass_kernel_spmd(nc, [arrays], core_ids=[0])
    return tuple(r.results[0][f"out_{i}"] for i in range(len(_OUTS)))
```

```python
from contextlib import ExitStack

import numpy as np

import concourse.bass as bass
from concourse import mybir

F32 = mybir.dt.float32
F32R = mybir.dt.float32r
ALU = mybir.AluOpType
ACT = mybir.ActivationFunctionType
AX_X = mybir.AxisListType.X

P = 128
D = 1024
KD = D // P
S = 1024
SD = 32
T = S + SD
NCH = 3
CH = T // NCH
PAST = 256
TK = S + PAST + SD
HEADS = 8
NOPE, ROPE, VH = 64, 32, 64
HALF = ROPE // 2
KVR, QR = 256, 768
KQ, KKV = QR // P, KVR // P
DCONV = 512
NJ = DCONV // P
CW = 3
DFF = 2816
NG = DFF // (2 * P)
CHUNK = 64
EPS = 1e-6
SCALE = float(NOPE + ROPE) ** -0.5
BIG = 1e30
ARENA = 207 * 1024

C_KV = QR
C_KR = C_KV + KVR
C_U = C_KR + ROPE
C_GB = C_U + DCONV
C_GC = C_GB + DCONV

V_BADA, V_NMIX, V_QG, V_KVG, V_CW, V_CB, V_FFN, V_FIN, V_C, V_ST, V_END = (
    0, 48, 56, 62, 64, 76, 80, 88, 96, 112, 120)
SH1, SC1, G1, SH2, SC2, G2 = (8 * n for n in range(6))

S_CONV = 0
S_COUT = S_CONV + 3 * NJ
S_CKV = S_COUT + 4
S_KR = S_CKV + KKV
S_CQ = S_KR + 1
S_AOUT = S_CQ + KQ
S_FFN = S_AOUT + 4
S_LOOP = S_FFN + 4
S_LAST = S_LOOP + 6 * (NG - 1)
S_END = S_LAST + 2
G_N1 = 0
G_CONV = 1
G_COUT = G_CONV + 3 * NJ
G_CKV = G_COUT + KD
G_KR = G_CKV + KKV
G_NKV = G_KR + 1
G_CQ = G_NKV + 1
G_XA = G_CQ + KQ
G_NQ = G_XA + 1
G_XB = G_NQ + 1
G_AOUT = G_XB + 1
G_N2 = G_AOUT + KD
G_FFN = G_N2 + 1
G_LOOP = G_FFN + 4
G_LAST = G_LOOP + 12 * (NG - 1)

UNITS = 9
PAIR_UNITS = 2 * UNITS


UNIT_ORDER = [it for n in range(UNITS) for it in ((0, (UNITS - 1 - n) % UNITS), (1, (n - 1) % UNITS))]


def unit_of(u):
    e, t = UNIT_ORDER[u]
    if t < UNITS - 1:
        return e, P * t, P, 0, P * (t + 1), [(v, P) for v in range(t + 1)]
    return e, S, SD, S, PAST + SD, [(8, P), (9, P), (10, SD)]


def build(nc, x_prompt, x_sample, c_prompt, c_sample, cache_kv_latent, cache_k_rope, state_conv,
          w_ada, b_ada, norm_mix_g, w_in, q_norm_g, w_uq, kv_norm_g, w_ukv, conv_w, conv_b, w_out,
          norm_ffn_g, w_gate, w_up, w_down, final_norm_g, c_ident, c_cos, c_sin, c_qmask, c_kmask,
          y_prompt, y_sample, lat_p, kr_p, cv_p, lat_s, kr_s, cv_s):
    ctx = ExitStack()
    with ctx:
        U = T * 4
        start = nc.sbuf_base
        ctx.enter_context(nc.sbuf_tensor("arena", [P, ARENA // 4], F32))

        def at(name, shape, dt, off):
            size = 4 * int(np.prod(shape[1:]))
            assert off % 32 == 0 and off + size <= ARENA, (name, off, size)
            return nc.alloc_sbuf_tensor_at(name, shape, dt, offset=ARENA0 + off)

        ARENA0 = -(-start // 32) * 32
        X = at("X", [P, KD, T], F32, 0)
        RAW = at("RAW", [P, 2, KD * P], F32, 8 * U)
        WH = at("WH", [P, 2, KD * P], F32R, 8 * U + 8192)
        WL = at("WL", [P, 2, KD * P], F32R, 8 * U + 16384)
        o = 8 * U + 24576
        COS = at("COS", [P, T], F32, o)
        SIN = at("SIN", [P, T], F32, o + U)
        PTS = at("PTS", [P, 2, KD * P], F32, o)
        IDENT = at("IDENT", [P, P], F32, o + 2 * U)
        ONES = at("ONES", [P, P], F32, o + 2 * U + 512)
        VEC = at("VEC", [P, P], F32, o + 2 * U + 1024)
        CS = at("CS", [P, KD, 2], F32, o + 2 * U + 1536)
        MOD = at("MOD", [P, 48, 2], F32, o + 2 * U + 1600)
        A1 = at("A1", [P, 2, KD], F32, o + 2 * U + 1984)
        A2 = at("A2", [P, 2, KD], F32, o + 2 * U + 2048)
        MX = at("MX", [P, 2], F32, o + 2 * U + 2112)
        NM = at("NM", [P, 2], F32, o + 2 * U + 2144)
        SUM = at("SUM", [P, 2], F32, o + 2 * U + 2176)
        RCP = at("RCP", [P, 2], F32, o + 2 * U + 2208)
        ST = at("ST", [P, NJ, 2 * (CW - 1)], F32, o + 2 * U + 2240)
        MS = at("MS", [P, UNITS + 7], F32, o + 2 * U + 2304)
        RT = at("RT", [P, UNITS + 7], F32, o + 2 * U + 2368)
        ZERO = RT[:, UNITS + 6:UNITS + 7]
        B = o + 2 * U + 2432
        HH = at("HH", [P, KD, T], F32R, B)
        HL = at("HL", [P, KD, T], F32R, B + 8 * U)
        YH = at("YH", [P, NJ, T], F32R, B + 16 * U)
        YL = at("YL", [P, NJ, T], F32R, B + 20 * U)
        ADA0 = at("ADA0", [P, KD, 16 * P], F32, B)
        XN = at("XN", [P, KD, T], F32, B + 16 * U)
        XJ = at("XJ", [P, D], F32, B + 16 * U)
        XR = at("XR", [P, 4, D], F32, B + 24 * U)
        VR = at("VR", [P, P], F32, B + 24 * U + 16384)
        UU = at("UU", [P, T + 2], F32, B + 24 * U)
        CC = at("CC", [P, T], F32, B + 24 * U + 4256)
        BB = at("BB", [P, T], F32, B + 25 * U + 4256)
        GG = at("GG", [P, T + 4], F32, B + 26 * U + 4256)
        ADA = at("ADA", [P, 2, KD, 2 * P], F32, B + 28 * U + 4256)
        ACC0 = at("ACC0", [P, 2, 2, 4 * P], F32, B + 24 * U)
        ACC = at("ACC", [P, 2, 2, 2 * P], F32, 8 * U + 24576)
        CQ = at("CQ", [P, KQ, T], F32, B + 16 * U)
        CKV = at("CKV", [P, KKV, T], F32, B + 22 * U)
        KR = at("KR", [P, TK], F32, B + 24 * U)
        o = B + 24 * U + 5248
        SQ2 = at("SQ2", [P, T], F32, o)
        SSK = at("SSK", [P, T], F32, o + U)
        SSQ = at("SSQ", [P, T], F32, o + 2 * U)
        TR = at("TR", [P, T], F32, o + 3 * U)
        WQ = at("WQ", [P, KQ, QR], F32, o + 4 * U)
        WKV = at("WKV", [P, KKV, HEADS * (NOPE + VH)], F32, B)
        LAT = at("LAT", [P, KKV, TK], F32, B + 2 * U)
        o = B + 2 * U + 10496
        KT = [at(f"KT{e}", [P, TK], F32, o + 5248 * e) for e in range(2)]
        QT = [at(f"QT{e}", [P, T], F32, o + 10496 + U * e) for e in range(2)]
        o = o + 10496 + 2 * U
        V = at("V", [P, 11, P], F32, o)
        WQP = at("WQP", [P, KQ, 2, NOPE], F32, o + 5632)
        WKP = at("WKP", [P, KKV, 2, NOPE], F32, o + 8704)
        WVP = at("WVP", [P, KKV, 2, VH], F32, o + 10752)
        o = o + 12800
        AOH = at("AOH", [P, NJ, T], F32R, o)
        assert o + 4 * U <= B + 16 * U
        QF = at("QF", [P, T], F32, o)
        PL = at("PL", [P, 2, KVR], F32, o + U)
        PK = at("PK", [P, 2, ROPE], F32, o + U + 2048)
        LO = at("LO", [P, 2, KVR], F32, o + U + 2304)
        KO = at("KO", [P, 2, ROPE], F32, o + U + 4352)
        WQR = at("WQR", [P, KQ, 2, HEADS, HALF], F32, o + U + 4608)
        QROT = at("QROT", [P, 2, T], F32, B + 22 * U)
        RSQ = at("RSQ", [P, T], F32, B + 28 * U + 1024)
        PP = at("PP", [P, 2, D], F32, B + 22 * U)
        AOL = at("AOL", [P, NJ, T], F32R, B + 24 * U)
        SQ3 = at("SQ3", [P, 2, T], F32, B)
        SS3 = at("SS3", [P, T], F32, B + 2 * U)
        TT3 = at("TT3", [P, 2, T], F32, B + 3 * U)
        H2H = at("H2H", [P, KD, T], F32R, B + 16 * U)
        H2L = at("H2L", [P, KD, T], F32R, B + 24 * U)
        AH = at("AH", [P, 4, T], F32R, B + 5 * U)
        AL = at("AL", [P, 4, T], F32R, B + 9 * U)
        SG = at("SG", [P, 2, T], F32, B + 13 * U)
        SQ4 = at("SQ4", [P, 2, T], F32, B + 16 * U)
        SS4 = at("SS4", [P, T], F32, B + 18 * U)
        ORW = at("ORW", [P, 4, D], F32, B + 19 * U)

        PS = ctx.enter_context(nc.psum_tensor("PS", [P, 8, 512], F32))
        rope_dram = nc.dram_tensor("q_rope_rows", [2, P, T], F32, kind="Internal").ap()

        def sem(name):
            return ctx.enter_context(nc.semaphore(name))

        vec_loaded = sem("vec_loaded")
        ident_loaded = sem("ident_loaded")
        tables_loaded = sem("tables_loaded")
        ones_set = sem("ones_set")
        vec_full = sem("vec_full")
        vec_ready = sem("vec_ready")
        x_turned = sem("x_turned")
        x_kept_dve = sem("x_kept_dve")
        x_kept_act = sem("x_kept_act")
        cond_ready = sem("cond_ready")
        square_summed = sem("square_summed")
        tok_var = sem("tok_var")
        tok_dev = sem("tok_dev")
        tok_rstd = sem("tok_rstd")
        totals_ready = sem("totals_ready")
        acc0_ready = sem("acc0_ready")
        ada0_used = sem("ada0_used")
        acc_step = sem("acc_step")
        acc_ready = sem("acc_ready")
        ada_used = sem("ada_used")
        mod_kept = sem("mod_kept")
        scales_ready = sem("scales_ready")
        w_hi = sem("w_hi")
        w_lo = sem("w_lo")
        kr_half_loaded = sem("kr_half_loaded")
        squared = sem("squared")
        summed = sem("summed")
        dev_ready = sem("dev_ready")
        rstd_ready = sem("rstd_ready")
        h_scaled = sem("h_scaled")
        h_full = sem("h_full")
        h_full_dve = sem("h_full_dve")
        h_full_act = sem("h_full_act")
        h_hi = sem("h_hi")
        h_lo = sem("h_lo")
        pads_set = sem("pads_set")
        gated = sem("gated")
        conv_step = sem("conv_step")
        y_full = sem("y_full")
        y_hi = sem("y_hi")
        y_lo = sem("y_lo")
        states_kept = sem("states_kept")
        k_rope_part = sem("k_rope_part")
        k_rope_step = sem("k_rope_step")
        lat_ready = sem("lat_ready")
        wq_loaded = sem("wq_loaded")
        wkv_loaded = sem("wkv_loaded")
        past_loaded = sem("past_loaded")
        past_turned = sem("past_turned")
        past_kept = sem("past_kept")
        zeroed = sem("zeroed")
        wq_scaled = sem("wq_scaled")
        wq_rotary = sem("wq_rotary")
        pool_zeroed = sem("pool_zeroed")
        mask_loaded = sem("mask_loaded")
        q_part = sem("q_part")
        q_rope_step = sem("q_rope_step")
        rope_stored = sem("rope_stored")
        k_rope_copied = sem("k_rope_copied")
        rows_turned = sem("rows_turned")
        rows_kept = [sem(f"rows_kept{n}") for n in range(2)]
        wqp_ready = sem("wqp_ready")
        wkvp_ready = sem("wkvp_ready")
        q_full = sem("q_full")
        k_full = sem("k_full")
        v_full = sem("v_full")
        q_kept = sem("q_kept")
        k_kept_dve = sem("k_kept_dve")
        k_kept_act = sem("k_kept_act")
        v_kept = sem("v_kept")
        rope_loaded = sem("rope_loaded")
        s_full = sem("s_full")
        max_ready = sem("max_ready")
        nm_ready = sem("nm_ready")
        exp_done = sem("exp_done")
        rcp_ready = sem("rcp_ready")
        p_ready = sem("p_ready")
        p_turned = sem("p_turned")
        pt_kept = sem("pt_kept")
        o_full = sem("o_full")
        o_hi = sem("o_hi")
        o_kept = sem("o_kept")
        a_full = sem("a_full")
        a_hi = sem("a_hi")
        y_ready = sem("y_ready")
        y_turned = sem("y_turned")
        y_kept_dve = sem("y_kept_dve")
        y_kept_act = sem("y_kept_act")
        states_stored = sem("states_stored")
        x_loaded = [sem(f"x_loaded{n}") for n in range(4)]
        ada0_loaded = [sem(f"ada0_loaded{n}") for n in range(4)]
        ada_loaded = [sem(f"ada_loaded{n}") for n in range(2)]
        raw_loaded = [sem(f"raw_loaded{n}") for n in range(2)]
        ps_full = [sem(f"ps_full{n}") for n in range(2)]
        ps_free = [sem(f"ps_free{n}") for n in range(2)]
        rows_stored = [sem(f"rows_stored{n}") for n in range(2)]
        y_stored = [sem(f"y_stored{n}") for n in range(4)]
        block = ctx.enter_context(nc.Block())

        win = w_in[0].rearrange("(k p) m -> p k m", p=P)
        wada = w_ada[0].rearrange("(k p) m -> p k m", p=P)
        wout = w_out[0].rearrange("(k p) m -> p k m", p=P)
        wg = w_gate[0].rearrange("(k p) m -> p k m", p=P)
        wu = w_up[0].rearrange("(k p) m -> p k m", p=P)
        wd = w_down[0].rearrange("(k p) m -> p k m", p=P)

        def raw(s, k=KD):
            return RAW[:, s % 2, :].rearrange("p (k m) -> p k m", k=k)

        def hi_lo(s, k=KD):
            return [w[:, s % 2, :].rearrange("p (k m) -> p k m", k=k) for w in (WH, WL)]

        def chunks(g, rows=slice(0, P)):
            b = NCH * (g % 2)
            return PS[rows, b:b + NCH, 0:CH]

        def in_chunks(ap):
            return ap.rearrange("p (n c) -> p n c", n=NCH)

        def streams(g):
            b = NCH * (g % 2)
            return [(PS[:, b:b + 2, 0:CH], slice(0, 2 * CH), 0), (PS[:, b + 2, 0:S - 2 * CH], slice(2 * CH, S), 0),
                    (PS[:, b + 2, S - 2 * CH:CH], slice(S, T), 1)]

        def tile_of(buf, k):
            return buf[:, k, :] if isinstance(k, int) else \
                buf[:, bass.ds(k, 1), :].rearrange("p a t -> p (a t)")

        def wait_filled(eng, g, dyn=0):
            eng.wait_ge(ps_full[g % 2], dyn + (g // 2 + 1))

        def wait_kept(eng, g, dyn=0):
            eng.wait_ge(ps_free[g % 2], dyn + (g // 2 + 2))

        def wait_loaded(eng, s, dyn=0):
            eng.wait_ge(raw_loaded[s % 2], 16 * dyn + 16 * (s // 2 + 1))

        @block.sync
        def _(sp):
            sp.dma_start(IDENT[:], c_ident).then_inc(ident_loaded, 16)

            for n in range(UNITS):
                if n >= 4:
                    sp.wait_ge(x_turned, n - 3)
                    sp.wait_ge(square_summed, n - 3)
                src = x_prompt[0, n * P:(n + 1) * P, :] if n < KD else x_sample[0]
                sp.dma_start(XR[0:P if n < KD else SD, n % 4], src).then_inc(x_loaded[n % 4], 16)
            for n in range(4):
                sp.dma_start(ADA0[:, :, n * 4 * P:(n + 1) * 4 * P], wada[:, :, n * 4 * P:(n + 1) * 4 * P])\
                    .then_inc(ada0_loaded[n], 16)

            def load_ada(n, col):
                sp.dma_start(ADA[:, n % 2], wada[:, :, bass.ds(col, 2 * P)]).then_inc(ada_loaded[n % 2], 16)

            def load_slot(s, src, k=KD, dyn=0):
                sp.wait_ge(w_lo, 2 * dyn + (s + 1))
                sp.dma_start(raw(s, k), src).then_inc(raw_loaded[s % 2], 16)

            with sp.Fori(0, 2) as i:
                for n in range(6):
                    j, q = divmod(n, 3)
                    load_slot(n, win[:, :, bass.ds((2 * i + j) * P + (C_U, C_GC, C_GB)[q], P)], dyn=3 * i)
                    sp.wait_ge(acc_ready, 12 * i + (2 * n + 2))
                    load_ada(n, (6 * i + (n + 8)) * (2 * P))
            with sp.Fori(0, 2) as i:
                for n in range(2):
                    load_slot(S_COUT + n, wout[:, NJ:KD, bass.ds((2 * i + n) * (2 * P), 2 * P)], k=NJ, dyn=i)
                    sp.wait_ge(acc_ready, 4 * i + (2 * n + 26))
                    load_ada(n, (2 * i + (n + 20)) * (2 * P))
            sp.wait_ge(states_kept, NJ)
            for dst, col in ((cv_p, 0), (cv_s, CW - 1)):
                for j in range(NJ):
                    sp.dma_start(dst[0, 0][:, j * P:(j + 1) * P].rearrange("r p -> p r"),
                                 ST[:, j, col:col + CW - 1],
                                 allow_slow_non_contiguous=True).then_inc(states_stored, 16)
            for n in range(KKV):
                load_slot(S_CKV + n, win[:, :, C_KV + n * P:C_KV + (n + 1) * P])
            sp.wait_ge(w_lo, S_KR + 1)
            for q, done in ((0, kr_half_loaded), (1, raw_loaded[S_KR % 2])):
                sp.dma_start(raw(S_KR)[:, :, 32 * q:32 * q + HALF],
                             win[:, :, C_KR + q * HALF:C_KR + (q + 1) * HALF]).then_inc(done, 16)
            sp.wait_ge(ada_used, 18)
            sp.dma_start(COS[:], c_cos).then_inc(tables_loaded, 16)
            sp.dma_start(SIN[:], c_sin).then_inc(tables_loaded, 16)
            for n in range(KQ):
                load_slot(S_CQ + n, win[:, :, n * P:(n + 1) * P])
                if n == 0:
                    sp.dma_start(WQ[:], w_uq[0].rearrange("(k p) m -> p k m", p=P)).then_inc(wq_loaded, 16)
            for n in range(2):
                load_slot(S_AOUT + n, wout[:, 0:NJ, n * 2 * P:(n + 1) * 2 * P], k=NJ)
            wait_filled(sp, G_CQ + KQ - 1)
            sp.dma_start(PL[:], cache_kv_latent[0, 0].rearrange("(n p) m -> p n m", p=P)).then_inc(past_loaded, 16)
            sp.dma_start(PK[:], cache_k_rope[0, 0].rearrange("(n p) m -> p n m", p=P)).then_inc(past_loaded, 16)
            sp.dma_start(WKV[:], w_ukv[0].rearrange("(k p) m -> p k m", p=P)).then_inc(wkv_loaded, 16)
            sp.wait_ge(pool_zeroed, 4)
            for e, row in ((0, 80), (1, 16)):
                sp.dma_start(QT[e][row:row + KD, :], c_qmask).then_inc(mask_loaded, 16)
                sp.dma_start(KT[e][row:row + KD, :], c_kmask).then_inc(mask_loaded, 16)
            sp.wait_ge(q_rope_step, 6)
            for q in range(2):
                sp.dma_start(rope_dram[q], QROT[:, q]).then_inc(rope_stored, 16)
            sp.wait_ge(rope_stored, 32)

            def load_rope(first_row):
                for e, rows in ((0, (64, 96)), (1, (0, 32))):
                    for q in range(2):
                        sp.dma_start(QT[e][rows[q]:rows[q] + HALF, :],
                                     rope_dram[q, bass.ds(first_row + HALF * e, HALF), :]).then_inc(rope_loaded, 16)

            load_rope(0)
            for n in range(UNITS):
                sp.wait_ge(rows_kept[n % 2], n // 2 + 1)
                r, dst, kdst = (slice(0, P), lat_p, kr_p) if n < KD else (slice(0, SD), lat_s, kr_s)
                t = slice(n * P, (n + 1) * P) if n < KD else slice(0, SD)
                sp.dma_start(dst[0, 0, t, :], LO[r, n % 2]).then_inc(rows_stored[n % 2], 16)
                sp.dma_start(kdst[0, 0, t, :], KO[r, n % 2]).then_inc(rows_stored[n % 2], 16)
            with sp.Fori(1, NJ) as j:
                sp.wait_ge(s_full, PAIR_UNITS * j)
                load_rope(2 * HALF * j)
            for n in range(2, 4):
                load_slot(S_AOUT + n, wout[:, 0:NJ, n * 2 * P:(n + 1) * 2 * P], k=NJ)

            def load_gate_up(s, tile, dyn=0):
                for n in range(4):
                    load_slot(s + n, (wg, wu)[n % 2][:, :, bass.ds(tile * P + (n // 2) * P, P)], dyn=dyn)

            def load_down(s, tile, dyn=0):
                for n in range(2):
                    load_slot(s + n, wd[:, bass.ds(tile, 2), n * 512:(n + 1) * 512], k=2, dyn=dyn)

            load_gate_up(S_FFN, 0)
            with sp.Fori(0, (NG - 1) // 2) as i:
                for n in range(2):
                    load_gate_up(S_LOOP + 6 * n, 4 * i + 2 * (n + 1), dyn=6 * i)
                    load_down(S_LOOP + 6 * n + 4, 4 * i + 2 * n, dyn=6 * i)
            load_down(S_LAST, 2 * (NG - 1))
            for n in range(UNITS):
                sp.wait_ge(y_kept_dve, n + 1)
                sp.wait_ge(y_kept_act, n + 1)
                dst = y_prompt[0, n * P:(n + 1) * P, :] if n < KD else y_sample[0]
                sp.dma_start(dst, ORW[0:P if n < KD else SD, n % 4]).then_inc(y_stored[n % 4], 16)
            sp.wait_ge(states_stored, 16 * 2 * NJ)
            for n in range(2):
                sp.wait_ge(rows_stored[n], 32 * (5 - n))
            for n in range(4):
                sp.wait_ge(y_stored[n], 16 * len(range(n, UNITS, 4)))

        @block.tensor
        def _(pe):
            pe.sem_inc(ada_used, 2)
            pe.sem_inc(q_full, 1)
            pe.sem_inc(v_full, 1)
            pe.wait_ge(ident_loaded, 16)
            for n in range(UNITS):
                r = P if n < KD else SD
                pe.wait_ge(x_loaded[n % 4], 16 * (n // 4 + 1))
                if n >= 2:
                    pe.wait_ge(x_kept_dve, n - 1)
                    pe.wait_ge(x_kept_act, n - 1)
                for k in range(KD):
                    mm = pe.transpose(PS[:, 2 * (n % 2) + k // 4, (k % 4) * P:(k % 4) * P + r],
                                      XR[0:r, n % 4, k * P:(k + 1) * P], IDENT[0:r, 0:r])
                mm.then_inc(x_turned, 1)
                if n == 3:
                    pe.wait_ge(vec_loaded, 16 * 11)
                    pe.transpose(PS[:, 7, 0:V_END], VR[0:V_END, :], IDENT[0:V_END, 0:V_END]).then_inc(vec_full, 1)

            def ada(n, bank, col, dyn=0):
                pe.wait_ge(acc_ready, 2 * dyn + (2 * n + 6))
                for m in range(2):
                    for st in range(2):
                        mm = pe.matmul(PS[:, bank, bass.ds(col + (2 * m + st), 1)],
                                       ACC[:, n % 2, st, m * P:(m + 1) * P], ONES[:, 0:1], start=True, stop=True)
                mm.then_inc(ada_used, 1)

            def begin_slot(s, dyn=0):
                pe.wait_ge(w_lo, 2 * dyn + (s + 3))

            def begin_group(g, dyn=0):
                pe.wait_ge(ps_free[g % 2], dyn + (g // 2 + 1))

            def step(g, weights, moving, k, first, last):
                b = NCH * (g % 2)
                for w, xs in ((weights[0][k], moving), (weights[1][k], moving[:1])):
                    for n in range(NCH):
                        for x in xs:
                            mm = pe.matmul(PS[:, b + n, 0:CH], w, x[k][:, n * CH:(n + 1) * CH],
                                           start=(first and w is weights[0][k] and x is xs[0]),
                                           stop=(last and w is weights[1][k]))
                if last:
                    mm.then_inc(ps_full[g % 2], 1)

            def product(g, weights, moving, ks, before=None):
                for k in ks:
                    if before:
                        before(k)
                    step(g, weights, moving, k, k == 0, k == ks[-1])

            def cut(pair, first=0):
                return [{k: buf[:, first + k, :] for k in range(buf.shape[1] - first)} for buf in pair]

            def weights_of(s, k=KD, m=0):
                return [{n: w[:, n, m * P:(m + 1) * P] for n in range(k)} for w in hi_lo(s, k)]

            def total(g, ss, tiles_summed):
                pe.wait_ge(summed, tiles_summed)
                begin_group(g)
                for n in range(NCH):
                    mm = pe.matmul(PS[:, NCH * (g % 2) + n, 0:CH], ONES[:], ss[:, n * CH:(n + 1) * CH],
                                   start=True, stop=True)
                mm.then_inc(ps_full[g % 2], 1)

            def token_totals(bank, col, ss, tiles_summed):
                pe.wait_ge(summed, tiles_summed)
                for n in range(UNITS):
                    r = P if n < KD else SD
                    mm = pe.matmul(PS[0:r, bank, col + n:col + n + 1], ss[:, n * P:n * P + r], ONES[:, 0:1],
                                   start=True, stop=True)
                mm.then_inc(totals_ready, 1)

            def spread(g, norm):
                pe.wait_ge(tok_rstd, norm)
                begin_group(g)
                for n in range(UNITS):
                    r = P if n < KD else SD
                    mm = pe.matmul(PS[:, NCH * (g % 2) + n // 4, (n % 4) * P:(n % 4) * P + r],
                                   RT[0:r, n:n + 1].broadcast_to([r, P]), IDENT[0:r, 0:r], start=True, stop=True)
                mm.then_inc(ps_full[g % 2], 1)

            pe.wait_ge(x_kept_dve, UNITS)
            pe.wait_ge(x_kept_act, UNITS)
            spread(G_N1, 1)
            pe.wait_ge(cond_ready, 1)
            for m in (0, 1, 2, 3, 8, 9, 10, 11):
                if m % 4 == 0:
                    pe.wait_ge(ada0_loaded[m // 4], 16)
                for k in range(KD):
                    pe.matmul(PS[:, 6, 2 * m:2 * m + 2], ADA0[:, k, m * P:(m + 1) * P], CS[:, k, :],
                              start=(k == 0), stop=(k == KD - 1))
            for c in range(2):
                pe.wait_ge(acc0_ready, 2 * c + 2)
                for m in range(4):
                    for st in range(2):
                        col = 2 * (4 * (2 * c + 1) + m) + st
                        mm = pe.matmul(PS[:, 6, col:col + 1], ACC0[:, c, st, m * P:(m + 1) * P], ONES[:, 0:1],
                                       start=True, stop=True)
            mm.then_inc(ada0_used, 1)
            h = cut((HH, HL))
            with pe.Fori(0, 2) as i:
                for n in range(6):
                    begin_slot(n, 3 * i)
                    begin_group(G_CONV + n, 3 * i)
                    product(G_CONV + n, weights_of(n), h, range(KD),
                            before=(lambda k: pe.wait_ge(h_lo, k + 1)) if n == 0 else None)
                    for a in ((), (n - 1, n), (n,))[n % 3]:
                        ada(a, 7, 24 * i + 4 * a, 6 * i)
            y = cut((YH, YL))
            with pe.Fori(0, 2) as i:
                for n in range(2):
                    begin_slot(S_COUT + n, i)
                    for m in range(2):
                        g = G_COUT + 2 * n + m
                        begin_group(g, 2 * i)
                        product(g, weights_of(S_COUT + n, NJ, m), y, range(NJ),
                                before=(lambda k: pe.wait_ge(y_lo, k + 2)) if n + m == 0 else None)
                    ada(n, 6, 8 * i + 4 * n, 2 * i + 12)
            for n in range(KKV + 1):
                begin_slot(S_CKV + n)
                begin_group(G_CKV + n)
                product(G_CKV + n, weights_of(S_CKV + n), h, range(KD))
            total(G_NKV, SSK, 1)
            with pe.Fori(0, KQ // 2) as i:
                for n in range(2):
                    begin_slot(S_CQ + n, i)
                    begin_group(G_CQ + n, i)
                    product(G_CQ + n, weights_of(S_CQ + n), h, range(KD))
            for q, g in enumerate((G_XA, G_XB)):
                pe.wait_ge(wq_rotary, q + 1)
                begin_group(g)
                for k in range(KQ):
                    if q == 0 and k == KQ - 1:
                        wait_kept(pe, G_CQ + k)
                    for n in range(NCH):
                        mm = pe.matmul(PS[:, NCH * (g % 2) + n, 0:CH],
                                       WQR[:, k, q].rearrange("p h c -> p (h c)"),
                                       CQ[:, k, n * CH:(n + 1) * CH], start=(k == 0), stop=(k == KQ - 1))
                mm.then_inc(ps_full[g % 2], 1)
                if q == 0:
                    total(G_NQ, SSQ, 7)
            def query_product(j):
                pe.wait_ge(wqp_ready, j + 1)
                pe.wait_ge(exp_done, PAIR_UNITS * j + 1)
                for k in range(KQ):
                    for n in range(NCH):
                        mm = pe.matmul(PS[:, n, 0:CH], WQP[:, k].rearrange("p e d -> p (e d)"),
                                       CQ[:, k, n * CH:(n + 1) * CH], start=(k == 0), stop=(k == KQ - 1))
                mm.then_inc(q_full, 1)

            begin_group(G_NQ + 2)
            query_product(0)
            pe.wait_ge(past_loaded, 32)
            for n in range(2):
                for f in range(KKV):
                    pe.transpose(PS[:, 6, (2 * f + n) * P:(2 * f + n + 1) * P], PL[:, n, f * P:(f + 1) * P], IDENT[:])
                for q in range(2):
                    mm = pe.transpose(PS[0:HALF, 7, (2 * q + n) * P:(2 * q + n + 1) * P],
                                      PK[:, n, q * HALF:(q + 1) * HALF], IDENT[:])
            mm.then_inc(past_turned, 1)

            pe.wait_ge(lat_ready, 4)
            pe.wait_ge(k_rope_step, 4)
            pe.wait_ge(past_kept, 3)
            for n in range(UNITS):
                r = P if n < KD else SD
                col = n * P if n < KD else S + PAST
                if n >= 2:
                    pe.wait_ge(rows_kept[n % 2], n // 2)
                for f in range(KKV):
                    pe.transpose(PS[0:r, 6 + n % 2, f * P:(f + 1) * P], LAT[:, f, col:col + r], IDENT[:])
                pe.transpose(PS[0:r, 6 + n % 2, KVR:KVR + 48], KR[0:48, col:col + r], IDENT[0:48, 0:48])\
                    .then_inc(rows_turned, 1)
            for n in range(2):
                pe.wait_ge(rows_kept[n], UNITS // 2 + 1 - n)
            pe.wait_ge(mask_loaded, 64)
            begin_group(G_XB + 2)

            def pair(j, more):
                pe.wait_ge(wkvp_ready, j + 1)
                pe.wait_ge(pt_kept, PAIR_UNITS * j + 1)

                def value_product(tiles):
                    for v in tiles:
                        r = P if v < 10 else SD
                        for k in range(KKV):
                            mm = pe.matmul(PS[0:r, 3 + v // 4, (v % 4) * P:(v % 4 + 1) * P],
                                           LAT[:, k, v * P:v * P + r], WVP[:, k].rearrange("p e d -> p (e d)"),
                                           start=(k == 0), stop=(k == 1))
                    return mm

                value_product(range(8)).then_inc(v_full, 1)
                pe.wait_ge(q_kept, 2 * j + 2)
                for n, c in enumerate(range(0, TK, 512)):
                    w = min(512, TK - c)
                    for k in range(KKV):
                        mm = pe.matmul(PS[:, n, 0:w], WKP[:, k].rearrange("p e d -> p (e d)"),
                                       LAT[:, k, c:c + w], start=(k == 0), stop=(k == 1))
                mm.then_inc(k_full, 1)
                value_product(range(8, 11)).then_inc(v_full, 1)
                pe.wait_ge(k_kept_dve, j + 1)
                pe.wait_ge(k_kept_act, j + 1)
                pe.wait_ge(rope_loaded, 64 * j + 64)

                def scores(u):
                    e, q0, nq, k0, nk, _ = unit_of(u)
                    if u == 1:
                        pe.wait_ge(v_kept, 2 * j + 1)
                    if u >= 2:
                        pe.wait_ge(exp_done, PAIR_UNITS * j + u)
                    for c in range(0, nk, 512):
                        w = min(512, nk - c)
                        mm = pe.matmul(PS[0:nq, 2 * (u % 2) + c // 512, 0:w], QT[e][:, q0:q0 + nq],
                                       KT[e][:, k0 + c:k0 + c + w], start=True, stop=True)
                    mm.then_inc(s_full, 1)

                def turn(u):
                    e, q0, nq, k0, nk, tiles = unit_of(u)
                    pe.wait_ge(p_ready, PAIR_UNITS * j + (u + 1))
                    if u == 0:
                        pe.wait_ge(v_kept, 2 * j + 2)
                    if u >= 1:
                        pe.wait_ge(pt_kept, PAIR_UNITS * j + (u + 1))
                    for b, (_, r) in enumerate(tiles):
                        mm = pe.transpose(PS[0:r, 4 + b // 4, (b % 4) * P:(b % 4 + 1) * P],
                                          PP[:, u % 2, b * P:b * P + r], IDENT[:])
                    mm.then_inc(p_turned, 1)

                def values(u):
                    e, q0, nq, k0, nk, tiles = unit_of(u)
                    pe.wait_ge(pt_kept, PAIR_UNITS * j + (u + 2))
                    pe.wait_ge(o_kept, PAIR_UNITS * j + max(u, 1))
                    for b, (v, r) in enumerate(tiles):
                        mm = pe.matmul(PS[:, 6 + u % 2, 0:nq], V[0:r, v, :], PTS[0:r, u % 2, b * P:b * P + nq],
                                       start=(b == 0), stop=(b == len(tiles) - 1))
                    mm.then_inc(o_full, 1)

                scores(0)
                for u in range(PAIR_UNITS):
                    if u + 1 < PAIR_UNITS:
                        scores(u + 1)
                    if u >= 1:
                        turn(u - 1)
                    if u >= 2:
                        values(u - 2)
                if more:
                    query_product(j + 1)
                turn(PAIR_UNITS - 1)
                values(PAIR_UNITS - 2)
                values(PAIR_UNITS - 1)

            with pe.Fori(0, NJ - 1) as j:
                pair(j, True)
            pair(NJ - 1, False)

            ao = cut((AOH, AOL))
            pe.wait_ge(o_kept, PAIR_UNITS * NJ + 1)
            with pe.Fori(0, 2) as i:
                for n in range(2):
                    begin_slot(S_AOUT + n, i)
                    for m in range(2):
                        g = G_AOUT + 2 * n + m
                        begin_group(g, 2 * i)
                        product(g, weights_of(S_AOUT + n, NJ, m), ao, range(NJ))
            token_totals(7, 0, SS3, 15)
            spread(G_N2, 2)
            h2 = cut((H2H, H2L))

            def gate_up(s, g, dyn_s=0, dyn_g=0, first=0):
                for n in range(first, 4):
                    begin_slot(s + n, dyn_s)
                    begin_group(g + n, dyn_g)
                    product(g + n, weights_of(s + n), h2, range(KD))

            def down(s, g, a0, tiles_ready, dyn_s=0, dyn_g=0):
                pe.wait_ge(a_full, tiles_ready)
                for n in range(2):
                    begin_slot(s + n, dyn_s)
                    for m in range(4):
                        begin_group(g + 4 * n + m, dyn_g)
                        product(g + 4 * n + m, weights_of(s + n, 2, m), cut((AH, AL), a0), range(2))

            for n in range(2):
                begin_slot(S_FFN + n)
            for k in range(KD):
                pe.wait_ge(h_lo, KD + k + 1)
                for n in range(2):
                    if k == 0:
                        begin_group(G_FFN + n)
                    step(G_FFN + n, weights_of(S_FFN + n), h2, k, k == 0, k == KD - 1)
            gate_up(S_FFN, G_FFN, first=2)
            with pe.Fori(0, (NG - 1) // 2) as i:
                for n in range(2):
                    gate_up(S_LOOP + 6 * n, G_LOOP + 12 * n, 6 * i, 12 * i)
                    down(S_LOOP + 6 * n + 4, G_LOOP + 12 * n + 4, 2 * n, 4 * i + (2 * n + 4), 6 * i, 12 * i)
            down(S_LAST, G_LAST, 0, 2 * NG + 2)
            for n in range(UNITS):
                r = P if n < KD else SD
                if n >= 3:
                    pe.wait_ge(y_kept_dve, n - 2)
                    pe.wait_ge(y_kept_act, n - 2)
                for k in range(KD):
                    if n == 0:
                        if k == 0:
                            begin_group(G_LAST + 8)
                            begin_group(G_LAST + 9)
                        pe.wait_ge(y_ready, k + 1)
                    mm = pe.transpose(PS[0:r, 2 * (n % 3) + k // 4, (k % 4) * P:(k % 4 + 1) * P],
                                      X[:, k, n * P:n * P + r], IDENT[:])
                mm.then_inc(y_turned, 1)
                if n == 0:
                    token_totals(7, 0, SS4, 23)

        @block.scalar
        def _(act):
            def split_hi(s, g, dyn=0, dyn_g=0):
                wait_loaded(act, s, dyn)
                wait_filled(act, g, dyn_g)
                act.activation(WH[:, s % 2, :], RAW[:, s % 2, :], ACT.Copy).then_inc(w_hi, 1)

            act.dma_start(VR[V_BADA:V_NMIX, :], b_ada[0].rearrange("(j p) -> j p", p=P)).then_inc(vec_loaded, 16)
            for row, src in ((V_NMIX, norm_mix_g[0]), (V_QG, q_norm_g[0]), (V_KVG, kv_norm_g[0]),
                             (V_CB, conv_b[0]), (V_FFN, norm_ffn_g[0]), (V_FIN, final_norm_g),
                             (V_C, c_prompt[0]), (V_C + KD, c_sample[0])):
                n = src.shape[0] // P
                act.dma_start(VR[row:row + n, :], src.rearrange("(j p) -> j p", p=P)).then_inc(vec_loaded, 16)
            act.dma_start(VR[V_CW:V_CB, :], conv_w[0].rearrange("w (j p) -> (w j) p", p=P)).then_inc(vec_loaded, 16)
            act.dma_start(VR[V_ST:V_END, :], state_conv[0, 0].rearrange("r (j p) -> (r j) p", p=P))\
                .then_inc(vec_loaded, 16)
            for n in range(UNITS):
                r = P if n < KD else SD
                act.wait_ge(x_loaded[n % 4], 16 * (n // 4 + 1))
                if n == 0:
                    act.wait_ge(ones_set, 1)
                else:
                    act.wait_ge(square_summed, n)
                act.activation(XJ[0:r, :], XR[0:r, n % 4], ACT.Square, accum_out=MS[0:r, n:n + 1])\
                    .then_inc(square_summed, 1)
                act.wait_ge(x_turned, n + 1)
                act.activation(X[:, 4:8, n * P:n * P + r],
                               PS[:, 2 * (n % 2) + 1, :].rearrange("p (k t) -> p k t", k=4)[:, :, 0:r], ACT.Copy)\
                    .then_inc(x_kept_act, 1)
            act.wait_ge(vec_ready, 1)
            act.activation(CS[:].rearrange("p k s -> p s k"),
                           VEC[:, V_C:V_C + 2 * KD].rearrange("p (s k) -> p s k", s=2), ACT.Silu)\
                .then_inc(cond_ready, 1)
            act.wait_ge(tok_var, 1)
            act.activation(MS[:, 0:UNITS], MS[:, 0:UNITS], ACT.Sqrt).then_inc(tok_dev, 1)
            wait_loaded(act, 0)
            act.activation(WH[:, 0, :], RAW[:, 0, :], ACT.Copy).then_inc(w_hi, 1)
            wait_loaded(act, 1)
            act.activation(WH[:, 1, :], RAW[:, 1, :], ACT.Copy).then_inc(w_hi, 1)

            act.wait_ge(scales_ready, 2)
            for k in range(KD):
                act.wait_ge(h_scaled, k + 1)
                for st, t in ((0, slice(0, S)), (1, slice(S, T))):
                    ins = act.activation(HH[:, k, t], XN[:, k, t], ACT.Identity,
                                         bias=MOD[:, SH1 + k, st:st + 1], scale=A1[:, st, k:k + 1])
                ins.then_inc(h_hi, 1)
                if k % 2 == 1:
                    act.wait_ge(h_hi, k + 1)
                    for st, t in ((0, slice(0, S)), (1, slice(S, T))):
                        ins = act.activation(XN[:, k, t], XN[:, k, t], ACT.Identity,
                                             bias=MOD[:, SH1 + k, st:st + 1], scale=A1[:, st, k:k + 1])
                    ins.then_inc(h_full_act, 1)

            def token_root(norm):
                act.wait_ge(tok_var, norm)
                act.activation(MS[:, 0:UNITS], MS[:, 0:UNITS], ACT.Sqrt).then_inc(tok_dev, 1)

            def root(ss, g):
                wait_kept(act, g)
                act.activation(ss[:], ss[:], ACT.Sqrt).then_inc(dev_ready, 1)

            def modulate(tt, hh, a, shift, n):
                for k in range(KD):
                    act.wait_ge(h_scaled, KD * n + k + 1)
                    for st, t in ((0, slice(0, S)), (1, slice(S, T))):
                        ins = act.activation(tt[:, k % 2, t], tt[:, k % 2, t], ACT.Identity,
                                             bias=MOD[:, shift + k, st:st + 1], scale=a[:, st, k:k + 1])
                    ins.then_inc(h_full, 1)
                    act.wait_ge(h_full, k + 1)
                    act.activation(hh[:, k, :], tt[:, k % 2, :], ACT.Copy).then_inc(h_hi, 1)

            def keep(g, dst, dyn=0):
                wait_filled(act, g, dyn)
                act.activation(in_chunks(dst), chunks(g), ACT.Copy).then_inc(ps_free[g % 2], 1)

            with act.Fori(0, 2) as i:
                for n in range(6):
                    j, q = divmod(n, 3)
                    act.wait_ge((y_full, y_lo, y_full)[q], 2 * i + (j + 1))
                    keep(G_CONV + n, (UU[:, 0:T], CC[:], BB[:])[q], 3 * i)
                    split_hi(n + 2, G_CONV + n, 3 * i, 3 * i)
            for n in range(1, 4):
                split_hi(S_COUT + n + 1, G_COUT + 2 * n - 1)
            for n in range(KKV):
                if n == 1:
                    act.wait_ge(kr_half_loaded, 16)
                split_hi(S_CKV + n + 1, G_CKV + n - 1)
                keep(G_CKV + n, CKV[:, n, :])
                wait_kept(act, G_CKV + n)
                act.activation((SSK, SQ2)[n][:], CKV[:, n, :], ACT.Square).then_inc(squared, 1)
            split_hi(S_KR + 1, G_KR - 1)
            wait_filled(act, G_KR)
            act.activation(in_chunks(CQ[0:64, KQ - 1, :]), chunks(G_KR, slice(0, 64)), ACT.Copy)\
                .then_inc(ps_free[G_KR % 2], 1)
            root(SSK, G_NKV)
            def rotary_columns(q):
                c = NOPE + q * HALF
                act.activation(WQR[:, :, q], WQ[:].rearrange("p k (h c) -> p k h c", h=HEADS)[:, :, :, c:c + HALF],
                               ACT.Copy).then_inc(wq_rotary, 1)

            for n in range(KQ):
                split_hi(S_CQ + n + 1, G_CQ + n - 1)
                if n == KQ - 1:
                    act.wait_ge(wq_scaled, KQ)
                    wait_filled(act, G_CQ + n)
                    rotary_columns(0)
                    act.wait_ge(k_rope_step, 4)
                keep(G_CQ + n, CQ[:, n, :])
                wait_kept(act, G_CQ + n)
                act.wait_ge(summed, n + 1)
                act.activation(SQ2[:], CQ[:, n, :], ACT.Square).then_inc(squared, 1)
            rotary_columns(1)
            root(SSQ, G_NQ)

            act.wait_ge(past_turned, 1)
            act.activation(LAT[:, :, S:S + PAST], PS[:, 6, :].rearrange("p (f t) -> p f t", f=KKV), ACT.Copy)\
                .then_inc(past_kept, 1)
            for q in range(2):
                act.activation(KR[32 * q:32 * q + HALF, S:S + PAST], PS[0:HALF, 7, q * PAST:(q + 1) * PAST], ACT.Copy)\
                    .then_inc(past_kept, 1)
            for n in range(0, UNITS, 2):
                r = slice(0, P if n < KD else SD)
                act.wait_ge(rows_turned, n + 1)
                if n >= 2:
                    act.wait_ge(rows_stored[0], 32 * (n // 2))
                act.activation(LO[r, 0, :], PS[r, 6, 0:KVR], ACT.Copy)
                act.activation(KO[r, 0, :].rearrange("p (q d) -> p q d", q=2),
                               PS[r, 6, KVR:KVR + 64].rearrange("p (q d) -> p q d", q=2)[:, :, 0:HALF],
                               ACT.Copy).then_inc(rows_kept[0], 1)

            with act.Fori(0, NJ) as j:
                act.wait_ge(v_full, 2 * j + 2)
                act.activation(V[:, 0:8, :], PS[:, 3:5, :].rearrange("p n (v d) -> p (n v) d", d=P), ACT.Copy)\
                    .then_inc(v_kept, 1)
                act.wait_ge(k_full, j + 1)
                act.activation(KT[1][NOPE:, :], PS[NOPE:, 0:3, :].rearrange("p n c -> p (n c)")[:, 0:TK], ACT.Copy)\
                    .then_inc(k_kept_act, 1)
                act.wait_ge(v_full, 2 * j + 3)
                act.activation(V[:, 8:10, :], PS[:, 5, 0:2 * P].rearrange("p (v d) -> p v d", d=P), ACT.Copy)
                act.activation(V[0:SD, 10, :], PS[0:SD, 5, 2 * P:3 * P], ACT.Copy).then_inc(v_kept, 1)

                def exponentials(u):
                    e, q0, nq, k0, nk, tiles = unit_of(u)
                    act.wait_ge(nm_ready, PAIR_UNITS * j + (u + 1))
                    if u >= 2:
                        act.wait_ge(p_turned, PAIR_UNITS * j + (u - 1))
                    src = PS[0:nq, 2 * (u % 2):2 * (u % 2) + 2, :].rearrange("p b k -> p (b k)")[:, 0:nk]
                    act.activation(PP[0:nq, u % 2, 0:nk], src, ACT.Exp, bias=NM[0:nq, u % 2:u % 2 + 1],
                                   scale=SCALE, accum_out=SUM[0:nq, u % 2:u % 2 + 1]).then_inc(exp_done, 1)

                def keep_turned(u):
                    e, q0, nq, k0, nk, tiles = unit_of(u)
                    act.wait_ge(p_turned, PAIR_UNITS * j + (u + 1))
                    if u >= 2:
                        act.wait_ge(o_full, PAIR_UNITS * j + (u - 1))
                    whole = [r for _, r in tiles].count(P)
                    src = PS[:, 4:6, :].rearrange("p b (k q) -> p (b k) q", q=P)
                    dst = PTS[:, u % 2, :].rearrange("p (k q) -> p k q", q=P)
                    ins = act.activation(dst[:, 0:whole, 0:nq], src[:, 0:whole, 0:nq], ACT.Copy)
                    if whole < len(tiles):
                        ins = act.activation(dst[0:SD, whole, 0:nq], src[0:SD, whole, 0:nq], ACT.Copy)
                    ins.then_inc(pt_kept, 1)

                for u in range(PAIR_UNITS):
                    if u >= 2:
                        keep_turned(u - 2)
                    exponentials(u)
                keep_turned(PAIR_UNITS - 2)
                keep_turned(PAIR_UNITS - 1)

            for m in range(KD):
                if m % 2 == 0:
                    split_hi(S_AOUT + m // 2 + 1, G_AOUT + m - 1)
                wait_kept(act, G_AOUT + m)
                act.wait_ge(summed, m + 7)
                act.activation(SQ3[:, 0, :], X[:, m, :], ACT.Square).then_inc(squared, 1)
            split_hi(S_FFN + 1, G_AOUT + KD - 1)
            token_root(2)
            act.wait_ge(scales_ready, 4)
            modulate(TT3, H2H, A2, SH2, 1)

            def gate_up(s, g, tile, dyn_s=0, dyn_g=0, dyn_t=0):
                for n in range(4):
                    if (s, n) != (S_FFN, 0):
                        split_hi(s + n + 1, g + n - 1, dyn_s, dyn_g)
                    if n % 2 == 0:
                        act.wait_ge(a_full, dyn_t + (tile + n // 2 + 1))
                        wait_filled(act, g + n, dyn_g)
                        act.activation(in_chunks(SG[:, n // 2, :]), chunks(g + n), ACT.Silu)\
                            .then_inc(ps_free[(g + n) % 2], 1)

            def down(s, g, dyn_s=0, dyn_g=0):
                for n in range(2):
                    split_hi(s + n + 1, g + 4 * n - 1, dyn_s, dyn_g)

            gate_up(S_FFN, G_FFN, 0)
            with act.Fori(0, (NG - 1) // 2) as i:
                for n in range(2):
                    gate_up(S_LOOP + 6 * n, G_LOOP + 12 * n, 2 * (n + 1), 6 * i, 12 * i, 4 * i)
                    down(S_LOOP + 6 * n + 4, G_LOOP + 12 * n + 4, 6 * i, 12 * i)
            split_hi(S_LAST + 1, G_LAST - 1)
            for m in range(KD):
                wait_kept(act, G_LAST + m)
                act.wait_ge(summed, 15 + m)
                act.activation(SQ4[:, 0, :], X[:, m, :], ACT.Square).then_inc(squared, 1)
                act.wait_ge(squared, 17 + m)
                act.activation(X[:, m, :], X[:, m, :], ACT.Identity, bias=ZERO, scale=VEC[:, V_FIN + m:V_FIN + m + 1])\
                    .then_inc(y_ready, 1)
            token_root(3)
            act.wait_ge(tok_rstd, 3)
            for n in range(UNITS):
                r = P if n < KD else SD
                act.wait_ge(y_turned, n + 1)
                if n >= 4:
                    act.wait_ge(y_stored[n % 4], 16 * (n // 4))
                act.activation(ORW[0:r, n % 4, 512:D], PS[0:r, 2 * (n % 3) + 1, :], ACT.Identity, bias=ZERO[0:r],
                               scale=RT[0:r, n:n + 1]).then_inc(y_kept_act, 1)

        @block.vector
        def _(dve):
            dve.sem_inc(w_lo, 2)
            dve.sem_inc(y_full, 1)
            dve.sem_inc(y_lo, 1)
            dve.sem_inc(a_full, 2)
            dve.sem_inc(o_kept, 1)
            dve.sem_inc(exp_done, 1)
            dve.sem_inc(pt_kept, 1)
            for n in range(2):
                dve.sem_inc(ps_free[n], 1)
            dve.sem_inc(acc_ready, 4)
            dve.memset(ONES[:], 1.0)
            dve.memset(ZERO, 0.0)
            dve.memset(MS[:], 1.0).then_inc(ones_set, 1)
            for n in range(UNITS):
                r = P if n < KD else SD
                dve.wait_ge(x_turned, n + 1)
                dve.tensor_copy(X[:, 0:4, n * P:n * P + r],
                                PS[:, 2 * (n % 2), :].rearrange("p (k t) -> p k t", k=4)[:, :, 0:r])\
                    .then_inc(x_kept_dve, 1)
                if n == 3:
                    dve.wait_ge(vec_full, 1)
                    dve.tensor_copy(VEC[:, 0:V_END], PS[:, 7, 0:V_END]).then_inc(vec_ready, 1)

            def add_square(ss, sq, sums, done=0):
                dve.wait_ge(squared, sums)
                dve.wait_ge(summed, done)
                dve.tensor_tensor(ss[:], ss[:], sq, ALU.add).then_inc(summed, 1)

            dve.wait_ge(square_summed, UNITS)
            dve.tensor_scalar(MS[:, 0:UNITS], MS[:, 0:UNITS], 1.0 / D, EPS, ALU.mult, ALU.add).then_inc(tok_var, 1)
            dve.wait_ge(tok_dev, 1)
            dve.reciprocal(RT[:, 0:UNITS], MS[:, 0:UNITS]).then_inc(tok_rstd, 1)

            def token_rstd(norm):
                dve.wait_ge(totals_ready, norm - 1)
                dve.tensor_scalar(MS[:, 0:KD], PS[:, 7, 0:KD], 1.0 / D, EPS, ALU.mult, ALU.add)
                dve.tensor_scalar(MS[0:SD, KD:UNITS], PS[0:SD, 7, KD:UNITS], 1.0 / D, EPS, ALU.mult, ALU.add)\
                    .then_inc(tok_var, 1)
                dve.wait_ge(tok_dev, norm)
                dve.reciprocal(RT[:, 0:UNITS], MS[:, 0:UNITS]).then_inc(tok_rstd, 1)

            def variance(ss, g, width):
                wait_filled(dve, g)
                dve.tensor_scalar(in_chunks(ss[:]), chunks(g), 1.0 / width, EPS, ALU.mult, ALU.add)\
                    .then_inc(ps_free[g % 2], 1)

            def invert(ss, n):
                dve.wait_ge(dev_ready, n + 1)
                dve.reciprocal(ss[:], ss[:]).then_inc(rstd_ready, 1)
                dve.wait_ge(rstd_ready, n + 1)

            def add_bias(bank, first, n, done):
                src = PS[:, bank, 0:2 * n].rearrange("p (m s) -> p m s", s=2)
                for st in range(2):
                    ins = dve.tensor_tensor(MOD[:, first:first + n, st], src[:, :, st], VEC[:, first:first + n], ALU.add)
                ins.then_inc(mod_kept, 1)
                dve.wait_ge(mod_kept, done)

            def scales(a, sc, gain):
                for st in range(2):
                    dve.scalar_tensor_tensor(a[:, st, :], MOD[:, sc:sc + KD, st], 1.0, VEC[:, gain:gain + KD],
                                             ALU.add, ALU.mult).then_inc(scales_ready, 1)

            dve.wait_ge(vec_ready, 1)
            def weighted_sum(dst, src, steps, ready):
                for k in range(KD):
                    for st in range(2):
                        if k == 0:
                            ins = dve.tensor_scalar(dst[:, st, :], src[:, k, :], CS[:, k, st:st + 1], None, ALU.mult)
                        else:
                            dve.wait_ge(acc_step, steps + (2 * k - 1 + st))
                            ins = dve.scalar_tensor_tensor(dst[:, st, :], src[:, k, :], CS[:, k, st:st + 1],
                                                           dst[:, st, :], ALU.mult, ALU.add)
                        ins.then_inc(acc_step if k < KD - 1 else ready, 1)

            def accumulate_first(c):
                dve.wait_ge(ada0_loaded[2 * c + 1], 16)
                weighted_sum(ACC0[:, c], ADA0[:, :, (2 * c + 1) * 4 * P:(2 * c + 2) * 4 * P], 14 * c, acc0_ready)

            wait_filled(dve, G_N1)
            dve.wait_ge(x_kept_dve, UNITS)
            dve.wait_ge(x_kept_act, UNITS)
            for k in range(KD):
                dve.tensor_tensor(XN[:, k, :], X[:, k, :], PS[:, 0:NCH, :].rearrange("p n c -> p (n c)")[:, 0:T],
                                  ALU.mult).then_inc(h_scaled, 1)
            dve.wait_ge(h_scaled, KD)
            dve.sem_inc(ps_free[G_N1 % 2], 1)
            dve.wait_ge(cond_ready, 1)
            accumulate_first(0)
            accumulate_first(1)
            dve.wait_ge(ada0_used, 1)
            add_bias(6, 0, 16, 1)
            scales(A1, SC1, V_NMIX)
            dve.wait_ge(scales_ready, 2)

            def split_lo(s, dyn=0):
                dve.wait_ge(w_hi, 2 * dyn + (s + 1))
                dve.tensor_tensor(WL[:, s % 2, :], RAW[:, s % 2, :], WH[:, s % 2, :].bitcast(F32), ALU.subtract)\
                    .then_inc(w_lo, 1)

            split_lo(0)
            split_lo(1)

            def normed(tt, ss, hh, hl, n):
                def rest(k):
                    dve.wait_ge(h_hi, KD * n + k + 1)
                    dve.tensor_tensor(hl[:, k, :], tt[:, k % 2, :], hh[:, k, :].bitcast(F32), ALU.subtract)\
                        .then_inc(h_lo, 1)
                for k in range(KD):
                    if k >= 2:
                        dve.wait_ge(h_lo, KD * n + k - 1)
                    dve.tensor_tensor(tt[:, k % 2, :], X[:, k, :], ss[:], ALU.mult).then_inc(h_scaled, 1)
                    if k >= 1:
                        rest(k - 1)
                rest(KD - 1)

            for k in range(KD):
                if k % 2 == 0:
                    dve.wait_ge(h_hi, k + 1)
                    for st, t in ((0, slice(0, S)), (1, slice(S, T))):
                        ins = dve.tensor_scalar(XN[:, k, t], XN[:, k, t], A1[:, st, k:k + 1],
                                                MOD[:, SH1 + k, st:st + 1], ALU.mult, ALU.add)
                    ins.then_inc(h_full_dve, 1)
                    dve.wait_ge(h_full_dve, k // 2 + 1)
                else:
                    dve.wait_ge(h_full_act, k // 2 + 1)
                dve.tensor_tensor(HL[:, k, :], XN[:, k, :], HH[:, k, :].bitcast(F32), ALU.subtract).then_inc(h_lo, 1)
            dve.wait_ge(h_lo, KD)

            def accumulate(n, dyn=0):
                dve.wait_ge(ada_loaded[n % 2], 8 * dyn + 16 * (n // 2 + 1))
                dve.wait_ge(ada_used, dyn + (n + 1))
                weighted_sum(ACC[:, n % 2], ADA[:, n % 2], 14 * dyn + (14 * n + 28), acc_ready)

            dve.memset(GG[:, 0:CW - 1], 0.0).then_inc(pads_set, 1)

            with dve.Fori(0, 2) as i:
                for n in range(6):
                    accumulate(n, 6 * i)
                    if n % 3 < 2:
                        split_lo(n + 2, 3 * i)
                        continue
                    jj = n // 3
                    j = 2 * i + jj
                    g = G_CONV + n
                    wait_kept(dve, g - 2, 3 * i)
                    wait_kept(dve, g - 1, 3 * i)
                    dve.wait_ge(y_full, j + 1)
                    dve.tensor_copy(GG[:, S + 2:S + 4],
                                    VEC[:, V_ST:V_END].rearrange("p (r j) -> p r j", r=CW - 1)[:, :, bass.ds(j, 1)]
                                    .rearrange("p r a -> p (r a)"))
                    dve.tensor_tensor(GG[:, 2:S + 2], CC[:, 0:S], UU[:, 0:S], ALU.mult)
                    dve.tensor_tensor(GG[:, S + 4:], CC[:, S:T], UU[:, S:T], ALU.mult).then_inc(gated, 1)
                    dve.wait_ge(gated, j + 1)
                    dve.tensor_copy(tile_of(ST, j)[:, 0:2], GG[:, S:S + 2])
                    dve.tensor_copy(tile_of(ST, j)[:, 2:4], GG[:, T + 2:T + 4]).then_inc(states_kept, 1)
                    taps = [VEC[:, bass.ds(V_CW + NJ * w + j, 1)] for w in range(CW)]
                    dve.tensor_scalar(UU[:], GG[:, 0:T + 2], taps[0], VEC[:, bass.ds(V_CB + j, 1)],
                                      ALU.mult, ALU.add).then_inc(conv_step, 1)
                    for w in (1, 2):
                        dve.wait_ge(conv_step, 3 * j + w)
                        dve.scalar_tensor_tensor(UU[:], GG[:, w:T + 2 + w], taps[w], UU[:], ALU.mult, ALU.add)\
                            .then_inc(conv_step, 1)
                    split_lo(n + 2, 3 * i)
                    wait_kept(dve, g, 3 * i)
                    dve.wait_ge(conv_step, 3 * j + 3)
                    dve.tensor_tensor(CC[:, 0:S], BB[:, 0:S], UU[:, 0:S], ALU.mult)
                    dve.tensor_tensor(CC[:, S:T], BB[:, S:T], UU[:, S + 2:T + 2], ALU.mult).then_inc(y_full, 1)
                    dve.wait_ge(y_full, j + 2)
                    dve.tensor_copy(tile_of(YH, j), CC[:]).then_inc(y_hi, 1)
                    dve.wait_ge(y_hi, j + 1)
                    dve.tensor_tensor(tile_of(YL, j), CC[:], tile_of(YH, j).bitcast(F32), ALU.subtract)\
                        .then_inc(y_lo, 1)

            dve.wait_ge(ada_used, 14)
            add_bias(7, 16, 24, 2)
            scales(A2, SC2, V_FFN)

            def add_gated(g, gate, m, dyn_g=0):
                wait_filled(dve, g, dyn_g)
                for src, t, st in streams(g):
                    dst = X[:, m, t] if isinstance(m, int) else X[:, bass.ds(m, 1), t].rearrange("p a t -> p (a t)")
                    if t.start == 0:
                        dst = dst.rearrange("p (n c) -> p n c", n=2)
                    scalar = MOD[:, gate + m, st:st + 1] if isinstance(m, int) else \
                        MOD[:, bass.ds(m + gate, 1), st:st + 1].rearrange("p a s -> p (a s)")
                    ins = dve.scalar_tensor_tensor(dst, src, scalar, dst, ALU.mult, ALU.add)
                ins.then_inc(ps_free[g % 2], 1)

            for n in range(4):
                if n >= 1:
                    split_lo(S_COUT + n + 1)
                accumulate(n, 12)
                for m in range(2):
                    add_gated(G_COUT + 2 * n + m, G1, 2 * n + m)
            dve.wait_ge(ada_used, 18)
            add_bias(6, 40, 8, 3)
            dve.memset(KR[0:64, :], 0.0).then_inc(zeroed, 1)
            dve.memset(SSQ[:], 0.0).then_inc(zeroed, 1)
            for n in range(KKV):
                split_lo(S_CKV + n + 1)
            split_lo(S_KR + 1)
            dve.wait_ge(squared, 2)
            dve.tensor_tensor(SSK[:], SSK[:], SQ2[:], ALU.add).then_inc(summed, 1)

            g = G_KR
            dve.wait_ge(tables_loaded, 32)
            dve.wait_ge(zeroed, 2)
            wait_kept(dve, g)
            lo, up = slice(0, HALF), slice(32, 32 + HALF)
            parts = ((slice(0, S), 0), (slice(S, T), PAST))
            for dst, wide, rows, src_rows, table in (
                    (KR, 1, lo, lo, COS), (TR, 0, lo, up, SIN), (KR, 1, up, lo, SIN), (TR, 0, up, up, COS)):
                for t, off in parts:
                    ins = dve.tensor_tensor(dst[rows, t.start + off * wide:t.stop + off * wide],
                                            CQ[src_rows, KQ - 1, t], table[src_rows, t], ALU.mult)
            ins.then_inc(k_rope_part, 1)
            dve.wait_ge(k_rope_part, 1)
            for rows, op in ((lo, ALU.subtract), (up, ALU.add)):
                for t, off in parts:
                    k = KR[rows, t.start + off:t.stop + off]
                    dve.tensor_tensor(k, k, TR[rows, t], op).then_inc(k_rope_step, 1)

            variance(SSK, G_NKV, KVR)
            with dve.Fori(0, KQ // 2) as i:
                for n in range(2):
                    split_lo(S_CQ + n + 1, i)
                    dve.wait_ge(wq_loaded, 16)
                    dve.tensor_scalar(tile_of(WQ, 2 * i + n), tile_of(WQ, 2 * i + n),
                                      VEC[:, bass.ds(2 * i + (V_QG + n), 1)], None, ALU.mult).then_inc(wq_scaled, 1)
                    dve.wait_ge(squared, 2 * i + (n + 3))
                    dve.wait_ge(summed, 2 * i + (n + 1))
                    dve.tensor_tensor(SSQ[:], SSQ[:], SQ2[:], ALU.add).then_inc(summed, 1)
            invert(SSK, 0)
            wait_filled(dve, G_CQ + KQ - 1)
            for f in range(KKV):
                for t, off in ((slice(0, S), 0), (slice(S, T), PAST)):
                    dve.scalar_tensor_tensor(LAT[:, f, t.start + off:t.stop + off], CKV[:, f, t],
                                             VEC[:, V_KVG + f:V_KVG + f + 1], SSK[:, t], ALU.mult, ALU.mult)\
                        .then_inc(lat_ready, 1)
            dve.wait_ge(lat_ready, 4)
            wait_filled(dve, G_XA)
            dve.tensor_tensor(in_chunks(QROT[:, 0, :]), chunks(G_XA), in_chunks(COS[:]), ALU.mult)
            dve.tensor_tensor(in_chunks(QROT[:, 1, :]), chunks(G_XA), in_chunks(SIN[:]), ALU.mult)\
                .then_inc(ps_free[G_XA % 2], 1)
            variance(SSQ, G_NQ, QR)
            dve.wait_ge(dev_ready, 2)
            dve.reciprocal(RSQ[:], SSQ[:]).then_inc(rstd_ready, 1)
            dve.wait_ge(rstd_ready, 2)
            wait_kept(dve, G_XA)
            for buf in (QROT[:, 0, :], QROT[:, 1, :], SIN[:], COS[:]):
                dve.tensor_tensor(buf, buf, RSQ[:], ALU.mult).then_inc(q_rope_step, 1)
            wait_filled(dve, G_XB)
            dve.wait_ge(q_rope_step, 4)
            ins = dve.tensor_tensor(in_chunks(QF[:]), chunks(G_XB), in_chunks(SIN[:]), ALU.mult)
            ins.then_inc(q_part, 1)
            dve.wait_ge(q_part, 1)
            dve.tensor_tensor(QROT[:, 0, :], QROT[:, 0, :], QF[:], ALU.subtract).then_inc(q_rope_step, 1)
            dve.wait_ge(q_rope_step, 5)
            dve.tensor_tensor(in_chunks(QF[:]), chunks(G_XB), in_chunks(COS[:]), ALU.mult)\
                .then_inc(ps_free[G_XB % 2], 1)
            wait_kept(dve, G_XB)
            dve.tensor_tensor(QROT[:, 1, :], QROT[:, 1, :], QF[:], ALU.add).then_inc(q_rope_step, 1)
            dve.wait_ge(k_rope_step, 4)
            dve.wait_ge(past_kept, 3)
            dve.wait_ge(pool_zeroed, 4)
            for e, rows in ((0, (64, 96)), (1, (0, 32))):
                for q in range(2):
                    dve.tensor_copy(KT[e][rows[q]:rows[q] + HALF, :], KR[32 * q:32 * q + HALF, :])\
                        .then_inc(k_rope_copied, 1)

            for n in range(1, UNITS, 2):
                dve.wait_ge(rows_turned, n + 1)
                if n >= 2:
                    dve.wait_ge(rows_stored[1], 32 * (n // 2))
                dve.tensor_copy(LO[:, 1, :], PS[:, 7, 0:KVR])
                dve.tensor_copy(KO[:, 1, :].rearrange("p (q d) -> p q d", q=2),
                                PS[:, 7, KVR:KVR + 64].rearrange("p (q d) -> p q d", q=2)[:, :, 0:HALF])\
                    .then_inc(rows_kept[1], 1)

            with dve.Fori(0, NJ) as j:
                dve.wait_ge(q_full, j + 2)
                for e in range(2):
                    rows = slice(NOPE * e, NOPE * (e + 1))
                    dve.tensor_tensor(in_chunks(QT[e][rows, :]), PS[rows, 0:NCH, 0:CH], in_chunks(RSQ[rows, :]), ALU.mult)\
                        .then_inc(q_kept, 1)
                dve.wait_ge(k_full, j + 1)
                dve.tensor_copy(KT[0][0:NOPE, :], PS[0:NOPE, 0:3, :].rearrange("p n c -> p (n c)")[:, 0:TK])\
                    .then_inc(k_kept_dve, 1)

                def maxima(u):
                    e, q0, nq, k0, nk, tiles = unit_of(u)
                    U0 = PAIR_UNITS * j
                    dve.wait_ge(s_full, U0 + (u + 1))
                    src = PS[0:nq, 2 * (u % 2):2 * (u % 2) + 2, :].rearrange("p b k -> p (b k)")[:, 0:nk]
                    dve.reduce_max(MX[0:nq, u % 2:u % 2 + 1], src, AX_X).then_inc(max_ready, 1)
                    dve.wait_ge(max_ready, U0 + (u + 1))
                    dve.tensor_scalar(NM[0:nq, u % 2:u % 2 + 1], MX[0:nq, u % 2:u % 2 + 1], -SCALE, None, ALU.mult)\
                        .then_inc(nm_ready, 1)

                def divide(u):
                    e, q0, nq, k0, nk, tiles = unit_of(u)
                    U0 = PAIR_UNITS * j
                    dve.wait_ge(exp_done, U0 + (u + 2))
                    dve.reciprocal(RCP[0:nq, u % 2:u % 2 + 1], SUM[0:nq, u % 2:u % 2 + 1]).then_inc(rcp_ready, 1)
                    dve.wait_ge(rcp_ready, U0 + (u + 1))
                    dve.tensor_scalar(PP[0:nq, u % 2, 0:nk], PP[0:nq, u % 2, 0:nk], RCP[0:nq, u % 2:u % 2 + 1], None,
                                      ALU.mult).then_inc(p_ready, 1)

                def keep_output(u):
                    e, q0, nq, k0, nk, tiles = unit_of(u)
                    U0 = PAIR_UNITS * j
                    dve.wait_ge(o_full, U0 + (u + 1))
                    rows = slice(VH * e, VH * (e + 1))
                    src = PS[rows, 6 + u % 2, 0:nq]
                    hi = AOH[rows, bass.ds(j, 1), q0:q0 + nq].rearrange("p a t -> p (a t)")
                    lo = AOL[rows, bass.ds(j, 1), q0:q0 + nq].rearrange("p a t -> p (a t)")
                    dve.tensor_copy(hi, src).then_inc(o_hi, 1)
                    dve.wait_ge(o_hi, U0 + (u + 1))
                    dve.tensor_tensor(lo, src, hi.bitcast(F32), ALU.subtract).then_inc(o_kept, 1)

                for u in range(PAIR_UNITS):
                    maxima(u)
                    if u >= 1:
                        divide(u - 1)
                    if u >= 3:
                        keep_output(u - 3)
                divide(PAIR_UNITS - 1)
                keep_output(PAIR_UNITS - 3)
                keep_output(PAIR_UNITS - 2)
                keep_output(PAIR_UNITS - 1)

            dve.memset(SS3[:], 0.0).then_inc(zeroed, 1)
            dve.wait_ge(zeroed, 3)

            with dve.Fori(0, 2) as i:
                for n in range(2):
                    split_lo(S_AOUT + n + 1, i)
                    for m in range(2):
                        add_gated(G_AOUT + 2 * n + m, G1, 4 * i + (2 * n + m), 2 * i)
                        dve.wait_ge(squared, 4 * i + (2 * n + m + 9))
                        dve.wait_ge(summed, 4 * i + (2 * n + m + 7))
                        dve.tensor_tensor(SS3[:], SS3[:], SQ3[:, 0, :], ALU.add).then_inc(summed, 1)
            split_lo(S_FFN + 1)
            token_rstd(2)
            wait_filled(dve, G_N2)
            b = NCH * (G_N2 % 2)
            dve.tensor_copy(SS3[:], PS[:, b:b + NCH, :].rearrange("p n c -> p (n c)")[:, 0:T])\
                .then_inc(ps_free[G_N2 % 2], 1)
            wait_kept(dve, G_N2)
            normed(TT3, SS3, H2H, H2L, 1)

            def gate_up(s, g, tile, a0, dyn_s=0, dyn_g=0, dyn_t=0):
                for n in range(4):
                    if (s, n) != (S_FFN, 0):
                        split_lo(s + n + 1, dyn_s)
                    if n % 2 == 1:
                        t = n // 2
                        count = dyn_t + (tile + t + 1)
                        wait_kept(dve, g + n - 1, dyn_g)
                        wait_filled(dve, g + n, dyn_g)
                        dve.tensor_tensor(in_chunks(SG[:, t, :]), chunks(g + n), in_chunks(SG[:, t, :]), ALU.mult)\
                            .then_inc(ps_free[(g + n) % 2], 1)
                        wait_kept(dve, g + n, dyn_g)
                        dve.tensor_copy(AH[:, a0 + t, :], SG[:, t, :]).then_inc(a_hi, 1)
                        dve.wait_ge(a_hi, count)
                        dve.tensor_tensor(AL[:, a0 + t, :], SG[:, t, :], AH[:, a0 + t, :].bitcast(F32), ALU.subtract)\
                            .then_inc(a_full, 1)

            def down(s, g, dyn_s=0, dyn_g=0):
                for n in range(2):
                    split_lo(s + n + 1, dyn_s)
                    for m in range(4):
                        add_gated(g + 4 * n + m, G2, 4 * n + m, dyn_g)

            gate_up(S_FFN, G_FFN, 0, 0)
            with dve.Fori(0, (NG - 1) // 2) as i:
                for n in range(2):
                    gate_up(S_LOOP + 6 * n, G_LOOP + 12 * n, 2 * (n + 1), 2 * (1 - n), 6 * i, 12 * i, 4 * i)
                    down(S_LOOP + 6 * n + 4, G_LOOP + 12 * n + 4, 6 * i, 12 * i)
            split_lo(S_LAST + 1)
            dve.memset(SS4[:], 0.0).then_inc(zeroed, 1)
            dve.wait_ge(zeroed, 4)
            for m in range(KD):
                add_gated(G_LAST + m, G2, m)
                if m >= 1:
                    add_square(SS4, SQ4[:, 0, :], 16 + m, 14 + m)
            add_square(SS4, SQ4[:, 0, :], 16 + KD, 14 + KD)
            token_rstd(3)
            dve.wait_ge(tok_rstd, 3)
            for n in range(UNITS):
                r = P if n < KD else SD
                dve.wait_ge(y_turned, n + 1)
                if n >= 4:
                    dve.wait_ge(y_stored[n % 4], 16 * (n // 4))
                dve.tensor_scalar(ORW[0:r, n % 4, 0:512], PS[0:r, 2 * (n % 3), :], RT[0:r, n:n + 1], None, ALU.mult)\
                    .then_inc(y_kept_dve, 1)

        @block.gpsimd
        def _(pool):
            wait_filled(pool, G_CQ + KQ - 1)
            for e in range(2):
                pool.memset(QT[e][:], 0.0).then_inc(pool_zeroed, 1)
                pool.memset(KT[e][:], 0.0).then_inc(pool_zeroed, 1)
            pool.wait_ge(wq_scaled, KQ)
            with pool.Fori(0, NJ) as j:
                pool.wait_ge(q_full, j + 1)
                for e in range(2):
                    h = 2 * j + e
                    ins = pool.tensor_copy(WQP[:, :, e, :], WQ[:, :, bass.ds(h * (NOPE + ROPE), NOPE)])
                ins.then_inc(wqp_ready, 1)
                pool.wait_ge(v_full, 2 * j + 1)
                pool.wait_ge(wkv_loaded, 16)
                for e in range(2):
                    h = 2 * j + e
                    pool.tensor_copy(WKP[:, :, e, :], WKV[:, :, bass.ds(h * (NOPE + VH), NOPE)])
                    ins = pool.tensor_copy(WVP[:, :, e, :], WKV[:, :, bass.ds(h * (NOPE + VH) + NOPE, VH)])
                ins.then_inc(wkvp_ready, 1)


_INS = ["x_prompt", "x_sample", "c_prompt", "c_sample", "cache_kv_latent", "cache_k_rope", "state_conv",
        "w_ada", "b_ada", "norm_mix_g", "w_in", "q_norm_g", "w_uq", "kv_norm_g", "w_ukv", "conv_w", "conv_b",
        "w_out", "norm_ffn_g", "w_gate", "w_up", "w_down", "final_norm_g"]
_OUTS = [(1, S, D), (1, SD, D), (1, 1, S, KVR), (1, 1, S, ROPE), (1, 1, CW - 1, DCONV),
         (1, 1, SD, KVR), (1, 1, SD, ROPE), (1, 1, CW - 1, DCONV)]


def constants():
    inv = np.float32(10000.0) ** (-np.arange(HALF, dtype=np.float32) / np.float32(HALF))
    pos = np.concatenate([np.arange(S), PAST + np.arange(SD)]).astype(np.float32)
    ang = (pos[:, None] * inv[None, :]).astype(np.float32)
    cos = np.tile(np.cos(ang).T, (HEADS, 1)).astype(np.float32)
    sin = np.tile(np.sin(ang).T, (HEADS, 1)).astype(np.float32)
    qmask = np.zeros((KD, T), np.float32)
    kmask = np.zeros((KD, TK), np.float32)
    for t in range(KD):
        qmask[t, t * P:t * P + CHUNK] = -BIG
        kmask[t, t * P + CHUNK:(t + 1) * P] = 1.0
    return {"c_ident": np.eye(P, dtype=np.float32), "c_cos": cos, "c_sin": sin, "c_qmask": qmask, "c_kmask": kmask}


def kernel(**inputs):
    import concourse.bacc as bacc
    from concourse.bass_utils import run_bass_kernel_spmd

    nc = bacc.Bacc("TRN2", target_bir_lowering=False, num_devices=1)
    arrays, args = {}, []
    named = [(n, np.ascontiguousarray(inputs[n])) for n in _INS] + list(constants().items())
    for name, a in named:
        arrays[f"in_{name}"] = a
        args.append(nc.dram_tensor(f"in_{name}", a.shape, mybir.dt.from_np(a.dtype), kind="ExternalInput").ap())
    for i, shape in enumerate(_OUTS):
        args.append(nc.dram_tensor(f"out_{i}", shape, F32, kind="ExternalOutput").ap())
    build(nc, *args)
    r = run_bass_kernel_spmd(nc, [arrays], core_ids=[0])
    return tuple(r.results[0][f"out_{i}"] for i in range(len(_OUTS)))
```
